# Optimizing a Trainium2 kernel written in Bass

```python
import jax, jax.numpy as jnp
from jax import lax
import numpy as np

D_MODEL = 1024
BATCH = 1
SEQ = 512
DEPTH = 1
DEC_BATCH = 8
DEC_SEQ = 8
PAST_LEN = 256
PAGE_SIZE = 128

D_RNN = D_MODEL
LRU_BLOCKS = 16
LRU_BLOCK = D_RNN // LRU_BLOCKS
LRU_CONV = 4
LRU_C = 8.0
ATT_PATTERNS = ((128, 1), (512, 4), (2048, 16))
N_GROUPS = len(ATT_PATTERNS)
HEADS_PER_GROUP = 4
HEAD_DIM = 128
ATT_W = N_GROUPS * HEADS_PER_GROUP * HEAD_DIM
ATT_OUT = HEADS_PER_GROUP * HEAD_DIM
ATT_Q_BLOCK = 128
D_FF = 3 * D_MODEL
FFN_CONV = 3
N_IN = 2 * D_RNN + 3 * ATT_W + 2 * D_MODEL
IN_SPLITS = (D_RNN, 2 * D_RNN, 2 * D_RNN + ATT_W, 2 * D_RNN + 2 * ATT_W,
             2 * D_RNN + 3 * ATT_W, 2 * D_RNN + 3 * ATT_W + D_MODEL)
NORM_EPS = 1e-6
NEG_BIG = -1e30

kernel_name = 'hawk_dilated_swa_convffn_step'

def rmsnorm(x, g):
    xf = x.astype(jnp.float32)
    y = xf * lax.rsqrt(jnp.mean(xf * xf, axis=-1, keepdims=True) + NORM_EPS) * g.astype(jnp.float32)
    return y.astype(x.dtype)

def causal_dwconv(u, buf, w, b):
    width = w.shape[0]
    T = u.shape[1]
    ext = jnp.concatenate([buf.astype(u.dtype), u], axis=1)
    out = b + ext[:, 0:T] * w[0]
    for i in range(1, width):
        out = out + ext[:, i:i + T] * w[i]
    return out, ext[:, T:]

def rg_lru(xc, pos, h0, wa, ba, wx, bx, lam):
    B, T, D = xc.shape
    xf = xc.astype(jnp.float32)
    xb = xf.reshape(B, T, LRU_BLOCKS, LRU_BLOCK)
    r = jax.nn.sigmoid(jnp.einsum('btnd,nde->btne', xb, wa).reshape(B, T, D) + ba)
    i = jax.nn.sigmoid(jnp.einsum('btnd,nde->btne', xb, wx).reshape(B, T, D) + bx)
    log_a = -LRU_C * r * jax.nn.softplus(-lam.astype(jnp.float32))
    a = jnp.exp(log_a)
    mult = jnp.sqrt(-jnp.expm1(2.0 * log_a))
    mult = jnp.where((pos == 0)[None, :, None], 1.0, mult)
    u = mult * i * xf

    def step(h, au):
        a_t, u_t = au
        h = a_t * h + u_t
        return h, h

    h_T, hs = lax.scan(step, h0.astype(jnp.float32),
                       (jnp.swapaxes(a, 0, 1), jnp.swapaxes(u, 0, 1)))
    return jnp.swapaxes(hs, 0, 1).astype(xc.dtype), h_T.astype(xc.dtype)

def dilated_attn(q, k_ext, v_ext, q_pos, ext_start, window, dilation):
    B, Tq, H, Dh = q.shape
    L = k_ext.shape[1]
    offs = jnp.arange(window // dilation + 1, dtype=jnp.int32) * dilation
    qb = ATT_Q_BLOCK if Tq % ATT_Q_BLOCK == 0 else Tq
    nb = Tq // qb
    scale = HEAD_DIM ** -0.5

    def block(args):
        q_blk, pos_blk = args
        key_pos = pos_blk[:, None] - offs[None, :]
        valid = key_pos >= 0
        idx = jnp.clip(key_pos - ext_start, 0, L - 1)
        kg = k_ext[:, idx].astype(jnp.float32)
        vg = v_ext[:, idx].astype(jnp.float32)
        s = jnp.einsum('bqhd,bqjhd->bqhj', q_blk.astype(jnp.float32), kg) * scale
        s = jnp.where(valid[None, :, None, :], s, NEG_BIG)
        m = jnp.max(s, axis=-1, keepdims=True)
        p = jnp.exp(s - m)
        den = jnp.sum(p, axis=-1)
        o = jnp.einsum('bqhj,bqjhd->bqhd', p, vg) / den[..., None]
        return o, m[..., 0] + jnp.log(den)

    q_blocks = jnp.moveaxis(q.reshape(B, nb, qb, H, Dh), 1, 0)
    o, lse = lax.map(block, (q_blocks, q_pos.reshape(nb, qb)))
    o = jnp.moveaxis(o, 0, 1).reshape(B, Tq, H, Dh)
    lse = jnp.moveaxis(lse, 0, 1).reshape(B, Tq, H)
    return o, lse

def ring_to_chrono(buf, past_len):
    n = buf.shape[1]
    return jnp.roll(buf, -((past_len - n) % n), axis=1)

def chrono_to_ring(rows, end_pos):
    n = rows.shape[1]
    return jnp.roll(rows, (end_pos - n) % n, axis=1)

def hybrid_layer(x, pos0, lru_h0, lru_conv0, kv_past, ffn_conv0,
                 norm1_g, w_in, conv_a_w, conv_a_b, lru_wa, lru_ba, lru_wx, lru_bx, lru_lambda,
                 q_norm_g, k_norm_g, w_br_a, w_br_b, w_out, norm2_g, w_up, conv_f_w, conv_f_b, w_down):
    B, T, _ = x.shape
    pos = pos0 + jnp.arange(T, dtype=jnp.int32)
    h = rmsnorm(x, norm1_g)
    xa, ga, q, k, v, gate_a, gate_b = jnp.split(jnp.einsum('btd,de->bte', h, w_in), IN_SPLITS, axis=-1)

    xc, new_conv_a = causal_dwconv(xa, lru_conv0, conv_a_w, conv_a_b)
    lru_y, new_h = rg_lru(xc, pos, lru_h0, lru_wa, lru_ba, lru_wx, lru_bx, lru_lambda)
    branch_a = jnp.einsum('btc,cd->btd', lru_y * jax.nn.gelu(ga), w_br_a)

    shp = (B, T, N_GROUPS, HEADS_PER_GROUP, HEAD_DIM)
    q = rmsnorm(q.reshape(shp), q_norm_g[:, None, :])
    k = rmsnorm(k.reshape(shp), k_norm_g[:, None, :])
    v = v.reshape(shp)
    outs, lses, new_kv = [], [], []
    for g, (window, dilation) in enumerate(ATT_PATTERNS):
        qg, kg, vg = q[:, :, g], k[:, :, g], v[:, :, g]
        if kv_past is None:
            k_ext, v_ext, ext_start = kg, vg, pos0
            keep = min(window, T)
            new_kv += [chrono_to_ring(kg[:, T - keep:], pos0 + T),
                       chrono_to_ring(vg[:, T - keep:], pos0 + T)]
        else:
            k_past, v_past = kv_past[g]
            k_ext = jnp.concatenate([k_past.astype(kg.dtype), kg], axis=1)
            v_ext = jnp.concatenate([v_past.astype(vg.dtype), vg], axis=1)
            ext_start = pos0 - k_past.shape[1]
            new_kv += [kg, vg]
        o, lse = dilated_attn(qg, k_ext, v_ext, pos, ext_start, window, dilation)
        outs.append(o)
        lses.append(lse)
    wts = jax.nn.softmax(jnp.stack(lses, axis=0), axis=0)
    att = jnp.sum(wts[..., None] * jnp.stack(outs, axis=0), axis=0)
    att = att.reshape(B, T, ATT_OUT).astype(x.dtype)
    branch_b = jnp.einsum('btc,cd->btd', att, w_br_b)

    merged = jax.nn.sigmoid(gate_a) * branch_a + jax.nn.sigmoid(gate_b) * branch_b
    x = x + jnp.einsum('btd,de->bte', merged, w_out)

    h2 = rmsnorm(x, norm2_g)
    up, new_conv_f = causal_dwconv(jnp.einsum('btd,df->btf', h2, w_up), ffn_conv0, conv_f_w, conv_f_b)
    gf, vf = jnp.split(up, 2, axis=-1)
    x = x + jnp.einsum('btf,fd->btd', jax.nn.gelu(gf) * vf, w_down)
    return x, (new_h, new_conv_a, new_kv[0], new_kv[1], new_kv[2], new_kv[3], new_kv[4], new_kv[5], new_conv_f)

def setup_inputs(seed: int = 0) -> dict:
    key = jax.random.key(seed)
    ks = jax.random.split(key, 32)

    def nrm(k, shape, scale=1.0):
        return scale * jax.random.normal(k, shape, jnp.float32)

    lw = [min(w, PAST_LEN) for w, _ in ATT_PATTERNS]
    kv_shape = lambda n: (DEPTH, DEC_BATCH, n, HEADS_PER_GROUP, HEAD_DIM)
    a0 = jax.random.uniform(ks[30], (DEPTH, D_RNN), jnp.float32, minval=0.9, maxval=0.999)
    return {
        'x_prompt': nrm(ks[0], (BATCH, SEQ, D_MODEL)),
        'x_sample': nrm(ks[1], (DEC_BATCH, DEC_SEQ, D_MODEL)),
        'state_lru_h': nrm(ks[2], (DEPTH, DEC_BATCH, D_RNN), 0.5),
        'state_lru_conv': nrm(ks[3], (DEPTH, DEC_BATCH, LRU_CONV - 1, D_RNN)),
        'cache_k_g0': nrm(ks[4], kv_shape(lw[0])),
        'cache_v_g0': nrm(ks[5], kv_shape(lw[0])),
        'cache_k_g1': nrm(ks[6], kv_shape(lw[1])),
        'cache_v_g1': nrm(ks[7], kv_shape(lw[1])),
        'cache_k_g2': nrm(ks[8], kv_shape(lw[2])),
        'cache_v_g2': nrm(ks[9], kv_shape(lw[2])),
        'state_ffn_conv': nrm(ks[10], (DEPTH, DEC_BATCH, FFN_CONV - 1, 2 * D_FF)),
        'norm1_g': 1.0 + nrm(ks[11], (DEPTH, D_MODEL), 0.1),
        'w_in': nrm(ks[12], (DEPTH, D_MODEL, N_IN), D_MODEL ** -0.5),
        'conv_a_w': nrm(ks[13], (DEPTH, LRU_CONV, D_RNN), LRU_CONV ** -0.5),
        'conv_a_b': nrm(ks[14], (DEPTH, D_RNN), 0.1),
        'lru_wa': nrm(ks[15], (DEPTH, LRU_BLOCKS, LRU_BLOCK, LRU_BLOCK), LRU_BLOCK ** -0.5),
        'lru_ba': nrm(ks[16], (DEPTH, D_RNN), 0.1),
        'lru_wx': nrm(ks[17], (DEPTH, LRU_BLOCKS, LRU_BLOCK, LRU_BLOCK), LRU_BLOCK ** -0.5),
        'lru_bx': nrm(ks[18], (DEPTH, D_RNN), 0.1),
        'lru_lambda': jnp.log(a0) - jnp.log1p(-a0),
        'q_norm_g': 1.0 + nrm(ks[19], (DEPTH, N_GROUPS, HEAD_DIM), 0.1),
        'k_norm_g': 1.0 + nrm(ks[20], (DEPTH, N_GROUPS, HEAD_DIM), 0.1),
        'w_br_a': nrm(ks[21], (DEPTH, D_RNN, D_MODEL), D_RNN ** -0.5),
        'w_br_b': nrm(ks[22], (DEPTH, ATT_OUT, D_MODEL), ATT_OUT ** -0.5),
        'w_out': nrm(ks[23], (DEPTH, D_MODEL, D_MODEL), D_MODEL ** -0.5),
        'norm2_g': 1.0 + nrm(ks[24], (DEPTH, D_MODEL), 0.1),
        'w_up': nrm(ks[25], (DEPTH, D_MODEL, 2 * D_FF), D_MODEL ** -0.5),
        'conv_f_w': nrm(ks[26], (DEPTH, FFN_CONV, 2 * D_FF), FFN_CONV ** -0.5),
        'conv_f_b': nrm(ks[27], (DEPTH, 2 * D_FF), 0.1),
        'w_down': nrm(ks[28], (DEPTH, D_FF, D_MODEL), D_FF ** -0.5),
    }

def reference(x_prompt, x_sample, state_lru_h, state_lru_conv, cache_k_g0, cache_v_g0,
              cache_k_g1, cache_v_g1, cache_k_g2, cache_v_g2, state_ffn_conv,
              norm1_g, w_in, conv_a_w, conv_a_b, lru_wa, lru_ba, lru_wx, lru_bx, lru_lambda,
              q_norm_g, k_norm_g, w_br_a, w_br_b, w_out, norm2_g, w_up, conv_f_w, conv_f_b, w_down):
    yp, ys = x_prompt, x_sample
    bp = x_prompt.shape[0]
    p_states = [[] for _ in range(9)]
    s_states = [[] for _ in range(9)]
    for l in range(DEPTH):
        params = (norm1_g[l], w_in[l], conv_a_w[l], conv_a_b[l], lru_wa[l], lru_ba[l], lru_wx[l],
                  lru_bx[l], lru_lambda[l], q_norm_g[l], k_norm_g[l], w_br_a[l], w_br_b[l], w_out[l],
                  norm2_g[l], w_up[l], conv_f_w[l], conv_f_b[l], w_down[l])
        yp, st_p = hybrid_layer(yp, 0,
                                jnp.zeros((bp, D_RNN), yp.dtype),
                                jnp.zeros((bp, LRU_CONV - 1, D_RNN), yp.dtype),
                                None,
                                jnp.zeros((bp, FFN_CONV - 1, 2 * D_FF), yp.dtype),
                                *params)
        past = ((ring_to_chrono(cache_k_g0[l], PAST_LEN), ring_to_chrono(cache_v_g0[l], PAST_LEN)),
                (ring_to_chrono(cache_k_g1[l], PAST_LEN), ring_to_chrono(cache_v_g1[l], PAST_LEN)),
                (ring_to_chrono(cache_k_g2[l], PAST_LEN), ring_to_chrono(cache_v_g2[l], PAST_LEN)))
        ys, st_s = hybrid_layer(ys, PAST_LEN, state_lru_h[l], state_lru_conv[l], past,
                                state_ffn_conv[l], *params)
        for i in range(9):
            p_states[i].append(st_p[i])
            s_states[i].append(st_s[i])
    (p_lru_h, p_lru_conv, p_k0, p_v0, p_k1, p_v1, p_k2, p_v2, p_ffn_conv) = [jnp.stack(s, axis=0) for s in p_states]
    (s_lru_h, s_lru_conv, s_k0, s_v0, s_k1, s_v1, s_k2, s_v2, s_ffn_conv) = [jnp.stack(s, axis=0) for s in s_states]
    return (yp, ys,
            p_lru_h, p_lru_conv, p_k0, p_v0, p_k1, p_v1, p_k2, p_v2, p_ffn_conv,
            s_lru_h, s_lru_conv, s_k0, s_v0, s_k1, s_v1, s_k2, s_v2, s_ffn_conv)


_drawn_inputs = setup_inputs


def setup_inputs(seed=0):
    import zlib

    import numpy as np

    out = dict(_drawn_inputs(seed))
    spreads = {}
    factors = {'cache_k_g2': 4.0,
     'cache_v_g2': 3.257,
     'q_norm_g': 6.931,
     'cache_k_g1': 8.0,
     'cache_v_g1': 8.0}
    for name, (base, spread) in spreads.items():
        noise = np.random.default_rng([zlib.crc32(name.encode()), seed]).standard_normal(out[name].shape)
        drawn = base * np.exp(spread * noise) if base else spread * noise
        out[name] = __import__('jax').numpy.asarray(drawn.astype(out[name].dtype))
    for name, factor in factors.items():
        out[name] = (out[name] * factor).astype(out[name].dtype)
    return out
```

```python
from contextlib import ExitStack

import concourse.bass as bass
from concourse import mybir

F32 = mybir.dt.float32
F32R = mybir.dt.float32r
ALU = mybir.AluOpType
ACT = mybir.ActivationFunctionType
AX_X = mybir.AxisListType.X

P = 128
D = 1024
KT = D // P
SEQ = 512
NB, NT = 8, 8
NS = NB * NT
TOK = SEQ + NS
HALF = TOK // 2
PAST = 256
NG, NH, HD = 3, 4, 128
AW = NG * NH * HD
DFF = 3 * D
FT = DFF // P
NCLS = 4
XA0, GA0, Q0, K0, V0, GTA0, GTB0 = 0, D, 2 * D, 2 * D + AW, 2 * D + 2 * AW, 2 * D + 3 * AW, 3 * D + 3 * AW
SCALE = HD ** -0.5
EPS = 1e-6
NEG = -1e30

C_ID, C_ONE, C_PM = 0, P, 2 * P
C_SM = C_PM + 9 * P
C_EPS = C_SM + 4 * P + NG * NS
C_N = C_EPS + 1

V_CW, V_CB, V_BA, V_BX, V_LAM, V_N1, V_N2, V_SC, V_H0 = 0, 4, 5, 6, 7, 8, 9, 10, 34
V_N = 42
F_W, F_B, F_S, F_N = 0, 3, 4, 20

XPAD, XSEQ = 3, 3 + NT
XS0 = XPAD + SEQ
XW = XS0 + NB * XSEQ
LW = XW - XPAD
LS0 = XS0
UPAD, USEQ = 2, 2 + NT
US0 = UPAD + SEQ
UW = US0 + NB * USEQ
CW = UW - UPAD

NRAW, NSPL = 4, 2
U_LRU = 9 * NH
U_MRG = U_LRU + 2 * KT
U_OUT = U_MRG + 4 * KT
U_FFN = U_OUT + KT
U_ALL = U_FFN + 2 * FT + 3 * KT
NPAIR, NRND = FT, 3
PPR = NPAIR // NRND


def up_unit(i):
    return U_FFN + 2 * i + KT * min((i - 1) // PPR if i else 0, NRND - 1)


def down_unit(r, m):
    pairs = min((r + 1) * PPR + 1, NPAIR)
    return U_FFN + 2 * pairs + KT * r + m


def ffn_steps():
    for i in range(NPAIR):
        yield "up", i, 0
        for r in range(NRND):
            if i == min((r + 1) * PPR, NPAIR - 1):
                for m in range(KT):
                    yield "down", r, m


def build(nc, t):
    w_in = t["w_in"][0].rearrange("(k p) n -> p k n", p=P)
    w_br_a = t["w_br_a"][0].rearrange("(k p) n -> p k n", p=P)
    w_br_b = t["w_br_b"][0].rearrange("(k p) n -> p k n", p=P)
    w_out = t["w_out"][0].rearrange("(k p) n -> p k n", p=P)
    w_up = t["w_up"][0].rearrange("(k p) n -> p k n", p=P)
    w_down = t["w_down"][0].rearrange("(k p) n -> p k n", p=P)
    out = t["out"]

    def cols(w, c, k0=0, kn=KT):
        return w[:, k0:k0 + kn, c:c + P]

    units = []
    for hp in range(NH):
        for g in range(NG):
            for base in (K0, Q0, V0):
                units.append(cols(w_in, base + (g * NH + hp) * HD))
    for c in range(KT):
        units += [cols(w_in, XA0 + c * P), cols(w_in, GA0 + c * P)]
    for m in range(KT):
        units += [cols(w_in, GTA0 + m * P), cols(w_br_a, m * P),
                  cols(w_in, GTB0 + m * P), cols(w_br_b, m * P, 0, NH)]
    for m in range(KT):
        units.append(cols(w_out, m * P))
    for kind, i, m in ffn_steps():
        if kind == "up":
            assert up_unit(i) == len(units)
            units += [cols(w_up, i * P), cols(w_up, DFF + i * P)]
        else:
            assert down_unit(i, m) == len(units)
            units.append(cols(w_down, m * P, i * PPR, PPR))
    assert len(units) == U_ALL
    nkt = [u.shape[1] for u in units]

    ctx = ExitStack()
    with ctx:
        def sb(name, shape, dt=F32, at=ctx):
            return at.enter_context(nc.sbuf_tensor(name, shape, dt))

        def sem(name):
            return ctx.enter_context(nc.semaphore(name))

        const = sb("const", [P, C_N])
        vt = sb("vt", [P, KT, V_N])
        ft = sb("ft", [P, 2 * FT, F_N])
        qkg = sb("qkg", [P, 2 * NG])
        sp4 = sb("sp4", [P, 4, KT])
        sp_t = sb("sp_t", [P, 2, KT])
        w_raw = sb("w_raw", [P, NRAW, KT, P])
        w_hi = sb("w_hi", [P, NSPL, KT, P], F32R)
        w_lo = sb("w_lo", [P, NSPL, KT, P], F32R)
        h_hi = sb("h_hi", [P, KT, TOK], F32R)
        h_lo = sb("h_lo", [P, KT, TOK], F32R)
        ident, ones = const[:, C_ID:C_ID + P], const[:, C_ONE:C_ONE + P]
        eps = const[:, C_EPS:C_EPS + 1]

        with ExitStack() as m:
            nat_v = sb("nat_v", [V_N, D], at=m)
            nat_f = sb("nat_f", [F_N, 2 * DFF], at=m)
            nat_g = sb("nat_g", [2 * NG, P], at=m)
            x_tok = sb("x_tok", [P, 5, D], at=m)
            x_t = sb("x_t", [P, KT, TOK], at=m)
            sq = sb("sq", [P, 2, TOK], at=m)
            root = sb("root", [P, TOK], at=m)
            rinv = sb("rinv", [P, TOK], at=m)
            hn = sb("hn", [P, 2, TOK], at=m)
        mid = ExitStack()
        att_hi = sb("att_hi", [P, NH, TOK], F32R, mid)
        att_lo = sb("att_lo", [P, NH, TOK], F32R, mid)
        with ExitStack() as m:
            kT = sb("kT", [P, NG, TOK], at=m)
            qT = sb("qT", [P, NG, TOK], at=m)
            k_tok = sb("k_tok", [P, 5, NG, HD], at=m)
            v_tok = sb("v_tok", [P, 5, NG, HD], at=m)
            qk_sq = sb("qk_sq", [P, TOK], at=m)
            qk_gn = sb("qk_gn", [P, 2, TOK], at=m)
            qk_rt = sb("qk_rt", [P, TOK], at=m)
            qk_ri = sb("qk_ri", [P, TOK], at=m)
            vT = sb("vT", [P, TOK], at=m)
            prob = sb("prob", [P, 2, 6 * P], at=m)
            probT = sb("probT", [P, 6 * P], at=m)
            q_dia = sb("q_dia", [P, NG, NB * (NS + NT)], at=m)
            p_dia = sb("p_dia", [P, 4, NB * (NS + NT)], at=m)
            p_new = sb("p_new", [NS, NG * NS], at=m)
            NKC = 6
            kc = sb("kc", [P, NKC, 4, HD], at=m)
            vc = sb("vc", [P, NB, 4, HD], at=m)
            kcT = sb("kcT", [P, 2, 4 * P], at=m)
            o_sb = sb("o_sb", [P, 2, HD], at=m)
            stat = sb("stat", [P, 4, 8], at=m)
        l_st = sb("l_st", [P, KT, 36], at=mid)
        l_row = sb("l_row", [36, D], at=mid)
        y_hi = sb("y_hi", [P, KT, TOK], F32R, mid)
        y_lo = sb("y_lo", [P, KT, TOK], F32R, mid)
        with ExitStack() as m:
            wa = sb("wa", [P, KT, P], at=m)
            wx = sb("wx", [P, KT, P], at=m)
            xa = sb("xa", [P, 2, XW], at=m)
            xc = sb("xc", [P, 2, LW], at=m)
            ga = sb("ga", [P, 2, TOK], at=m)
            g_r = sb("g_r", [P, LW], at=m)
            g_i = sb("g_i", [P, LW], at=m)
            a_s = sb("a_s", [P, LW], at=m)
            a_a = sb("a_a", [P, LW], at=m)
            a_2 = sb("a_2", [P, LW], at=m)
            l_u = sb("l_u", [P, LW], at=m)
            l_h = sb("l_h", [P, LW], at=m)
            l_y = sb("l_y", [P, TOK], at=m)
        with ExitStack() as m:
            mg_hi = sb("mg_hi", [P, KT, TOK], F32R, m)
            mg_lo = sb("mg_lo", [P, KT, TOK], F32R, m)
            sg_a = sb("sg_a", [P, TOK], at=m)
            sg_b = sb("sg_b", [P, TOK], at=m)
            mg_s = sb("mg_s", [P, 2, TOK], at=m)
        mid.close()
        x2 = sb("x2", [P, KT, TOK])
        with ExitStack() as m:
            x_tok2 = sb("x_tok2", [P, 5, D], at=m)
            sq2 = sb("sq2", [P, 2, TOK], at=m)
            xs = sb("xs", [P, TOK], at=m)
            root2 = sb("root2", [P, TOK], at=m)
            rinv2 = sb("rinv2", [P, TOK], at=m)
            hn2 = sb("hn2", [P, 2, TOK], at=m)
        g_hi, g_lo = [sb("g_hi0", [P, PPR, TOK], F32R)], [sb("g_lo0", [P, PPR, TOK], F32R)]
        ug = sb("ug", [P, 2, UW])
        uv = sb("uv", [P, 2, UW])
        cg = sb("cg", [P, CW])
        cv = sb("cv", [P, CW])
        gm = sb("gm", [P, TOK])
        f_st = sb("f_st", [P, 2 * PPR, 18])
        f_row = sb("f_row", [18, 4, 4 * P])
        with ExitStack() as m:
            g_hi.append(sb("g_hi1", [P, PPR, TOK], F32R, m))
            g_lo.append(sb("g_lo1", [P, PPR, TOK], F32R, m))
        y_tok = sb("y_tok", [P, 5, D])

        ps = [ctx.enter_context(nc.psum_tensor(f"ps{i}", [P, 1024], F32)) for i in range(4)]
        acc = [p[:, :].rearrange("p (h n) -> p h n", h=2)[:, :, 0:HALF] for p in ps]
        NORM, TRN = 2, 3

        s_const, s_nat, s_xin = sem("s_const"), sem("s_nat"), sem("s_xin")
        raw_in = [sem(f"raw_in{i}") for i in range(NRAW)]
        hi_ready, lo_ready, unit_done = sem("hi_ready"), sem("lo_ready"), sem("unit_done")
        acc_free = [sem("acc_free0"), sem("acc_free1")]
        vt_ps, vt_ready, tab_link = sem("vt_ps"), sem("vt_ready"), sem("tab_link")
        x_ps, x_copied, sq_ready, sq_used = sem("x_ps"), sem("x_copied"), sem("sq_ready"), sem("sq_used")
        root_ready, rinv_ready, hn_ready, hn_hi, hn_lo = (sem(x) for x in ("root_ready", "rinv_ready", "hn_ready", "hn_hi", "hn_lo"))
        qk_sqd, qk_sum, qk_root, qk_rinv, qk_ready = (sem(x) for x in ("qk_sqd", "qk_sum", "qk_root", "qk_rinv", "qk_ready"))
        tok_ps, tok_ready = sem("tok_ps"), sem("tok_ready")
        kv_out = [sem(f"kv_out{i}") for i in range(2 * NG)]
        s_zero, q_dia_rdy = sem("s_zero"), sem("q_dia_rdy")
        sc_ps, sc_read, mx_ready, p_ready, pT_ps, pT_ready = (sem(x) for x in ("sc_ps", "sc_read", "mx_ready", "p_ready", "pT_ps", "pT_ready"))
        o_ps, r_ready, o_ready, at_ps, at_hi_rdy, at_ready = (sem(x) for x in ("o_ps", "r_ready", "o_ready", "at_ps", "at_hi_rdy", "at_ready"))
        kc_in = [sem(f"kc_in{i}") for i in range(NKC)]
        vc_in = sem("vc_in")
        kcT_ps, kcT_used = sem("kcT_ps"), sem("kcT_used")
        kcT_rdy = [sem("kcT_rdy0"), sem("kcT_rdy1")]
        gw_zero, gw_in = sem("gw_zero"), sem("gw_in")
        l_link, xa_pad, xc_rdy, gate_ps, gate_read = (sem(x) for x in ("l_link", "xa_pad", "xc_rdy", "gate_ps", "gate_read"))
        as_rdy, aa_rdy, a2_rdy, m2_rdy, mul_rdy, y_rdy, y_hi_rdy, y_lo_rdy = (sem(x) for x in ("as_rdy", "aa_rdy", "a2_rdy", "m2_rdy", "mul_rdy", "y_rdy", "y_hi_rdy", "y_lo_rdy"))
        lst_rdy, lst_ps, lrow_rdy, l_out = sem("lst_rdy"), sem("lst_ps"), sem("lrow_rdy"), sem("l_out")
        mg_link, mg_rdy, mg_hi_rdy, mg_lo_rdy, br_b_rdy = (sem(x) for x in ("mg_link", "mg_rdy", "mg_hi_rdy", "mg_lo_rdy", "br_b_rdy"))
        x2_in, x2_ps, x2_cp, sq2_rdy, sq2_used = (sem(x) for x in ("x2_in", "x2_ps", "x2_cp", "sq2_rdy", "sq2_used"))
        root2_rdy, rinv2_rdy, hn2_rdy, hn2_hi, hn2_lo = (sem(x) for x in ("root2_rdy", "rinv2_rdy", "hn2_rdy", "hn2_hi", "hn2_lo"))
        u_pad, f_link, cg_rdy, gl_rdy, cv_rdy, gm_rdy, g_hi_rdy, g_lo_rdy = (sem(x) for x in ("u_pad", "f_link", "cg_rdy", "gl_rdy", "cv_rdy", "gm_rdy", "g_hi_rdy", "g_lo_rdy"))
        fst_rdy, fst_ps, frow_rdy, f_out = sem("fst_rdy"), sem("fst_ps"), sem("frow_rdy"), sem("f_out")
        yt_ps, yt_rdy, y_out = sem("yt_ps"), sem("yt_rdy"), sem("y_out")
        l_gr, ln_fix = sem("l_gr"), sem("ln_fix")

        def diag(row):
            return row.rearrange("p (b n) -> p b n", n=NS + NT)[:, :, 0:NT]

        def by_class(ap):
            return ap.rearrange("p (r i) -> p i r", r=NCLS)

        def in_time(ap):
            return ap.rearrange("p (i r) -> p i r", r=NCLS)

        def seqs(ap, width):
            return ap.rearrange("p (b n) -> p b n", n=width)

        def taken(eng, u):
            eng.wait_ge(acc_free[u % 2], u // 2 + 1)

        block = ctx.enter_context(nc.Block())

        @block.sync
        def _(sp):
            sp.dma_start(const[:, :], t["consts"]).then_inc(s_const, 16)
            for rows, name in ((slice(V_CW, V_CB), "conv_a_w"), (slice(V_CB, V_BA), "conv_a_b"),
                               (slice(V_BA, V_BX), "lru_ba"), (slice(V_BX, V_LAM), "lru_bx"),
                               (slice(V_LAM, V_N1), "lru_lambda"), (slice(V_N1, V_N2), "norm1_g"),
                               (slice(V_N2, V_SC), "norm2_g")):
                src = t[name]
                sp.dma_start(nat_v[rows, :], src[0] if len(src.shape) == 3 else src).then_inc(s_nat, 16)
            sp.dma_start(nat_v[V_SC:V_H0, :], t["state_lru_conv"][0].rearrange("b s d -> (b s) d")).then_inc(s_nat, 16)
            sp.dma_start(nat_v[V_H0:V_N, :], t["state_lru_h"][0]).then_inc(s_nat, 16)
            sp.dma_start(nat_g[0:NG, :], t["k_norm_g"][0]).then_inc(s_nat, 16)
            sp.dma_start(nat_g[NG:2 * NG, :], t["q_norm_g"][0]).then_inc(s_nat, 16)
            sp.dma_start(x_tok[:, 0:4, :], t["x_prompt"][0].rearrange("(n p) d -> p n d", p=P)).then_inc(s_xin, 16)
            sp.dma_start(x_tok[0:NS, 4, :], t["x_sample"].rearrange("b t d -> (b t) d")).then_inc(s_xin, 16)
            sp.dma_start(nat_f[F_W:F_B, :], t["conv_f_w"][0]).then_inc(s_nat, 16)
            sp.dma_start(nat_f[F_B:F_S, :], t["conv_f_b"]).then_inc(s_nat, 16)
            sp.dma_start(nat_f[F_S:F_N, :], t["state_ffn_conv"][0].rearrange("b s d -> (b s) d")).then_inc(s_nat, 16)
            for u, src in enumerate(units):
                if u >= NRAW:
                    sp.wait_ge(lo_ready, u - NRAW + 1)
                sp.dma_start(w_raw[:, u % NRAW, 0:nkt[u], :], src).then_inc(raw_in[u % NRAW], 16)

        @block.gpsimd
        def _(pool):
            pool.wait_ge(hn_lo, KT)
            pool.wait_ge(hn_hi, KT)
            pool.wait_ge(vt_ready, 3)
            pool.memset(q_dia[:, :, :], 0.0).then_inc(s_zero, 1)
            pool.memset(p_dia[:, :, :], 0.0).then_inc(s_zero, 1)

            def load_k(hp, b):
                n = hp * NB + b
                if n >= NKC:
                    pool.wait_ge(kcT_ps, n - NKC + 1)
                d = kc[:, n % NKC, :, :]
                s = kc_in[n % NKC]
                pool.dma_start(d[:, 0, :], t["cache_k_g0"][0, b, :, hp, :]).then_inc(s, 16)
                pool.dma_start(d[:, 1:3, :], t["cache_k_g1"][0, b, :, hp, :].rearrange("(n p) d -> p n d", p=P)).then_inc(s, 16)
                pool.dma_start(d[:, 3, :], t["cache_k_g2"][0, b, :, hp, :].rearrange("(c s) d -> c s d", s=16)[:, 0:NT, :]).then_inc(s, 16)

            def load_v(hp):
                if hp:
                    pool.wait_ge(o_ps, 5 * hp)
                for b in range(NB):
                    d = vc[:, b, :, :]
                    pool.dma_start(d[:, 0, :], t["cache_v_g0"][0, b, :, hp, :]).then_inc(vc_in, 16)
                    pool.dma_start(d[:, 1:3, :], t["cache_v_g1"][0, b, :, hp, :].rearrange("(n p) d -> p n d", p=P)).then_inc(vc_in, 16)
                    pool.dma_start(d[:, 3, :], t["cache_v_g2"][0, b, :, hp, :].rearrange("(c s) d -> c s d", s=16)[:, 0:NT, :]).then_inc(vc_in, 16)

            for hp in range(NH):
                load_v(hp)
                for b in range(min(NKC, NB)):
                    load_k(hp, b)
                for g in range(NG):
                    for kv, buf in enumerate((k_tok, v_tok)):
                        pool.wait_ge(tok_ready, hp * 6 + 2 * g + kv + 1)
                        o_p, o_s = out[4 + 2 * g + kv][0, 0], out[13 + 2 * g + kv]
                        s = kv_out[2 * g + kv]
                        if g == 0:
                            dst = o_p[:, hp, :].rearrange("(i r) d -> i r d", r=NCLS)
                            pool.dma_start(dst, buf[P - SEQ // 16:P, 0:4, g, :]).then_inc(s, 16)
                        else:
                            dst = o_p[:, hp, :].rearrange("(i r) d -> i r d", r=NCLS)
                            pool.dma_start(dst, buf[:, 0:4, g, :]).then_inc(s, 16)
                        pool.dma_start(o_s[0, :, :, hp, :].rearrange("b t d -> (b t) d"), buf[0:NS, 4, g, :]).then_inc(s, 16)
                for b in range(NKC, NB):
                    load_k(hp, b)
            pool.wait_ge(at_ready, 5 * NH)
            for s in kv_out:
                pool.wait_ge(s, 32 * NH)
            pool.memset(wa[:, :, :], 0.0).then_inc(gw_zero, 1)
            pool.memset(wx[:, :, :], 0.0).then_inc(gw_zero, 1)
            pool.memset(xa[:, :, 0:XPAD], 0.0).then_inc(gw_zero, 1)
            pool.wait_ge(gw_zero, 3)
            for buf, name in ((wa, "lru_wa"), (wx, "lru_wx")):
                src = t[name][0].rearrange("(c j) d e -> j d c e", j=2)
                for j in range(2):
                    pool.dma_start(buf[64 * j:64 * j + 64, :, 64 * j:64 * j + 64], src[j]).then_inc(gw_in, 16)
            for c in range(KT):
                pool.wait_ge(aa_rdy, c + 1)
                if c:
                    pool.wait_ge(m2_rdy, c)
                pool.tensor_tensor(a_2[:, :], a_a[:, :], a_a[:, :], ALU.mult).then_inc(a2_rdy, 1)
            pool.wait_ge(lrow_rdy, 1)
            pool.dma_start(out[3][0, 0], l_row[0:3, :]).then_inc(l_out, 16)
            pool.dma_start(out[12][0].rearrange("b s d -> (b s) d"), l_row[3:27, :]).then_inc(l_out, 16)
            pool.dma_start(out[2][0], l_row[27:28, :]).then_inc(l_out, 16)
            pool.dma_start(out[11][0], l_row[28:36, :]).then_inc(l_out, 16)
            pool.wait_ge(l_out, 64)
            pool.wait_ge(unit_done, U_OUT)
            pool.dma_start(x_tok2[:, 0:4, :], t["x_prompt"][0].rearrange("(n p) d -> p n d", p=P)).then_inc(x2_in, 16)
            pool.dma_start(x_tok2[0:NS, 4, :], t["x_sample"].rearrange("b t d -> (b t) d")).then_inc(x2_in, 16)
            for r in range(NRND):
                pool.wait_ge(frow_rdy, 4 * (r + 1))
                for half in range(2):
                    for q in range(2):
                        c0 = half * DFF + r * PPR * P + q * 4 * P
                        src = f_row[:, 2 * half + q, :]
                        pool.dma_start(out[10][0, 0, :, c0:c0 + 4 * P], src[0:2, :]).then_inc(f_out, 16)
                        pool.dma_start(out[19][0].rearrange("b s d -> (b s) d")[:, c0:c0 + 4 * P], src[2:18, :]).then_inc(f_out, 16)
            for m in range(KT):
                pool.wait_ge(yt_rdy, m + 1)
                pool.dma_start(out[0][0].rearrange("(n p) d -> p n d", p=P)[:, :, m * P:(m + 1) * P],
                               y_tok[:, 0:4, m * P:(m + 1) * P]).then_inc(y_out, 16)
                pool.dma_start(out[1].rearrange("b t d -> (b t) d")[:, m * P:(m + 1) * P],
                               y_tok[0:NS, 4, m * P:(m + 1) * P]).then_inc(y_out, 16)
            for s in kv_out:
                pool.wait_ge(s, 32 * NH)
            pool.wait_ge(l_out, 64)
            pool.wait_ge(f_out, 16 * 8 * NRND)
            pool.wait_ge(y_out, 32 * KT)

        @block.tensor
        def _(pe):
            mm, tr = pe.matmul, pe.transpose

            def unit(u, x_hi, x_lo):
                pe.wait_ge(lo_ready, u + 1)
                if u >= 2:
                    pe.wait_ge(acc_free[u % 2], u // 2)
                a, n = ps[u % 2], nkt[u]
                for k in range(n):
                    for w, x in ((w_hi, x_hi), (w_hi, x_lo), (w_lo, x_hi)):
                        for h in range(2):
                            last = mm(a[:, 512 * h:512 * h + HALF], w[:, u % NSPL, k, :],
                                      x[:, k, HALF * h:HALF * (h + 1)],
                                      start=(k == 0 and x is x_hi and w is w_hi), stop=(k == n - 1 and w is w_lo))
                last.then_inc(unit_done, 1)

            def feature_sum(src, k, n):
                for h in range(2):
                    last = mm(ps[NORM][:, 512 * h:512 * h + HALF], ones, src[:, HALF * h:HALF * (h + 1)],
                              start=(k == 0), stop=(k == n - 1))
                return last

            pe.wait_ge(s_const, 16)
            pe.wait_ge(s_nat, 16 * 14)
            for c in range(KT):
                tr(ps[2][:, c * V_N:(c + 1) * V_N], nat_v[:, c * P:(c + 1) * P], ident[0:V_N, 0:V_N])
            tr(ps[2][:, KT * V_N:KT * V_N + 2 * NG], nat_g[:, :], ident[0:2 * NG, 0:2 * NG]).then_inc(vt_ps, 1)
            for h in range(2):
                for c in range(FT):
                    last = tr(ps[3][:, 512 * h + c * F_N:512 * h + (c + 1) * F_N],
                              nat_f[:, (h * FT + c) * P:(h * FT + c + 1) * P], ident[0:F_N, 0:F_N])
            last.then_inc(vt_ps, 1)
            pe.wait_ge(s_xin, 32)
            for c in range(KT + 1):
                if c < KT:
                    if c >= 2:
                        pe.wait_ge(x_copied, c - 1)
                    for n in range(4):
                        tr(ps[c % 2][:, n * P:(n + 1) * P], x_tok[:, n, c * P:(c + 1) * P], ident)
                    tr(ps[c % 2][:, SEQ:TOK], x_tok[0:NS, 4, c * P:(c + 1) * P], ident[0:NS, 0:NS]).then_inc(x_ps, 1)
                if c:
                    if c == 1:
                        pe.wait_ge(vt_ready, 1)
                    pe.wait_ge(sq_ready, c)
                    feature_sum(sq[:, (c - 1) % 2, :], c - 1, KT).then_inc(sq_used, 1)
            pe.wait_ge(vt_ready, 2)
            pe.wait_ge(hn_lo, KT)
            pe.wait_ge(hn_hi, KT)
            pe.wait_ge(x_copied, KT)

            def qk_norm_sum(hp, j):
                n = hp * 6 + 2 * (j // 3) + j % 3
                pe.wait_ge(qk_sqd, n + 1)
                if n:
                    pe.wait_ge(qk_root, n)
                feature_sum(qk_sq, 0, 1).then_inc(qk_sum, 1)

            def to_rows(hp, g, kv):
                n = hp * 6 + 2 * g + kv
                if kv:
                    u = hp * 9 + 3 * g + 2
                    pe.wait_ge(acc_free[u % 2], u // 2 + 1)
                else:
                    pe.wait_ge(qk_ready, n + 1)
                if n:
                    pe.wait_ge(tok_ready, n)
                src = vT if kv else kT[:, g, :]
                for r in range(4):
                    tr(ps[TRN][:, r * P:(r + 1) * P], src[:, r * P:(r + 1) * P], ident)
                tr(ps[TRN][0:NS, SEQ:SEQ + P], src[:, SEQ:TOK], ident).then_inc(tok_ps, 1)

            def scores(hp, r):
                e = hp * 5 + r
                if r == 0:
                    pe.wait_ge(qk_ready, 6 * hp + 6)
                    pe.wait_ge(tok_ready, 6 * hp + 6)
                    for p in range(2):
                        pe.wait_ge(acc_free[p], (9 * hp + 9 + 1 - p) // 2)
                if e:
                    pe.wait_ge(sc_read, e)
                rows = slice(r * P, (r + 1) * P)
                mm(ps[2][:, 0:SEQ], qT[:, 0, rows], kT[:, 0, 0:SEQ], start=True, stop=True)
                mm(ps[2][:, SEQ:SEQ + P], qT[:, 1, rows], kT[:, 1, rows], start=True, stop=True)
                mm(ps[2][:, SEQ + P:SEQ + 2 * P], qT[:, 2, rows], kT[:, 2, rows], start=True, stop=True).then_inc(sc_ps, 1)

            def cached_keys_T(hp, b):
                n = hp * NB + b
                pe.wait_ge(kc_in[n % NKC], 48 * (n // NKC + 1))
                if n >= 2:
                    pe.wait_ge(kcT_rdy[n % 2], n // 2)
                bank = ps[1][:, 512 * (b % 2):512 * (b % 2) + 512]
                for i in range(4):
                    last = tr(bank[:, i * P:(i + 1) * P], kc[:, n % NKC, i, :], ident)
                last.then_inc(kcT_ps, 1)

            def sample_scores(hp):
                e = hp * 5 + 4
                for b in range(NB + 1):
                    if b < NB:
                        cached_keys_T(hp, b)
                    if b == 0:
                        pe.wait_ge(sc_read, e)
                        pe.wait_ge(q_dia_rdy, hp + 1)
                        continue
                    n = hp * NB + b - 1
                    pe.wait_ge(kcT_rdy[n % 2], n // 2 + 1)
                    for g, c0, cn in ((0, 0, P), (1, P, 2 * P), (2, 3 * P, P)):
                        last = mm(ps[2][0:NS, c0:c0 + cn], q_dia[:, g, (b - 1) * NS:b * NS], kcT[:, n % 2, c0:c0 + cn],
                                  start=(b == 1 and g == 0), stop=(b == NB), skip_group_check=True)
                    last.then_inc(kcT_used, 1)
                for g in range(NG):
                    last = mm(ps[2][0:NS, 512 + g * NS:512 + (g + 1) * NS], qT[:, g, SEQ:TOK], kT[:, g, SEQ:TOK],
                              start=True, stop=True)
                last.then_inc(sc_ps, 1)

            def probs_T(hp, r):
                e = hp * 5 + r
                pe.wait_ge(p_ready, e + 1)
                if e:
                    pe.wait_ge(pT_ready, e)
                pr = prob[:, e % 2, :]
                if r < 4:
                    for i in range(6):
                        last = tr(ps[TRN][:, i * P:(i + 1) * P], pr[:, i * P:(i + 1) * P], ident)
                else:
                    for i in range(4):
                        tr(ps[TRN][:, i * NS:(i + 1) * NS], pr[0:NS, i * P:(i + 1) * P], ident[0:NS, 0:NS])
                    for g in range(NG):
                        last = tr(ps[TRN][0:NS, 512 + g * NS:512 + (g + 1) * NS],
                                  pr[0:NS, 512 + g * NS:512 + (g + 1) * NS], ident[0:NS, 0:NS])
                last.then_inc(pT_ps, 1)

            def values(hp, r):
                e = hp * 5 + r
                pe.wait_ge(pT_ready, e + 1)
                if e:
                    pe.wait_ge(o_ready, e)
                if r < 4:
                    srcs = [(probT[:, c * P:(c + 1) * P], v_tok[:, c, 0, :]) for c in range(4)]
                    srcs += [(probT[:, (3 + g) * P:(4 + g) * P], v_tok[:, r, g, :]) for g in (1, 2)]
                    o = ps[0][:, 0:HD]
                else:
                    pe.wait_ge(vc_in, 48 * NB * (hp + 1))
                    srcs = [(p_dia[:, i, b * NS:(b + 1) * NS], vc[:, b, i, :]) for b in range(NB) for i in range(4)]
                    srcs += [(p_new[:, g * NS:(g + 1) * NS], v_tok[0:NS, 4, g, :]) for g in range(NG)]
                    o = ps[0][0:NS, 0:HD]
                for i, (p_, v_) in enumerate(srcs):
                    last = mm(o, p_, v_, start=(i == 0), stop=(i == len(srcs) - 1))
                last.then_inc(o_ps, 1)

            def out_T(hp, r):
                e = hp * 5 + r
                pe.wait_ge(o_ready, e + 1)
                if e:
                    pe.wait_ge(at_ready, e)
                n = P if r < 4 else NS
                tr(ps[0][:, 512:512 + n], o_sb[0:n, e % 2, :], ident[0:n, 0:n]).then_inc(at_ps, 1)

            for hp in range(NH):
                for j in range(9):
                    if hp and j < 2:
                        pe.wait_ge(at_ready, 5 * hp)
                        pe.wait_ge(kcT_rdy[0], 4 * hp)
                        pe.wait_ge(kcT_rdy[1], 4 * hp)
                    unit(hp * 9 + j, h_hi, h_lo)
                    if j and (j - 1) % 3 < 2:
                        qk_norm_sum(hp, j - 1)
                    if j and (j - 1) % 3 == 2:
                        to_rows(hp, (j - 1) // 3, 1)
                    if j >= 2 and (j - 2) % 3 == 0:
                        to_rows(hp, (j - 2) // 3, 0)
                to_rows(hp, 2, 1)
                for s in range(8):
                    if s < 4:
                        scores(hp, s)
                    if s == 4:
                        sample_scores(hp)
                    if 0 <= s - 1 < 5:
                        probs_T(hp, s - 1)
                    if 0 <= s - 2 < 5:
                        values(hp, s - 2)
                    if 0 <= s - 3 < 5:
                        out_T(hp, s - 3)

            pe.wait_ge(at_ready, 5 * NH)
            for c in range(KT):
                unit(U_LRU + 2 * c, h_hi, h_lo)
                unit(U_LRU + 2 * c + 1, h_hi, h_lo)
                if c == 0:
                    pe.wait_ge(gw_in, 64)
                pe.wait_ge(xc_rdy, c + 1)
                if c:
                    pe.wait_ge(gate_read, c)
                for i, w in enumerate((wa, wx)):
                    for h in range(2):
                        last = mm(ps[2 + i][:, 512 * h:512 * h + LW // 2], w[:, c, :],
                                  xc[:, c % 2, h * LW // 2:(h + 1) * LW // 2], start=True, stop=True)
                last.then_inc(gate_ps, 1)

            for m in range(KT):
                unit(U_MRG + 4 * m, h_hi, h_lo)
                if m == 0:
                    pe.wait_ge(gate_read, KT)
                    pe.wait_ge(lst_rdy, KT)
                    for c in range(KT):
                        last = tr(ps[2][0:36, c * P:(c + 1) * P], l_st[:, c, :], ident)
                    last.then_inc(lst_ps, 1)
                    pe.wait_ge(y_hi_rdy, KT)
                    pe.wait_ge(y_lo_rdy, KT)
                unit(U_MRG + 4 * m + 1, y_hi, y_lo)
                unit(U_MRG + 4 * m + 2, h_hi, h_lo)
                unit(U_MRG + 4 * m + 3, att_hi, att_lo)

            pe.wait_ge(mg_hi_rdy, KT)
            pe.wait_ge(mg_lo_rdy, KT)
            pe.wait_ge(lrow_rdy, 1)
            for c in range(KT + 1):
                if c < KT:
                    unit(U_OUT + c, mg_hi, mg_lo)
                    if c == 0:
                        pe.wait_ge(x2_in, 32)
                    else:
                        pe.wait_ge(x2_cp, c)
                    for n in range(4):
                        tr(ps[3][:, n * P:(n + 1) * P], x_tok2[:, n, c * P:(c + 1) * P], ident)
                    tr(ps[3][:, SEQ:TOK], x_tok2[0:NS, 4, c * P:(c + 1) * P], ident[0:NS, 0:NS]).then_inc(x2_ps, 1)
                if c:
                    pe.wait_ge(sq2_rdy, c)
                    feature_sum(sq2[:, (c - 1) % 2, :], c - 1, KT).then_inc(sq2_used, 1)
            pe.wait_ge(hn2_lo, KT)
            pe.wait_ge(hn2_hi, KT)

            def state_rows(r):
                pe.wait_ge(fst_rdy, (r + 1) * PPR)
                for q in range(4):
                    if r and q == 0:
                        pe.wait_ge(frow_rdy, 4 * r)
                    for i in range(4):
                        last = tr(ps[2 + q // 2][0:18, 512 * (q % 2) + i * P:512 * (q % 2) + (i + 1) * P],
                                  f_st[:, 4 * q + i, :], ident)
                last.then_inc(fst_ps, 1)

            def y_rows(m):
                taken(pe, down_unit(NRND - 1, m))
                if m == 0:
                    pe.wait_ge(frow_rdy, 4 * NRND)
                if m >= 1:
                    pe.wait_ge(yt_rdy, m)
                for n in range(4):
                    tr(ps[3][:, n * P:(n + 1) * P], x2[:, m, n * P:(n + 1) * P], ident)
                tr(ps[3][0:NS, SEQ:SEQ + P], x2[:, m, SEQ:TOK], ident).then_inc(yt_ps, 1)

            for kind, i, m in ffn_steps():
                if kind == "up":
                    unit(up_unit(i), h_hi, h_lo)
                    unit(up_unit(i) + 1, h_hi, h_lo)
                else:
                    if m == 0:
                        pe.wait_ge(g_hi_rdy, (i + 1) * PPR)
                        pe.wait_ge(g_lo_rdy, (i + 1) * PPR)
                    unit(down_unit(i, m), g_hi[i % 2], g_lo[i % 2])
                    if m == 0:
                        state_rows(i)
                    if i == NRND - 1 and m:
                        y_rows(m - 1)
            y_rows(KT - 1)

        @block.scalar
        def _(act):
            A = act.activation

            def hi_split(u):
                if u >= U_ALL:
                    return
                act.wait_ge(raw_in[u % NRAW], 16 * (u // NRAW + 1))
                if u >= NSPL:
                    act.wait_ge(unit_done, u - NSPL + 1)
                A(w_hi[:, u % NSPL, 0:nkt[u], :], w_raw[:, u % NRAW, 0:nkt[u], :], ACT.Copy).then_inc(hi_ready, 1)

            for u in range(NSPL):
                hi_split(u)
            for c in range(KT):
                act.wait_ge(x_copied, c + 1)
                if c >= 2:
                    act.wait_ge(sq_used, c - 1)
                A(sq[:, c % 2, :], x_t[:, c, :], ACT.Square).then_inc(sq_ready, 1)
            act.wait_ge(sq_used, KT)
            act.wait_ge(s_const, 16)
            A(root[:, :].rearrange("p (h n) -> p h n", h=2), acc[NORM], ACT.Sqrt, scale=1.0 / D, bias=eps).then_inc(root_ready, 1)
            for c in range(KT):
                act.wait_ge(hn_ready, c + 1)
                A(h_hi[:, c, :], hn[:, c % 2, :], ACT.Copy).then_inc(hn_hi, 1)
            act.wait_ge(ln_fix, 2)
            A(sp4[:, 1, :], sp4[:, 0, :], ACT.Exp, scale=-1.0).then_inc(tab_link, 1)
            act.wait_ge(ln_fix, 3)
            A(sp4[:, 3, :], sp4[:, 2, :], ACT.Ln).then_inc(tab_link, 1)
            act.wait_ge(hn_lo, KT)
            act.wait_ge(vt_ready, 3)

            def head_unit(hp, j):
                u, g = hp * 9 + j, j // 3
                hi_split(u + NSPL)
                act.wait_ge(unit_done, u + 1)
                a = acc[u % 2]
                if j % 3 < 2:
                    n = hp * 6 + 2 * g + j % 3
                    if n:
                        act.wait_ge(qk_sum, n)
                    A(qk_sq[:, :].rearrange("p (h n) -> p h n", h=2), a, ACT.Square).then_inc(qk_sqd, 1)
                    if n >= 2:
                        act.wait_ge(qk_ready, n - 1)
                    gain = qkg[:, (j % 3) * NG + g:(j % 3) * NG + g + 1]
                    A(qk_gn[:, n % 2, :].rearrange("p (h n) -> p h n", h=2), a, ACT.Identity, scale=gain).then_inc(acc_free[u % 2], 1)
                else:
                    n = hp * 6 + 2 * g + 1
                    if n >= 2:
                        act.wait_ge(tok_ps, n - 1)
                    i0 = HALF // NCLS
                    vi = by_class(vT[:, 0:SEQ])
                    A(vi[:, 0:i0, :], in_time(ps[u % 2][:, 0:HALF]), ACT.Copy)
                    A(vi[:, i0:P, :], in_time(ps[u % 2][:, 512:512 + SEQ - HALF]), ACT.Copy)
                    A(vT[:, SEQ:TOK], ps[u % 2][:, 512 + SEQ - HALF:512 + HALF], ACT.Copy).then_inc(acc_free[u % 2], 1)

            def qk_root_of(hp, j):
                n = hp * 6 + 2 * (j // 3) + j % 3
                act.wait_ge(qk_sum, n + 1)
                if n:
                    act.wait_ge(qk_rinv, n)
                A(qk_rt[:, :].rearrange("p (h n) -> p h n", h=2), acc[NORM], ACT.Sqrt, scale=1.0 / HD, bias=eps).then_inc(qk_root, 1)

            def rows_of(hp, g, kv):
                n = hp * 6 + 2 * g + kv
                act.wait_ge(tok_ps, n + 1)
                if hp:
                    act.wait_ge(kv_out[2 * g + kv], 32 * hp)
                buf = v_tok if kv else k_tok
                A(buf[:, 0:4, g, :], ps[TRN][:, 0:SEQ].rearrange("p (r d) -> p r d", r=4), ACT.Copy)
                A(buf[0:NS, 4, g, :], ps[TRN][0:NS, SEQ:SEQ + HD], ACT.Copy).then_inc(tok_ready, 1)

            def exps(hp, r):
                e = hp * 5 + r
                act.wait_ge(mx_ready, e + 1)
                rows, n = (P, 6 * P) if r < 4 else (NS, 4 * P + NG * NS)
                pr = prob[0:rows, e % 2, 0:n]
                A(pr, pr, ACT.Exp, bias=stat[0:rows, e % 4, 2:3], accum_out=stat[0:rows, e % 4, 3:4]).then_inc(p_ready, 1)

            def take_probs_T(hp, r):
                e = hp * 5 + r
                act.wait_ge(pT_ps, e + 1)
                if e:
                    act.wait_ge(o_ps, e)
                if r < 4:
                    A(probT[:, :], ps[TRN][:, 0:6 * P], ACT.Copy).then_inc(pT_ready, 1)
                else:
                    act.wait_ge(s_zero, 2)
                    for i in range(4):
                        src = ps[TRN][:, i * NS:(i + 1) * NS]
                        A(diag(p_dia[:, i, :]), src.rearrange("p (b t) -> p b t", b=NB), ACT.Copy)
                    A(p_new[:, :], ps[TRN][0:NS, 512:512 + NG * NS], ACT.Copy).then_inc(pT_ready, 1)

            def out_hi(hp, r):
                e = hp * 5 + r
                act.wait_ge(at_ps, e + 1)
                if r < 4:
                    A(in_time(att_hi[:, hp, 0:SEQ])[:, :, r], ps[0][:, 512:512 + P], ACT.Copy).then_inc(at_hi_rdy, 1)
                else:
                    A(att_hi[:, hp, SEQ:TOK], ps[0][:, 512:512 + NS], ACT.Copy).then_inc(at_hi_rdy, 1)

            def take_cached_T(hp, b):
                n = hp * NB + b
                act.wait_ge(kcT_ps, n + 1)
                if n >= 2:
                    act.wait_ge(kcT_used, n - 1)
                A(kcT[:, n % 2, :], ps[1][:, 512 * (b % 2):512 * (b % 2) + 512], ACT.Copy).then_inc(kcT_rdy[n % 2], 1)

            for hp in range(NH):
                for j in range(9):
                    head_unit(hp, j)
                    if j and (j - 1) % 3 < 2:
                        qk_root_of(hp, j - 1)
                    if j and (j - 1) % 3 == 2:
                        rows_of(hp, (j - 1) // 3, 1)
                    if j >= 2 and (j - 2) % 3 == 0:
                        rows_of(hp, (j - 2) // 3, 0)
                rows_of(hp, 2, 1)
                for s in range(8):
                    if s < 4:
                        exps(hp, s)
                    if s == 4:
                        for b in range(1, NB, 2):
                            take_cached_T(hp, b)
                    if s == 4:
                        exps(hp, 4)
                    if 0 <= s - 1 < 5:
                        take_probs_T(hp, s - 1)
                    if 0 <= s - 3 < 5:
                        out_hi(hp, s - 3)

            for s in kv_out:
                act.wait_ge(s, 32 * NH)
            act.wait_ge(at_ready, 5 * NH)
            act.wait_ge(kcT_used, NH * NB)

            def gates(c):
                act.wait_ge(gate_ps, c + 1)
                if c:
                    act.wait_ge(y_lo_rdy, c)
                for i, dst in enumerate((g_r, g_i)):
                    last = A(dst[:, :].rearrange("p (h n) -> p h n", h=2),
                             ps[2 + i][:, :].rearrange("p (h n) -> p h n", h=2)[:, :, 0:LW // 2], ACT.Tanh,
                             scale=0.5, bias=sp4[:, 2 + i, c:c + 1])
                    last.then_inc(gate_read if i else l_gr, 1)
                act.wait_ge(l_gr, c + 1)
                A(a_s[:, :], g_r[:, :], ACT.Tanh, scale=sp4[:, 0, c:c + 1], bias=sp4[:, 0, c:c + 1]).then_inc(as_rdy, 1)
                A(a_a[:, :], g_r[:, :], ACT.Exp, scale=sp4[:, 1, c:c + 1], bias=sp4[:, 1, c:c + 1]).then_inc(aa_rdy, 1)

            def y_part(c):
                act.wait_ge(y_rdy, c + 1)
                A(y_hi[:, c, :], l_y[:, :], ACT.Copy).then_inc(y_hi_rdy, 1)

            for c in range(KT + 1):
                if c < KT:
                    u = U_LRU + 2 * c
                    hi_split(u + NSPL)
                    act.wait_ge(unit_done, u + 1)
                    if c >= 2:
                        act.wait_ge(lst_rdy, c - 1)
                    p_ = ps[u % 2]
                    A(xa[:, c % 2, XPAD:XPAD + HALF], p_[:, 0:HALF], ACT.Copy)
                    A(xa[:, c % 2, XPAD + HALF:XS0], p_[:, 512:512 + SEQ - HALF], ACT.Copy)
                    A(seqs(xa[:, c % 2, XS0:XW], XSEQ)[:, :, XPAD:XSEQ],
                      seqs(p_[:, 512 + SEQ - HALF:512 + HALF], NT), ACT.Copy).then_inc(acc_free[u % 2], 1)
                if c:
                    gates(c - 1)
                if c < KT:
                    u += 1
                    hi_split(u + NSPL)
                    act.wait_ge(unit_done, u + 1)
                    if c >= 2:
                        act.wait_ge(y_rdy, c - 1)
                    A(ga[:, c % 2, :].rearrange("p (h n) -> p h n", h=2), acc[u % 2], ACT.Gelu_apprx_tanh).then_inc(acc_free[u % 2], 1)
                if c:
                    act.wait_ge(m2_rdy, c)
                    A(a_s[:, :], a_s[:, :], ACT.Sqrt).then_inc(mul_rdy, 1)
                    y_part(c - 1)

            for m in range(KT):
                for j, dst in ((0, sg_a), (1, None), (2, sg_b), (3, None)):
                    u = U_MRG + 4 * m + j
                    hi_split(u + NSPL)
                    if m == 0 and j == 1:
                        act.wait_ge(lst_ps, 1)
                        A(l_row[:, :], ps[2][0:36, :], ACT.Copy).then_inc(lrow_rdy, 1)
                    if dst is not None:
                        act.wait_ge(unit_done, u + 1)
                        if m == 0 and j == 0:
                            act.wait_ge(y_lo_rdy, KT)
                            act.wait_ge(lst_rdy, KT)
                        if m:
                            act.wait_ge(mg_rdy, m)
                        A(dst[:, :].rearrange("p (h n) -> p h n", h=2), acc[u % 2], ACT.Sigmoid).then_inc(acc_free[u % 2], 1)
                        if m and j == 0:
                            A(mg_hi[:, m - 1, :], mg_s[:, 0, :], ACT.Copy).then_inc(mg_hi_rdy, 1)
            act.wait_ge(mg_rdy, KT)
            A(mg_hi[:, KT - 1, :], mg_s[:, 0, :], ACT.Copy).then_inc(mg_hi_rdy, 1)

            for c in range(KT):
                hi_split(U_OUT + c + NSPL)
                act.wait_ge(x2_ps, c + 1)
                if c:
                    taken(act, U_OUT + c - 1)
                A(xs[:, :], ps[3][:, 0:TOK], ACT.Copy).then_inc(x2_cp, 1)
                taken(act, U_OUT + c)
                if c >= 2:
                    act.wait_ge(sq2_used, c - 1)
                A(sq2[:, c % 2, :], x2[:, c, :], ACT.Square).then_inc(sq2_rdy, 1)
            act.wait_ge(sq2_used, KT)
            A(root2[:, :].rearrange("p (h n) -> p h n", h=2), acc[NORM], ACT.Sqrt, scale=1.0 / D, bias=eps).then_inc(root2_rdy, 1)
            for c in range(KT):
                act.wait_ge(hn2_rdy, c + 1)
                A(h_hi[:, c, :], hn2[:, c % 2, :], ACT.Copy).then_inc(hn2_hi, 1)

            def gelu(i):
                act.wait_ge(cg_rdy, i + 1)
                A(cg[:, :], cg[:, :], ACT.Gelu_apprx_tanh).then_inc(gl_rdy, 1)

            def g_part(i):
                act.wait_ge(gm_rdy, i + 1)
                r = i // PPR
                if r >= 2:
                    act.wait_ge(unit_done, down_unit(r - 2, KT - 1) + 1)
                A(g_hi[r % 2][:, i % PPR, :], gm[:, :], ACT.Copy).then_inc(g_hi_rdy, 1)

            def frows(r):
                act.wait_ge(fst_ps, r + 1)
                if r:
                    act.wait_ge(f_out, 16 * 8 * r)
                for q in range(4):
                    A(f_row[:, q, :], ps[2 + q // 2][0:18, 512 * (q % 2):512 * (q % 2) + 512], ACT.Copy).then_inc(frow_rdy, 1)

            def y_take(m):
                act.wait_ge(yt_ps, m + 1)
                A(y_tok[:, 0:4, m * P:(m + 1) * P], ps[3][:, 0:SEQ].rearrange("p (n d) -> p n d", n=4), ACT.Copy)
                A(y_tok[0:NS, 4, m * P:(m + 1) * P], ps[3][0:NS, SEQ:SEQ + P], ACT.Copy).then_inc(yt_rdy, 1)

            act.wait_ge(hn2_lo, KT)
            act.wait_ge(u_pad, 2)
            for kind, i, m in ffn_steps():
                if kind == "up":
                    for j, buf in enumerate((ug, uv)):
                        u = up_unit(i) + j
                        hi_split(u + NSPL)
                        act.wait_ge(unit_done, u + 1)
                        if i >= 2:
                            act.wait_ge(fst_rdy, i - 1)
                        p_ = ps[u % 2]
                        A(buf[:, i % 2, UPAD:UPAD + HALF], p_[:, 0:HALF], ACT.Copy)
                        A(buf[:, i % 2, UPAD + HALF:US0], p_[:, 512:512 + SEQ - HALF], ACT.Copy)
                        A(seqs(buf[:, i % 2, US0:UW], USEQ)[:, :, UPAD:USEQ],
                          seqs(p_[:, 512 + SEQ - HALF:512 + HALF], NT), ACT.Copy).then_inc(acc_free[u % 2], 1)
                    gelu(i)
                    g_part(i)
                else:
                    hi_split(down_unit(i, m) + NSPL)
                    if m == 0:
                        frows(i)
                    if i == NRND - 1 and m:
                        y_take(m - 1)
            y_take(KT - 1)

        @block.vector
        def _(dve):
            STT, TT, TS = dve.scalar_tensor_tensor, dve.tensor_tensor, dve.tensor_scalar

            def lo_split(u):
                if u >= U_ALL:
                    return
                dve.wait_ge(hi_ready, u + 1)
                TT(w_lo[:, u % NSPL, 0:nkt[u], :], w_raw[:, u % NRAW, 0:nkt[u], :],
                   w_hi[:, u % NSPL, 0:nkt[u], :], ALU.subtract).then_inc(lo_ready, 1)

            for u in range(NSPL):
                lo_split(u)
            dve.wait_ge(vt_ps, 1)
            dve.tensor_copy(qkg[:, :], ps[2][:, KT * V_N:KT * V_N + 2 * NG])
            dve.tensor_copy(vt[:, :, :], ps[2][:, 0:KT * V_N].rearrange("p (c n) -> p c n", c=KT)).then_inc(vt_ready, 1)
            dve.wait_ge(vt_ps, 2)
            dve.tensor_copy(ft[:, :, :].rearrange("p (h c) n -> p h (c n)", h=2),
                            ps[3][:, :].rearrange("p (h n) -> p h n", h=2)[:, :, 0:FT * F_N]).then_inc(vt_ready, 1)
            for c in range(KT):
                dve.wait_ge(x_ps, c + 1)
                dve.tensor_copy(x_t[:, c, :], ps[c % 2][:, 0:TOK]).then_inc(x_copied, 1)
            dve.wait_ge(root_ready, 1)
            dve.reciprocal(rinv[:, :], root[:, :]).then_inc(rinv_ready, 1)
            dve.wait_ge(rinv_ready, 1)
            dve.wait_ge(x_copied, KT)
            for c in range(KT):
                if c >= 2:
                    dve.wait_ge(hn_hi, c - 1)
                    dve.wait_ge(hn_lo, c - 1)
                STT(hn[:, c % 2, :], x_t[:, c, :], vt[:, c, V_N1:V_N1 + 1], rinv[:, :], ALU.mult, ALU.mult).then_inc(hn_ready, 1)
                if c:
                    dve.wait_ge(hn_hi, c)
                    TT(h_lo[:, c - 1, :], hn[:, (c - 1) % 2, :], h_hi[:, c - 1, :], ALU.subtract).then_inc(hn_lo, 1)
            dve.wait_ge(hn_hi, KT)
            TT(h_lo[:, KT - 1, :], hn[:, (KT - 1) % 2, :], h_hi[:, KT - 1, :], ALU.subtract).then_inc(hn_lo, 1)
            lam = vt[:, :, V_LAM]

            def fixed(ins, n):
                ins.then_inc(ln_fix, 1)
                dve.wait_ge(ln_fix, n)

            dve.wait_ge(vt_ready, 1)
            fixed(TS(sp4[:, 2, :], lam, -1.0, None, ALU.mult), 1)
            fixed(TT(sp4[:, 0, :], lam, sp4[:, 2, :], ALU.max), 2)
            dve.wait_ge(tab_link, 1)
            fixed(TS(sp4[:, 2, :], sp4[:, 1, :], 1.0, None, ALU.add), 3)
            fixed(dve.reciprocal(sp_t[:, 0, :], sp4[:, 2, :]), 4)
            fixed(TS(sp_t[:, 1, :], sp4[:, 2, :], -1.0, None, ALU.add), 5)
            fixed(TT(sp_t[:, 1, :], sp4[:, 1, :], sp_t[:, 1, :], ALU.subtract), 6)
            fixed(TT(sp_t[:, 1, :], sp_t[:, 1, :], sp_t[:, 0, :], ALU.mult), 7)
            dve.wait_ge(tab_link, 2)
            fixed(TT(sp_t[:, 1, :], sp_t[:, 1, :], sp4[:, 3, :], ALU.add), 8)
            fixed(TS(sp_t[:, 0, :], lam, -1.0, 0.0, ALU.mult, ALU.max), 9)
            fixed(TT(sp_t[:, 0, :], sp_t[:, 0, :], sp_t[:, 1, :], ALU.add), 10)
            TS(sp4[:, 0, :], sp_t[:, 0, :], 4.0, None, ALU.mult)
            TS(sp4[:, 1, :], sp_t[:, 0, :], -4.0, None, ALU.mult)
            TS(sp4[:, 2, :], vt[:, :, V_BA], 0.5, None, ALU.mult)
            TS(sp4[:, 3, :], vt[:, :, V_BX], 0.5, None, ALU.mult).then_inc(vt_ready, 1)

            def qk_scale(hp, j):
                n, u, g = hp * 6 + 2 * (j // 3) + j % 3, hp * 9 + j, j // 3
                dve.wait_ge(qk_root, n + 1)
                if n:
                    dve.wait_ge(qk_ready, n)
                dve.reciprocal(qk_ri[:, :], qk_rt[:, :]).then_inc(qk_rinv, 1)
                dve.wait_ge(qk_rinv, n + 1)
                dve.wait_ge(acc_free[u % 2], u // 2 + 1)
                dst = (qT if j % 3 else kT)[:, g, :]
                TT(by_class(dst[:, 0:SEQ]), in_time(qk_gn[:, n % 2, 0:SEQ]), in_time(qk_ri[:, 0:SEQ]), ALU.mult)
                TT(dst[:, SEQ:TOK], qk_gn[:, n % 2, SEQ:TOK], qk_ri[:, SEQ:TOK], ALU.mult).then_inc(qk_ready, 1)

            def mask_max(hp, r):
                e = hp * 5 + r
                dve.wait_ge(sc_ps, e + 1)
                if e >= 2:
                    dve.wait_ge(pT_ps, e - 1)
                if e >= 4:
                    dve.wait_ge(o_ready, e - 3)
                st = stat[:, e % 4, :]
                if r < 4:
                    rows, n0, n1, m0, m1 = P, 4 * P, 2 * P, C_PM + (3 - r) * P, C_PM + 7 * P
                else:
                    rows, n0, n1, m0, m1 = NS, 4 * P, NG * NS, C_SM, C_SM + 4 * P
                for i, (s0, n, m) in enumerate(((0, n0, m0), (512, n1, m1))):
                    last = dve.tensor_tensor_reduce(prob[0:rows, e % 2, s0:s0 + n], ps[2][0:rows, s0:s0 + n],
                                                    const[0:rows, m:m + n], SCALE, -3e38, ALU.add, ALU.max,
                                                    st[0:rows, i:i + 1])
                last.then_inc(sc_read, 1)
                dve.wait_ge(sc_read, e + 1)
                dve.tensor_reduce(st[0:rows, 2:3], st[0:rows, 0:2], AX_X, ALU.max, negate=True).then_inc(mx_ready, 1)

            def normed(hp, r):
                e = hp * 5 + r
                rows = P if r < 4 else NS
                st = stat[0:rows, e % 4, :]
                dve.wait_ge(p_ready, e + 1)
                dve.reciprocal(st[:, 4:5], st[:, 3:4]).then_inc(r_ready, 1)
                dve.wait_ge(r_ready, e + 1)
                dve.wait_ge(o_ps, e + 1)
                if e >= 2:
                    dve.wait_ge(at_ps, e - 1)
                TS(o_sb[0:rows, e % 2, :], ps[0][0:rows, 0:HD], st[:, 4:5], None, ALU.mult).then_inc(o_ready, 1)

            def out_lo(hp, r):
                e = hp * 5 + r
                dve.wait_ge(at_hi_rdy, e + 1)
                if r < 4:
                    TT(in_time(att_lo[:, hp, 0:SEQ])[:, :, r], ps[0][:, 512:512 + P],
                       in_time(att_hi[:, hp, 0:SEQ])[:, :, r], ALU.subtract).then_inc(at_ready, 1)
                else:
                    TT(att_lo[:, hp, SEQ:TOK], ps[0][:, 512:512 + NS], att_hi[:, hp, SEQ:TOK], ALU.subtract).then_inc(at_ready, 1)

            for hp in range(NH):
                for j in range(9):
                    lo_split(hp * 9 + j + NSPL)
                    if j and (j - 1) % 3 < 2:
                        qk_scale(hp, j - 1)
                dve.wait_ge(qk_ready, 6 * hp + 6)
                dve.wait_ge(s_zero, 2)
                if hp:
                    dve.wait_ge(q_dia_rdy, hp)
                for g in range(NG):
                    last = dve.tensor_copy(diag(q_dia[:, g, :]), qT[:, g, SEQ:TOK].rearrange("p (b t) -> p b t", b=NB))
                last.then_inc(q_dia_rdy, 1)
                for s in range(8):
                    if s < 4:
                        mask_max(hp, s)
                    if s == 4:
                        for b in range(0, NB, 2):
                            n = hp * NB + b
                            dve.wait_ge(kcT_ps, n + 1)
                            if n >= 2:
                                dve.wait_ge(kcT_used, n - 1)
                            dve.tensor_copy(kcT[:, n % 2, :], ps[1][:, 512 * (b % 2):512 * (b % 2) + 512]).then_inc(kcT_rdy[n % 2], 1)
                        mask_max(hp, 4)
                    if 0 <= s - 2 < 5:
                        normed(hp, s - 2)
                    if 0 <= s - 3 < 5:
                        out_lo(hp, s - 3)

            link = [0]

            def linked(ins):
                ins.then_inc(l_link, 1)
                link[0] += 1
                dve.wait_ge(l_link, link[0])

            for s in kv_out:
                dve.wait_ge(s, 32 * NH)
            dve.wait_ge(gw_zero, 3)

            def conv(c):
                u = U_LRU + 2 * c
                x, y, v = xa[:, c % 2, :], xc[:, c % 2, :], vt[:, c, :]
                if c >= 2:
                    dve.wait_ge(lst_rdy, c - 1)
                dve.tensor_copy(seqs(x[:, XS0:XW], XSEQ)[:, :, 0:XPAD], seqs(v[:, V_SC:V_H0], 3)).then_inc(xa_pad, 1)
                dve.wait_ge(xa_pad, c + 1)
                dve.wait_ge(acc_free[u % 2], u // 2 + 1)
                linked(TS(y[:, :], x[:, 0:LW], v[:, V_CW:V_CW + 1], v[:, V_CB:V_CB + 1], ALU.mult, ALU.add))
                for i in (1, 2, 3):
                    ins = STT(y[:, :], x[:, i:i + LW], v[:, V_CW + i:V_CW + i + 1], y[:, :], ALU.mult, ALU.add)
                    if i < 3:
                        linked(ins)
                    else:
                        ins.then_inc(xc_rdy, 1)

            def recur(c):
                pads = lambda b: seqs(b[:, SEQ:LW], XSEQ)[:, :, XPAD - 1]
                dve.wait_ge(gate_read, c + 1)
                linked(STT(g_i[:, :], g_i[:, :], 1.0, xc[:, c % 2, :], ALU.add, ALU.mult))
                dve.wait_ge(as_rdy, c + 1)
                dve.wait_ge(a2_rdy, c + 1)
                STT(a_s[:, :], a_2[:, :], 1.0, a_s[:, :], ALU.add, ALU.mult).then_inc(m2_rdy, 1)
                dve.memset(pads(a_a[:, :]), 0.0)
                dve.wait_ge(mul_rdy, c + 1)
                linked(dve.memset(a_s[:, 0:1], 1.0))
                linked(STT(l_u[:, :], g_i[:, :], 0.5, a_s[:, :], ALU.mult, ALU.mult))
                linked(dve.tensor_copy(pads(l_u[:, :]), vt[:, c, V_H0:V_N]))
                if c:
                    dve.wait_ge(lst_rdy, c)
                    dve.wait_ge(y_lo_rdy, c)
                linked(dve.tensor_tensor_scan(l_h[:, :], a_a[:, :], l_u[:, :], 0.0, ALU.mult, ALU.add))
                g_ = ga[:, c % 2, :]
                u = U_LRU + 2 * c + 1
                dve.wait_ge(acc_free[u % 2], u // 2 + 1)
                TT(l_y[:, 0:SEQ], l_h[:, 0:SEQ], g_[:, 0:SEQ], ALU.mult)
                hs = seqs(l_h[:, SEQ:LW], XSEQ)[:, :, XPAD:XSEQ]
                TT(seqs(l_y[:, SEQ:TOK], NT), hs, seqs(g_[:, SEQ:TOK], NT), ALU.mult).then_inc(y_rdy, 1)
                x = xa[:, c % 2, :]
                dve.tensor_copy(l_st[:, c, 0:3], x[:, XS0 - 3:XS0])
                dve.tensor_copy(seqs(l_st[:, c, 3:27], 3), seqs(x[:, XS0:XW], XSEQ)[:, :, XSEQ - 3:XSEQ])
                dve.tensor_copy(l_st[:, c, 27:28], l_h[:, SEQ - 1:SEQ])
                dve.tensor_copy(l_st[:, c, 28:36], hs[:, :, NT - 1]).then_inc(lst_rdy, 1)
                dve.wait_ge(y_hi_rdy, c + 1)
                TT(y_lo[:, c, :], l_y[:, :], y_hi[:, c, :], ALU.subtract).then_inc(y_lo_rdy, 1)

            for c in range(KT + 1):
                if c < KT:
                    lo_split(U_LRU + 2 * c + NSPL)
                    conv(c)
                    lo_split(U_LRU + 2 * c + 1 + NSPL)
                if c:
                    recur(c - 1)

            for m in range(KT):
                for j in range(4):
                    u = U_MRG + 4 * m + j
                    lo_split(u + NSPL)
                    if j % 2:
                        dve.wait_ge(unit_done, u + 1)
                        sg = sg_b if j == 3 else sg_a
                        dve.wait_ge(acc_free[(u - 1) % 2], (u - 1) // 2 + 1)
                        if m:
                            dve.wait_ge(mg_lo_rdy, m)
                            dve.wait_ge(mg_hi_rdy, m)
                        TT(mg_s[:, j // 2, :].rearrange("p (h n) -> p h n", h=2), acc[u % 2],
                           sg[:, :].rearrange("p (h n) -> p h n", h=2), ALU.mult).then_inc(acc_free[u % 2], 1)
                    if m and j == 0:
                        dve.wait_ge(mg_hi_rdy, m)
                        TT(mg_lo[:, m - 1, :], mg_s[:, 0, :], mg_hi[:, m - 1, :], ALU.subtract).then_inc(mg_lo_rdy, 1)
                u = U_MRG + 4 * m
                for q in (1, 3):
                    dve.wait_ge(acc_free[(u + q) % 2], (u + q) // 2 + 1)
                TT(mg_s[:, 0, :], mg_s[:, 0, :], mg_s[:, 1, :], ALU.add).then_inc(mg_rdy, 1)
            dve.wait_ge(mg_hi_rdy, KT)
            TT(mg_lo[:, KT - 1, :], mg_s[:, 0, :], mg_hi[:, KT - 1, :], ALU.subtract).then_inc(mg_lo_rdy, 1)

            for c in range(KT):
                u = U_OUT + c
                lo_split(u + NSPL)
                dve.wait_ge(unit_done, u + 1)
                dve.wait_ge(x2_cp, c + 1)
                TT(x2[:, c, :].rearrange("p (h n) -> p h n", h=2), acc[u % 2],
                   xs[:, :].rearrange("p (h n) -> p h n", h=2), ALU.add).then_inc(acc_free[u % 2], 1)
            dve.wait_ge(root2_rdy, 1)
            for c in (KT - 2, KT - 1):
                taken(dve, U_OUT + c)
            dve.reciprocal(rinv2[:, :], root2[:, :]).then_inc(rinv2_rdy, 1)
            dve.wait_ge(rinv2_rdy, 1)
            for c in range(KT):
                if c >= 2:
                    dve.wait_ge(hn2_hi, c - 1)
                    dve.wait_ge(hn2_lo, c - 1)
                STT(hn2[:, c % 2, :], x2[:, c, :], vt[:, c, V_N2:V_N2 + 1], rinv2[:, :], ALU.mult, ALU.mult).then_inc(hn2_rdy, 1)
                if c:
                    dve.wait_ge(hn2_hi, c)
                    TT(h_lo[:, c - 1, :], hn2[:, (c - 1) % 2, :], h_hi[:, c - 1, :], ALU.subtract).then_inc(hn2_lo, 1)
            dve.wait_ge(hn2_hi, KT)
            TT(h_lo[:, KT - 1, :], hn2[:, (KT - 1) % 2, :], h_hi[:, KT - 1, :], ALU.subtract).then_inc(hn2_lo, 1)

            dve.wait_ge(hn2_lo, KT)
            dve.memset(ug[:, :, 0:UPAD], 0.0).then_inc(u_pad, 1)
            dve.memset(uv[:, :, 0:UPAD], 0.0).then_inc(u_pad, 1)
            flink = [0]

            def flinked(ins):
                ins.then_inc(f_link, 1)
                flink[0] += 1
                dve.wait_ge(f_link, flink[0])

            def ffn_conv(i, j):
                u, ti = up_unit(i) + j, i + j * FT
                x, y, v = (uv if j else ug)[:, i % 2, :], cv if j else cg, ft[:, ti, :]
                flinked(dve.tensor_copy(seqs(x[:, US0:UW], USEQ)[:, :, 0:UPAD], seqs(v[:, F_S:F_N], 2)))
                dve.wait_ge(acc_free[u % 2], u // 2 + 1)
                if j == 0 and i:
                    dve.wait_ge(gm_rdy, i)
                flinked(TS(y[:, :], x[:, 0:CW], v[:, F_W:F_W + 1], v[:, F_B:F_B + 1], ALU.mult, ALU.add))
                flinked(STT(y[:, :], x[:, 1:1 + CW], v[:, F_W + 1:F_W + 2], y[:, :], ALU.mult, ALU.add))
                STT(y[:, :], x[:, 2:2 + CW], v[:, F_W + 2:F_W + 3], y[:, :], ALU.mult, ALU.add).then_inc(cv_rdy if j else cg_rdy, 1)

            def product(i):
                dve.wait_ge(gl_rdy, i + 1)
                dve.wait_ge(cv_rdy, i + 1)
                if i:
                    dve.wait_ge(g_hi_rdy, i)
                    dve.wait_ge(g_lo_rdy, i)
                TT(gm[:, 0:SEQ], cg[:, 0:SEQ], cv[:, 0:SEQ], ALU.mult)
                ss = lambda b: b[:, SEQ:CW].rearrange("p (b n) -> p b n", n=USEQ)[:, :, UPAD:USEQ]
                TT(seqs(gm[:, SEQ:TOK], NT), ss(cg), ss(cv), ALU.mult).then_inc(gm_rdy, 1)
                q = i % PPR
                if q == 0 and i:
                    dve.wait_ge(fst_ps, i // PPR)
                for j, b in enumerate((ug, uv)):
                    x = b[:, i % 2, :]
                    dve.tensor_copy(f_st[:, j * PPR + q, 0:2], x[:, US0 - 2:US0])
                    last = dve.tensor_copy(seqs(f_st[:, j * PPR + q, 2:18], 2), seqs(x[:, US0:UW], USEQ)[:, :, USEQ - 2:USEQ])
                last.then_inc(fst_rdy, 1)
                dve.wait_ge(g_hi_rdy, i + 1)
                TT(g_lo[(i // PPR) % 2][:, i % PPR, :], gm[:, :], g_hi[(i // PPR) % 2][:, i % PPR, :], ALU.subtract).then_inc(g_lo_rdy, 1)

            for kind, i, m in ffn_steps():
                if kind == "up":
                    for j in range(2):
                        lo_split(up_unit(i) + j + NSPL)
                        ffn_conv(i, j)
                    product(i)
                else:
                    u = down_unit(i, m)
                    lo_split(u + NSPL)
                    dve.wait_ge(unit_done, u + 1)
                    TT(x2[:, m, :].rearrange("p (h n) -> p h n", h=2), acc[u % 2],
                       x2[:, m, :].rearrange("p (h n) -> p h n", h=2), ALU.add).then_inc(acc_free[u % 2], 1)


def constants(np):
    c = np.zeros((P, C_N), np.float32)
    c[:, C_ID:C_ID + P] = np.eye(P)
    c[:, C_ONE:C_ONE + P] = 1.0
    i, j = np.arange(P)[:, None], np.arange(P)[None, :]
    d = i - j
    below, same, above = (d >= 0) & (d <= 31), (d >= 0) & (d <= 32), (d >= 1) & (d <= 32)
    strip = [below] * 3 + [same] + [above] * 3
    strip += [d >= 0, (d >= 0) & (d % 4 == 0)]
    c[:, C_PM:C_PM + 9 * P] = np.where(np.concatenate(strip, 1), 0.0, NEG)
    b, t = np.divmod(np.arange(NS), NT)
    t = t[:, None]
    k = np.arange(PAST)[None, :]
    own = [np.arange(P)[None, :] >= t,
           (k - t) % 4 == 0,
           np.arange(P)[None, :] % NT == t]
    b2, t2 = np.divmod(np.arange(NS)[None, :], NT)
    mine = (b[:, None] == b2) & (t2 <= t)
    own += [mine, mine & ((t - t2) % 4 == 0), mine & (t == t2)]
    c[0:NS, C_SM:C_SM + 4 * P + NG * NS] = np.where(np.concatenate(own, 1), 0.0, NEG)
    c[:, C_EPS] = EPS
    return c


_INS = ["x_prompt", "x_sample", "state_lru_h", "state_lru_conv", "cache_k_g0", "cache_v_g0", "cache_k_g1", "cache_v_g1",
        "cache_k_g2", "cache_v_g2", "state_ffn_conv", "norm1_g", "w_in", "conv_a_w", "conv_a_b", "lru_wa", "lru_ba",
        "lru_wx", "lru_bx", "lru_lambda", "q_norm_g", "k_norm_g", "w_br_a", "w_br_b", "w_out", "norm2_g", "w_up",
        "conv_f_w", "conv_f_b", "w_down"]
_KV = [(P, P), (SEQ, SEQ), (SEQ, SEQ)]
_OUTS = ([(1, SEQ, D), (NB, NT, D), (1, 1, D), (1, 1, 3, D)]
         + [(1, 1, n, NH, HD) for pair in _KV for n in pair] + [(1, 1, 2, 2 * DFF)]
         + [(1, NB, D), (1, NB, 3, D)] + [(1, NB, NT, NH, HD)] * 6 + [(1, NB, 2, 2 * DFF)])


def kernel(**inputs):
    import numpy as np
    import concourse.bacc as bacc
    from concourse.bass_utils import run_bass_kernel_spmd

    nc = bacc.Bacc("TRN2", target_bir_lowering=False, num_devices=1)
    arrays = {f"in_{name}": np.ascontiguousarray(inputs[name]) for name in _INS}
    arrays["in_consts"] = constants(np)
    t = {name[3:]: nc.dram_tensor(name, a.shape, mybir.dt.from_np(a.dtype), kind="ExternalInput").ap()
         for name, a in arrays.items()}
    t["out"] = [nc.dram_tensor(f"out_{i}", shape, F32, kind="ExternalOutput").ap() for i, shape in enumerate(_OUTS)]
    build(nc, t)
    r = run_bass_kernel_spmd(nc, [arrays], core_ids=[0])
    return tuple(r.results[0][f"out_{i}"] for i in range(len(_OUTS)))
```

```python
from contextlib import ExitStack

import concourse.bass as bass
from concourse import mybir

F32 = mybir.dt.float32
F32R = mybir.dt.float32r
ALU = mybir.AluOpType
ACT = mybir.ActivationFunctionType
AX_X = mybir.AxisListType.X

P = 128
D = 1024
KT = D // P
SEQ = 512
NB, NT = 8, 8
NS = NB * NT
TOK = SEQ + NS
HALF = TOK // 2
PAST = 256
NG, NH, HD = 3, 4, 128
AW = NG * NH * HD
DFF = 3 * D
FT = DFF // P
NCLS = 4
XA0, GA0, Q0, K0, V0, GTA0, GTB0 = 0, D, 2 * D, 2 * D + AW, 2 * D + 2 * AW, 2 * D + 3 * AW, 3 * D + 3 * AW
SCALE = HD ** -0.5
EPS = 1e-6
NEG = -1e30

C_ID, C_ONE, C_PM = 0, P, 2 * P
C_SM = C_PM + 9 * P
C_EPS = C_SM + 4 * P + NG * NS
C_N = C_EPS + 1

V_CW, V_CB, V_BA, V_BX, V_LAM, V_N1, V_N2, V_SC, V_H0 = 0, 4, 5, 6, 7, 8, 9, 10, 34
V_N = 42
F_W, F_B, F_S, F_N = 0, 3, 4, 20

XPAD, XSEQ = 3, 3 + NT
XS0 = XPAD + SEQ
XW = XS0 + NB * XSEQ
LW = XW - XPAD
LS0 = XS0
UPAD, USEQ = 2, 2 + NT
US0 = UPAD + SEQ
UW = US0 + NB * USEQ
CW = UW - UPAD

NRAW, NSPL = 4, 2
U_LRU = 9 * NH
U_MRG = U_LRU + 2 * KT
U_OUT = U_MRG + 4 * KT
U_FFN = U_OUT + KT
U_ALL = U_FFN + 2 * FT + 3 * KT
NPAIR, NRND = FT, 3
NHN = 4
PPR = NPAIR // NRND


def up_unit(i):
    return U_FFN + 2 * i + KT * min((i - 1) // PPR if i else 0, NRND - 1)


def down_unit(r, m):
    pairs = min((r + 1) * PPR + 1, NPAIR)
    return U_FFN + 2 * pairs + KT * r + m


def ffn_steps():
    for i in range(NPAIR):
        yield "up", i, 0
        for r in range(NRND):
            if i == min((r + 1) * PPR, NPAIR - 1):
                for m in range(KT):
                    yield "down", r, m


ATT_PE = "S1 P0 S2 V0 P1 S3 V1 O0 P2 S4 V2 O1 P3 V3 O2 O3".split()
ATT_ACT = "E0 P0 E1 E2 P1 E3 H0 P2 E4 H1 P3 H2 H3".split()
ATT_DVE = "M0 M1 M2 N0 M3 N1 L0 M4 N2 L1 N3 L2 L3".split()


def build(nc, t):
    w_in = t["w_in"][0].rearrange("(k p) n -> p k n", p=P)
    w_br_a = t["w_br_a"][0].rearrange("(k p) n -> p k n", p=P)
    w_br_b = t["w_br_b"][0].rearrange("(k p) n -> p k n", p=P)
    w_out = t["w_out"][0].rearrange("(k p) n -> p k n", p=P)
    w_up = t["w_up"][0].rearrange("(k p) n -> p k n", p=P)
    w_down = t["w_down"][0].rearrange("(k p) n -> p k n", p=P)
    out = t["out"]

    def cols(w, c, k0=0, kn=KT):
        return w[:, k0:k0 + kn, c:c + P]

    units = []
    for hp in range(NH):
        for g in range(NG):
            for base in (K0, Q0):
                units.append(cols(w_in, base + (g * NH + hp) * HD))
        for g in range(NG):
            units.append(cols(w_in, V0 + (g * NH + hp) * HD))
    for c in range(KT):
        units += [cols(w_in, XA0 + c * P), cols(w_in, GA0 + c * P)]
    for m in range(KT):
        units += [cols(w_in, GTA0 + m * P), cols(w_in, GTB0 + m * P),
                  cols(w_br_b, m * P, 0, NH), cols(w_br_a, m * P)]
    for m in range(KT):
        units.append(cols(w_out, m * P))
    for kind, i, m in ffn_steps():
        if kind == "up":
            assert up_unit(i) == len(units)
            units += [cols(w_up, i * P), cols(w_up, DFF + i * P)]
        else:
            assert down_unit(i, m) == len(units)
            units.append(cols(w_down, m * P, i * PPR, PPR))
    assert len(units) == U_ALL
    nkt = [u.shape[1] for u in units]

    ctx = ExitStack()
    with ctx:
        def sb(name, shape, dt=F32, at=ctx):
            return at.enter_context(nc.sbuf_tensor(name, shape, dt))

        def sem(name):
            return ctx.enter_context(nc.semaphore(name))

        const = sb("const", [P, C_N])
        vt = sb("vt", [P, KT, V_N])
        ft = sb("ft", [P, 2 * FT, F_N])
        qkg = sb("qkg", [P, 2 * NG])
        sp4 = sb("sp4", [P, 4, KT])
        sp_t = sb("sp_t", [P, 2, KT])
        w_raw = sb("w_raw", [P, NRAW, KT, P])
        w_hi = sb("w_hi", [P, NSPL, KT, P], F32R)
        w_lo = sb("w_lo", [P, NSPL, KT, P], F32R)
        h_hi = sb("h_hi", [P, KT, TOK], F32R)
        h_lo = sb("h_lo", [P, KT, TOK], F32R)
        ident, ones = const[:, C_ID:C_ID + P], const[:, C_ONE:C_ONE + P]
        eps = const[:, C_EPS:C_EPS + 1]

        with ExitStack() as m:
            nat_v = sb("nat_v", [V_N, D], at=m)
            nat_f = sb("nat_f", [F_N, 2 * DFF], at=m)
            nat_g = sb("nat_g", [2 * NG, P], at=m)
            x_tok = sb("x_tok", [P, 5, D], at=m)
            x_t = sb("x_t", [P, KT, TOK], at=m)
            sq = sb("sq", [P, 2, TOK], at=m)
            root = sb("root", [P, TOK], at=m)
            rinv = sb("rinv", [P, TOK], at=m)
            hn = sb("hn", [P, NHN, TOK], at=m)
        mid = ExitStack()
        att_hi = sb("att_hi", [P, NH, TOK], F32R, mid)
        att_lo = sb("att_lo", [P, NH, TOK], F32R, mid)
        with ExitStack() as m:
            kT = sb("kT", [P, NG, TOK], at=m)
            qT = sb("qT", [P, NG, TOK], at=m)
            k_tok = sb("k_tok", [P, 5, NG, HD], at=m)
            v_tok = sb("v_tok", [P, 5, NG, HD], at=m)
            qk_sq = sb("qk_sq", [P, TOK], at=m)
            qk_gn = sb("qk_gn", [P, 2, TOK], at=m)
            qk_rt = sb("qk_rt", [P, TOK], at=m)
            qk_ri = sb("qk_ri", [P, TOK], at=m)
            vT = sb("vT", [P, TOK], at=m)
            prob = sb("prob", [P, 2, 6 * P], at=m)
            probT = sb("probT", [P, 6 * P], at=m)
            q_dia = sb("q_dia", [P, NG, NB * (NS + NT)], at=m)
            p_dia = sb("p_dia", [P, 4, NB * (NS + NT)], at=m)
            p_new = sb("p_new", [NS, NG * NS], at=m)
            NKC = 6
            kc = sb("kc", [P, NKC, 4, HD], at=m)
            vc = sb("vc", [P, NB, 4, HD], at=m)
            kcT = sb("kcT", [P, 2, 4 * P], at=m)
            o_sb = sb("o_sb", [P, 2, HD], at=m)
            stat = sb("stat", [P, 4, 8], at=m)
        l_st = sb("l_st", [P, KT, 36], at=mid)
        l_row = sb("l_row", [36, D], at=mid)
        y_hi = sb("y_hi", [P, KT, TOK], F32R, mid)
        y_lo = sb("y_lo", [P, KT, TOK], F32R, mid)
        with ExitStack() as m:
            wa = sb("wa", [P, KT, P], at=m)
            wx = sb("wx", [P, KT, P], at=m)
            xa = sb("xa", [P, 2, XW], at=m)
            xc = sb("xc", [P, 2, LW], at=m)
            ga = sb("ga", [P, 2, TOK], at=m)
            g_r = sb("g_r", [P, LW], at=m)
            g_i = sb("g_i", [P, LW], at=m)
            a_s = sb("a_s", [P, LW], at=m)
            a_a = sb("a_a", [P, LW], at=m)
            a_2 = sb("a_2", [P, LW], at=m)
            l_u = sb("l_u", [P, LW], at=m)
            l_h = sb("l_h", [P, LW], at=m)
            l_y = sb("l_y", [P, TOK], at=m)
        with ExitStack() as m:
            mg_hi = sb("mg_hi", [P, KT, TOK], F32R, m)
            mg_lo = sb("mg_lo", [P, KT, TOK], F32R, m)
            sg_a = sb("sg_a", [P, TOK], at=m)
            sg_b = sb("sg_b", [P, TOK], at=m)
            mg_s = sb("mg_s", [P, 2, TOK], at=m)
        mid.close()
        x2 = sb("x2", [P, KT, TOK])
        with ExitStack() as m:
            x_tok2 = sb("x_tok2", [P, 5, D], at=m)
            sq2 = sb("sq2", [P, 2, TOK], at=m)
            xs = sb("xs", [P, TOK], at=m)
            root2 = sb("root2", [P, TOK], at=m)
            rinv2 = sb("rinv2", [P, TOK], at=m)
            hn2 = sb("hn2", [P, NHN, TOK], at=m)
        g_hi, g_lo = [sb("g_hi0", [P, PPR, TOK], F32R)], [sb("g_lo0", [P, PPR, TOK], F32R)]
        ug = sb("ug", [P, 2, UW])
        uv = sb("uv", [P, 2, UW])
        cg = sb("cg", [P, CW])
        cv = sb("cv", [P, CW])
        gm = sb("gm", [P, TOK])
        f_st = sb("f_st", [P, 2 * PPR, 18])
        f_row = sb("f_row", [18, 4, 4 * P])
        with ExitStack() as m:
            g_hi.append(sb("g_hi1", [P, PPR, TOK], F32R, m))
            g_lo.append(sb("g_lo1", [P, PPR, TOK], F32R, m))
        y_tok = sb("y_tok", [P, 5, D])

        ps = [ctx.enter_context(nc.psum_tensor(f"ps{i}", [P, 1024], F32)) for i in range(4)]
        acc = [p[:, :].rearrange("p (h n) -> p h n", h=2)[:, :, 0:HALF] for p in ps]
        NORM, TRN = 2, 3

        s_const, s_nat = sem("s_const"), sem("s_nat")
        x_in = [sem(f"x_in{i}") for i in range(4)]
        raw_in = [sem(f"raw_in{i}") for i in range(NRAW)]
        hi_ready, lo_ready, unit_done = sem("hi_ready"), sem("lo_ready"), sem("unit_done")
        acc_free = [sem("acc_free0"), sem("acc_free1")]
        vt_ps, vt_ready, tab_link = sem("vt_ps"), sem("vt_ready"), sem("tab_link")
        x_ps, x_copied, sq_ready, sq_used = sem("x_ps"), sem("x_copied"), sem("sq_ready"), sem("sq_used")
        root_ready, rinv_ready, hn_ready, hn_hi = (sem(x) for x in ("root_ready", "rinv_ready", "hn_ready", "hn_hi"))
        hn_lo, hn2_lo = ([sem(f"{x}{i}") for i in range(2)] for x in ("hn_lo", "hn2_lo"))
        qk_sqd, qk_sum, qk_root, qk_rinv, qk_ready = (sem(x) for x in ("qk_sqd", "qk_sum", "qk_root", "qk_rinv", "qk_ready"))
        tok_ps, tok_ready = sem("tok_ps"), sem("tok_ready")
        kv_out = [sem(f"kv_out{i}") for i in range(2 * NG)]
        s_zero, q_dia_rdy = sem("s_zero"), sem("q_dia_rdy")
        sc_ps, sc_read, mx_ready, p_ready, pT_ps, pT_ready = (sem(x) for x in ("sc_ps", "sc_read", "mx_ready", "p_ready", "pT_ps", "pT_ready"))
        o_ps, r_ready, o_ready, at_ps, at_hi_rdy, at_ready = (sem(x) for x in ("o_ps", "r_ready", "o_ready", "at_ps", "at_hi_rdy", "at_ready"))
        kc_in = [sem(f"kc_in{i}") for i in range(NKC)]
        vc_in = sem("vc_in")
        kcT_ps, kcT_used = sem("kcT_ps"), sem("kcT_used")
        kcT_rdy = [sem("kcT_rdy0"), sem("kcT_rdy1")]
        gw_zero, gw_in = sem("gw_zero"), sem("gw_in")
        l_link, xa_pad, xc_rdy, gate_ps, gate_read = (sem(x) for x in ("l_link", "xa_pad", "xc_rdy", "gate_ps", "gate_read"))
        as_rdy, aa_rdy, a2_rdy, m2_rdy, mul_rdy, y_rdy, y_hi_rdy, y_lo_rdy = (sem(x) for x in ("as_rdy", "aa_rdy", "a2_rdy", "m2_rdy", "mul_rdy", "y_rdy", "y_hi_rdy", "y_lo_rdy"))
        lst_rdy, lst_ps, lrow_rdy, l_out = sem("lst_rdy"), sem("lst_ps"), sem("lrow_rdy"), sem("l_out")
        mg_link, mg_rdy, mg_hi_rdy, mg_lo_rdy, br_b_rdy = (sem(x) for x in ("mg_link", "mg_rdy", "mg_hi_rdy", "mg_lo_rdy", "br_b_rdy"))
        x2_in, x2_ps, x2_cp, sq2_rdy, sq2_used = (sem(x) for x in ("x2_in", "x2_ps", "x2_cp", "sq2_rdy", "sq2_used"))
        root2_rdy, rinv2_rdy, hn2_rdy, hn2_hi = (sem(x) for x in ("root2_rdy", "rinv2_rdy", "hn2_rdy", "hn2_hi"))
        u_pad, f_link, cg_rdy, gl_rdy, cv_rdy, gm_rdy, g_hi_rdy, g_lo_rdy = (sem(x) for x in ("u_pad", "f_link", "cg_rdy", "gl_rdy", "cv_rdy", "gm_rdy", "g_hi_rdy", "g_lo_rdy"))
        fst_rdy, fst_ps, frow_rdy, f_out = sem("fst_rdy"), sem("fst_ps"), sem("frow_rdy"), sem("f_out")
        yt_ps, yt_rdy, y_out = sem("yt_ps"), sem("yt_rdy"), sem("y_out")
        l_gr, ln_fix = sem("l_gr"), sem("ln_fix")

        def diag(row):
            return row.rearrange("p (b n) -> p b n", n=NS + NT)[:, :, 0:NT]

        def o_bank(i):
            return ps[TRN][:, 6 * P:7 * P] if i == 4 else ps[0][0:P if i else NS, 0:HD]

        def oT_bank(i):
            return ps[TRN][:, 7 * P:8 * P] if i == 4 else ps[0][:, 512:512 + (P if i else NS)]

        def out_cols(buf, hp, i):
            return in_time(buf[:, hp, 0:SEQ])[:, :, i - 1] if i else buf[:, hp, SEQ:TOK]

        def by_class(ap):
            return ap.rearrange("p (r i) -> p i r", r=NCLS)

        def in_time(ap):
            return ap.rearrange("p (i r) -> p i r", r=NCLS)

        def seqs(ap, width):
            return ap.rearrange("p (b n) -> p b n", n=width)

        def taken(eng, u):
            eng.wait_ge(acc_free[u % 2], u // 2 + 1)

        block = ctx.enter_context(nc.Block())

        @block.sync
        def _(sp):
            for q in range(4):
                c = slice(q * D // 4, (q + 1) * D // 4)
                sp.dma_start(x_tok[:, 0:4, c], t["x_prompt"][0].rearrange("(n p) d -> p n d", p=P)[:, :, c]).then_inc(x_in[q], 16)
                sp.dma_start(x_tok[0:NS, 4, c], t["x_sample"].rearrange("b t d -> (b t) d")[:, c]).then_inc(x_in[q], 16)
                if q == 0:
                    sp.dma_start(const[:, :], t["consts"]).then_inc(s_const, 16)
            for u, src in enumerate(units):
                if u >= NRAW:
                    sp.wait_ge(lo_ready, u - NRAW + 1)
                sp.dma_start(w_raw[:, u % NRAW, 0:nkt[u], :], src).then_inc(raw_in[u % NRAW], 16)

        @block.gpsimd
        def _(pool):
            def odd_lows(buf, ready, his, los):
                for c in range(1, KT, 2):
                    pool.wait_ge(his, c + 1)
                    pool.tensor_tensor(h_lo[:, c, :], buf[:, c % NHN, :], h_hi[:, c, :], ALU.subtract).then_inc(los[1], 1)

            odd_lows(hn, hn_ready, hn_hi, hn_lo)
            pool.wait_ge(hn_lo[0], KT // 2)
            pool.wait_ge(hn_lo[1], KT // 2)
            pool.wait_ge(vt_ready, 3)
            pool.memset(q_dia[:, :, :], 0.0).then_inc(s_zero, 1)
            pool.memset(p_dia[:, :, :], 0.0).then_inc(s_zero, 1)

            def load_k(hp, b):
                n = hp * NB + b
                if n >= NKC:
                    pool.wait_ge(kcT_ps, n - NKC + 1)
                d = kc[:, n % NKC, :, :]
                s = kc_in[n % NKC]
                pool.dma_start(d[:, 0, :], t["cache_k_g0"][0, b, :, hp, :]).then_inc(s, 16)
                pool.dma_start(d[:, 1:3, :], t["cache_k_g1"][0, b, :, hp, :].rearrange("(n p) d -> p n d", p=P)).then_inc(s, 16)
                pool.dma_start(d[:, 3, :], t["cache_k_g2"][0, b, :, hp, :].rearrange("(c s) d -> c s d", s=16)[:, 0:NT, :]).then_inc(s, 16)

            def load_v(hp):
                if hp:
                    pool.wait_ge(o_ps, 5 * hp - 4)
                for b in range(NB):
                    d = vc[:, b, :, :]
                    pool.dma_start(d[:, 0, :], t["cache_v_g0"][0, b, :, hp, :]).then_inc(vc_in, 16)
                    pool.dma_start(d[:, 1:3, :], t["cache_v_g1"][0, b, :, hp, :].rearrange("(n p) d -> p n d", p=P)).then_inc(vc_in, 16)
                    pool.dma_start(d[:, 3, :], t["cache_v_g2"][0, b, :, hp, :].rearrange("(c s) d -> c s d", s=16)[:, 0:NT, :]).then_inc(vc_in, 16)

            for hp in range(NH):
                load_v(hp)
                for b in range(min(NKC, NB)):
                    load_k(hp, b)
                for kv, buf in enumerate((k_tok, v_tok)):
                    for g in range(NG):
                        pool.wait_ge(tok_ready, hp * 6 + NG * kv + g + 1)
                        o_p, o_s = out[4 + 2 * g + kv][0, 0], out[13 + 2 * g + kv]
                        s = kv_out[2 * g + kv]
                        if g == 0:
                            dst = o_p[:, hp, :].rearrange("(i r) d -> i r d", r=NCLS)
                            pool.dma_start(dst, buf[P - SEQ // 16:P, 0:4, g, :]).then_inc(s, 16)
                        else:
                            dst = o_p[:, hp, :].rearrange("(i r) d -> i r d", r=NCLS)
                            pool.dma_start(dst, buf[:, 0:4, g, :]).then_inc(s, 16)
                        pool.dma_start(o_s[0, :, :, hp, :].rearrange("b t d -> (b t) d"), buf[0:NS, 4, g, :]).then_inc(s, 16)
                for b in range(NKC, NB):
                    load_k(hp, b)
            pool.wait_ge(at_ready, 5 * NH)
            for s in kv_out:
                pool.wait_ge(s, 32 * NH)
            pool.memset(wa[:, :, :], 0.0).then_inc(gw_zero, 1)
            pool.memset(wx[:, :, :], 0.0).then_inc(gw_zero, 1)
            pool.memset(xa[:, :, 0:XPAD], 0.0).then_inc(gw_zero, 1)
            pool.wait_ge(gw_zero, 3)
            for buf, name in ((wa, "lru_wa"), (wx, "lru_wx")):
                src = t[name][0].rearrange("(c j) d e -> j d c e", j=2)
                for j in range(2):
                    pool.dma_start(buf[64 * j:64 * j + 64, :, 64 * j:64 * j + 64], src[j]).then_inc(gw_in, 16)
            for c in range(KT):
                pool.wait_ge(aa_rdy, c + 1)
                if c:
                    pool.wait_ge(m2_rdy, c)
                pool.tensor_tensor(a_2[:, :], a_a[:, :], a_a[:, :], ALU.mult).then_inc(a2_rdy, 1)
            pool.wait_ge(lrow_rdy, 1)
            pool.dma_start(out[3][0, 0], l_row[0:3, :]).then_inc(l_out, 16)
            pool.dma_start(out[12][0].rearrange("b s d -> (b s) d"), l_row[3:27, :]).then_inc(l_out, 16)
            pool.dma_start(out[2][0], l_row[27:28, :]).then_inc(l_out, 16)
            pool.dma_start(out[11][0], l_row[28:36, :]).then_inc(l_out, 16)
            pool.wait_ge(l_out, 64)
            pool.wait_ge(unit_done, U_OUT)
            pool.dma_start(x_tok2[:, 0:4, :], t["x_prompt"][0].rearrange("(n p) d -> p n d", p=P)).then_inc(x2_in, 16)
            pool.dma_start(x_tok2[0:NS, 4, :], t["x_sample"].rearrange("b t d -> (b t) d")).then_inc(x2_in, 16)
            odd_lows(hn2, hn2_rdy, hn2_hi, hn2_lo)
            for r in range(NRND):
                pool.wait_ge(frow_rdy, 4 * (r + 1))
                for half in range(2):
                    for q in range(2):
                        c0 = half * DFF + r * PPR * P + q * 4 * P
                        src = f_row[:, 2 * half + q, :]
                        pool.dma_start(out[10][0, 0, :, c0:c0 + 4 * P], src[0:2, :]).then_inc(f_out, 16)
                        pool.dma_start(out[19][0].rearrange("b s d -> (b s) d")[:, c0:c0 + 4 * P], src[2:18, :]).then_inc(f_out, 16)
            for m in range(KT):
                pool.wait_ge(yt_rdy, m + 1)
                pool.dma_start(out[0][0].rearrange("(n p) d -> p n d", p=P)[:, :, m * P:(m + 1) * P],
                               y_tok[:, 0:4, m * P:(m + 1) * P]).then_inc(y_out, 16)
                pool.dma_start(out[1].rearrange("b t d -> (b t) d")[:, m * P:(m + 1) * P],
                               y_tok[0:NS, 4, m * P:(m + 1) * P]).then_inc(y_out, 16)
            for s in kv_out:
                pool.wait_ge(s, 32 * NH)
            pool.wait_ge(l_out, 64)
            pool.wait_ge(f_out, 16 * 8 * NRND)
            pool.wait_ge(y_out, 32 * KT)

        @block.tensor
        def _(pe):
            mm, tr = pe.matmul, pe.transpose

            def unit(u, x_hi, x_lo, ready=None, middle=None):
                pe.wait_ge(lo_ready, u + 1)
                if u >= 2:
                    pe.wait_ge(acc_free[u % 2], u // 2)
                a, n = ps[u % 2], nkt[u]
                for k in range(n):
                    if ready:
                        ready(k)
                    if middle and k == n // 2:
                        middle()
                    for w, x in ((w_hi, x_hi), (w_hi, x_lo), (w_lo, x_hi)):
                        for h in range(2):
                            last = mm(a[:, 512 * h:512 * h + HALF], w[:, u % NSPL, k, :],
                                      x[:, k, HALF * h:HALF * (h + 1)],
                                      start=(k == 0 and x is x_hi and w is w_hi), stop=(k == n - 1 and w is w_lo))
                last.then_inc(unit_done, 1)

            def feature_sum(src, k, n):
                for h in range(2):
                    last = mm(ps[NORM][:, 512 * h:512 * h + HALF], ones, src[:, HALF * h:HALF * (h + 1)],
                              start=(k == 0), stop=(k == n - 1))
                return last

            pe.wait_ge(s_const, 16)
            for c in range(KT + 1):
                if c < KT:
                    pe.wait_ge(x_in[4 * c // KT], 32)
                    if c >= 2:
                        pe.wait_ge(x_copied, c - 1)
                    for n in range(4):
                        tr(ps[c % 2][:, n * P:(n + 1) * P], x_tok[:, n, c * P:(c + 1) * P], ident)
                    tr(ps[c % 2][:, SEQ:TOK], x_tok[0:NS, 4, c * P:(c + 1) * P], ident[0:NS, 0:NS]).then_inc(x_ps, 1)
                if c:
                    pe.wait_ge(sq_ready, c)
                    feature_sum(sq[:, (c - 1) % 2, :], c - 1, KT).then_inc(sq_used, 1)
            pe.wait_ge(s_nat, 16 * 14)
            pe.wait_ge(x_copied, KT)
            for c in range(KT):
                tr(ps[0][:, c * V_N:(c + 1) * V_N], nat_v[:, c * P:(c + 1) * P], ident[0:V_N, 0:V_N])
            tr(ps[0][:, KT * V_N:KT * V_N + 2 * NG], nat_g[:, :], ident[0:2 * NG, 0:2 * NG]).then_inc(vt_ps, 1)
            for h in range(2):
                for c in range(FT):
                    last = tr(ps[3][:, 512 * h + c * F_N:512 * h + (c + 1) * F_N],
                              nat_f[:, (h * FT + c) * P:(h * FT + c + 1) * P], ident[0:F_N, 0:F_N])
            last.then_inc(vt_ps, 1)
            pe.wait_ge(x_copied, KT)

            def qk_norm_sum(hp, j):
                n = hp * 6 + j
                pe.wait_ge(qk_sqd, n + 1)
                if n:
                    pe.wait_ge(qk_root, n)
                if hp and j == 0:
                    pe.wait_ge(sc_read, 5 * hp)
                feature_sum(qk_sq, 0, 1).then_inc(qk_sum, 1)

            def to_rows(hp, g, kv):
                n = hp * 6 + NG * kv + g
                if kv:
                    taken(pe, hp * 9 + 6 + g)
                else:
                    pe.wait_ge(qk_ready, hp * 6 + 2 * g + 1)
                if n:
                    pe.wait_ge(tok_ready, n)
                if hp and g == 0 and not kv:
                    pe.wait_ge(at_ready, 5 * hp)
                elif n == 0:
                    pe.wait_ge(vt_ready, 2)
                src = vT if kv else kT[:, g, :]
                for r in range(4):
                    tr(ps[TRN][:, r * P:(r + 1) * P], src[:, r * P:(r + 1) * P], ident)
                tr(ps[TRN][0:NS, SEQ:SEQ + P], src[:, SEQ:TOK], ident).then_inc(tok_ps, 1)

            def scores(hp, i):
                e, r = hp * 5 + i, i - 1
                if i == 1:
                    for p in range(2):
                        pe.wait_ge(kcT_rdy[p], 4 * (hp + 1))
                else:
                    pe.wait_ge(sc_read, e - 1)
                rows, s = slice(r * P, (r + 1) * P), ps[2 - i % 2]
                mm(s[:, 0:SEQ], qT[:, 0, rows], kT[:, 0, 0:SEQ], start=True, stop=True)
                mm(s[:, SEQ:SEQ + P], qT[:, 1, rows], kT[:, 1, rows], start=True, stop=True)
                mm(s[:, SEQ + P:SEQ + 2 * P], qT[:, 2, rows], kT[:, 2, rows], start=True, stop=True).then_inc(sc_ps, 1)

            def cached_keys_T(hp, b):
                n = hp * NB + b
                pe.wait_ge(kc_in[n % NKC], 48 * (n // NKC + 1))
                if n >= 2:
                    pe.wait_ge(kcT_rdy[n % 2], n // 2)
                bank = ps[1][:, 512 * (b % 2):512 * (b % 2) + 512]
                for i in range(4):
                    last = tr(bank[:, i * P:(i + 1) * P], kc[:, n % NKC, i, :], ident)
                last.then_inc(kcT_ps, 1)

            def sample_scores(hp):
                pe.wait_ge(tok_ready, 6 * hp + 6)
                for p in range(2):
                    pe.wait_ge(acc_free[p], (9 * hp + 9 + 1 - p) // 2)
                for b in range(NB + 1):
                    if b < NB:
                        cached_keys_T(hp, b)
                    if b == 0:
                        pe.wait_ge(q_dia_rdy, hp + 1)
                        continue
                    n = hp * NB + b - 1
                    pe.wait_ge(kcT_rdy[n % 2], n // 2 + 1)
                    for g, c0, cn in ((0, 0, P), (1, P, 2 * P), (2, 3 * P, P)):
                        last = mm(ps[2][0:NS, c0:c0 + cn], q_dia[:, g, (b - 1) * NS:b * NS], kcT[:, n % 2, c0:c0 + cn],
                                  start=(b == 1 and g == 0), stop=(b == NB), skip_group_check=True)
                    last.then_inc(kcT_used, 1)
                for g in range(NG):
                    last = mm(ps[2][0:NS, 512 + g * NS:512 + (g + 1) * NS], qT[:, g, SEQ:TOK], kT[:, g, SEQ:TOK],
                              start=True, stop=True)
                last.then_inc(sc_ps, 1)

            def probs_T(hp, i):
                e = hp * 5 + i
                pe.wait_ge(p_ready, e + 1)
                if e:
                    pe.wait_ge(pT_ready, e)
                pr = prob[:, e % 2, :]
                if i:
                    for n in range(6):
                        last = tr(ps[TRN][:, n * P:(n + 1) * P], pr[:, n * P:(n + 1) * P], ident)
                else:
                    for n in range(4):
                        tr(ps[TRN][:, n * NS:(n + 1) * NS], pr[0:NS, n * P:(n + 1) * P], ident[0:NS, 0:NS])
                    for g in range(NG):
                        last = tr(ps[TRN][0:NS, 512 + g * NS:512 + (g + 1) * NS],
                                  pr[0:NS, 512 + g * NS:512 + (g + 1) * NS], ident[0:NS, 0:NS])
                last.then_inc(pT_ps, 1)

            def values(hp, i):
                e, r = hp * 5 + i, i - 1
                pe.wait_ge(pT_ready, e + 1)
                if e:
                    pe.wait_ge(o_ready, e)
                if i:
                    srcs = [(probT[:, c * P:(c + 1) * P], v_tok[:, c, 0, :]) for c in range(4)]
                    srcs += [(probT[:, (3 + g) * P:(4 + g) * P], v_tok[:, r, g, :]) for g in (1, 2)]
                else:
                    pe.wait_ge(vc_in, 48 * NB * (hp + 1))
                    srcs = [(p_dia[:, n, b * NS:(b + 1) * NS], vc[:, b, n, :]) for b in range(NB) for n in range(4)]
                    srcs += [(p_new[:, g * NS:(g + 1) * NS], v_tok[0:NS, 4, g, :]) for g in range(NG)]
                for n, (p_, v_) in enumerate(srcs):
                    last = mm(o_bank(i), p_, v_, start=(n == 0), stop=(n == len(srcs) - 1))
                last.then_inc(o_ps, 1)

            def out_T(hp, i):
                e = hp * 5 + i
                pe.wait_ge(o_ready, e + 1)
                if e:
                    pe.wait_ge(at_ready, e)
                n = P if i else NS
                tr(oT_bank(i), o_sb[0:n, e % 2, :], ident[0:n, 0:n]).then_inc(at_ps, 1)

            def last_item(hp, step):
                (probs_T, values, out_T)[step](hp, 4)

            for hp in range(NH):
                for j in range(9):
                    def middle():
                        if hp and j < 3:
                            last_item(hp - 1, j)
                        if 1 <= j <= 6:
                            qk_norm_sum(hp, j - 1)
                        if j in (3, 5, 7):
                            to_rows(hp, (j - 3) // 2, 0)
                        if j >= 7:
                            to_rows(hp, j - 7, 1)

                    if hp and j == 0:
                        pe.wait_ge(at_ready, 5 * hp - 1)
                    if hp and j == 1:
                        pe.wait_ge(sc_read, 5 * hp - 1)
                    first = (lambda k: (pe.wait_ge(hn_hi, k + 1), pe.wait_ge(hn_lo[k % 2], k // 2 + 1))) if hp + j == 0 else None
                    if hp + j == 0:
                        pe.wait_ge(vt_ready, 1)
                    unit(hp * 9 + j, h_hi, h_lo, first, middle)
                to_rows(hp, 2, 1)
                sample_scores(hp)
                for step in ATT_PE:
                    {"S": scores, "P": probs_T, "V": values, "O": out_T}[step[0]](hp, int(step[1]))
            for step in range(3):
                last_item(NH - 1, step)

            pe.wait_ge(at_ready, 5 * NH)
            for c in range(KT):
                unit(U_LRU + 2 * c, h_hi, h_lo)
                unit(U_LRU + 2 * c + 1, h_hi, h_lo)
                if c == 0:
                    pe.wait_ge(gw_in, 64)
                pe.wait_ge(xc_rdy, c + 1)
                if c:
                    pe.wait_ge(gate_read, c)
                for i, w in enumerate((wa, wx)):
                    for h in range(2):
                        last = mm(ps[2 + i][:, 512 * h:512 * h + LW // 2], w[:, c, :],
                                  xc[:, c % 2, h * LW // 2:(h + 1) * LW // 2], start=True, stop=True)
                last.then_inc(gate_ps, 1)

            for m in range(KT):
                unit(U_MRG + 4 * m, h_hi, h_lo)
                unit(U_MRG + 4 * m + 1, h_hi, h_lo)
                unit(U_MRG + 4 * m + 2, att_hi, att_lo)
                if m == 0:
                    pe.wait_ge(y_hi_rdy, KT)
                    pe.wait_ge(y_lo_rdy, KT)
                unit(U_MRG + 4 * m + 3, y_hi, y_lo)
                if m == 0:
                    pe.wait_ge(gate_read, KT)
                    pe.wait_ge(lst_rdy, KT)
                    for c in range(KT):
                        last = tr(ps[2][0:36, c * P:(c + 1) * P], l_st[:, c, :], ident)
                    last.then_inc(lst_ps, 1)

            pe.wait_ge(lrow_rdy, 1)
            for c in range(KT + 1):
                if c < KT:
                    unit(U_OUT + c, mg_hi, mg_lo,
                         (lambda k: (pe.wait_ge(mg_hi_rdy, k + 1), pe.wait_ge(mg_lo_rdy, k + 1))) if c == 0 else None)
                    if c == 0:
                        pe.wait_ge(x2_in, 32)
                    else:
                        pe.wait_ge(x2_cp, c)
                    for n in range(4):
                        tr(ps[3][:, n * P:(n + 1) * P], x_tok2[:, n, c * P:(c + 1) * P], ident)
                    tr(ps[3][:, SEQ:TOK], x_tok2[0:NS, 4, c * P:(c + 1) * P], ident[0:NS, 0:NS]).then_inc(x2_ps, 1)
                if c:
                    pe.wait_ge(sq2_rdy, c)
                    feature_sum(sq2[:, (c - 1) % 2, :], c - 1, KT).then_inc(sq2_used, 1)
            def state_rows(r):
                pe.wait_ge(fst_rdy, (r + 1) * PPR)
                for q in range(4):
                    if r and q == 0:
                        pe.wait_ge(frow_rdy, 4 * r)
                    for i in range(4):
                        last = tr(ps[2 + q // 2][0:18, 512 * (q % 2) + i * P:512 * (q % 2) + (i + 1) * P],
                                  f_st[:, 4 * q + i, :], ident)
                last.then_inc(fst_ps, 1)

            def y_rows(m):
                taken(pe, down_unit(NRND - 1, m))
                if m == 0:
                    pe.wait_ge(frow_rdy, 4 * NRND)
                if m >= 1:
                    pe.wait_ge(yt_rdy, m)
                for n in range(4):
                    tr(ps[3][:, n * P:(n + 1) * P], x2[:, m, n * P:(n + 1) * P], ident)
                tr(ps[3][0:NS, SEQ:SEQ + P], x2[:, m, SEQ:TOK], ident).then_inc(yt_ps, 1)

            for kind, i, m in ffn_steps():
                if kind == "up":
                    unit(up_unit(i), h_hi, h_lo,
                         (lambda k: (pe.wait_ge(hn2_hi, k + 1), pe.wait_ge(hn2_lo[k % 2], k // 2 + 1))) if i == 0 else None)
                    unit(up_unit(i) + 1, h_hi, h_lo)
                else:
                    unit(down_unit(i, m), g_hi[i % 2], g_lo[i % 2],
                         (lambda k: (pe.wait_ge(g_hi_rdy, i * PPR + k + 1), pe.wait_ge(g_lo_rdy, i * PPR + k + 1))) if m == 0 else None)
                    if m == 0:
                        state_rows(i)
                    if i == NRND - 1 and m:
                        y_rows(m - 1)
            y_rows(KT - 1)

        @block.scalar
        def _(act):
            A = act.activation

            def hi_split(u):
                if u >= U_ALL:
                    return
                act.wait_ge(raw_in[u % NRAW], 16 * (u // NRAW + 1))
                if u >= NSPL:
                    act.wait_ge(unit_done, u - NSPL + 1)
                A(w_hi[:, u % NSPL, 0:nkt[u], :], w_raw[:, u % NRAW, 0:nkt[u], :], ACT.Copy).then_inc(hi_ready, 1)

            for rows, name in ((slice(V_CW, V_CB), "conv_a_w"), (slice(V_CB, V_BA), "conv_a_b"),
                               (slice(V_BA, V_BX), "lru_ba"), (slice(V_BX, V_LAM), "lru_bx"),
                               (slice(V_LAM, V_N1), "lru_lambda"), (slice(V_N1, V_N2), "norm1_g"),
                               (slice(V_N2, V_SC), "norm2_g")):
                src = t[name]
                act.dma_start(nat_v[rows, :], src[0] if len(src.shape) == 3 else src).then_inc(s_nat, 16)
            act.dma_start(nat_v[V_SC:V_H0, :], t["state_lru_conv"][0].rearrange("b s d -> (b s) d")).then_inc(s_nat, 16)
            act.dma_start(nat_v[V_H0:V_N, :], t["state_lru_h"][0]).then_inc(s_nat, 16)
            act.dma_start(nat_g[0:NG, :], t["k_norm_g"][0]).then_inc(s_nat, 16)
            act.dma_start(nat_g[NG:2 * NG, :], t["q_norm_g"][0]).then_inc(s_nat, 16)
            act.dma_start(nat_f[F_W:F_B, :], t["conv_f_w"][0]).then_inc(s_nat, 16)
            act.dma_start(nat_f[F_B:F_S, :], t["conv_f_b"]).then_inc(s_nat, 16)
            act.dma_start(nat_f[F_S:F_N, :], t["state_ffn_conv"][0].rearrange("b s d -> (b s) d")).then_inc(s_nat, 16)
            for c in range(KT):
                act.wait_ge(x_copied, c + 1)
                if c >= 2:
                    act.wait_ge(sq_used, c - 1)
                A(sq[:, c % 2, :], x_t[:, c, :], ACT.Square).then_inc(sq_ready, 1)
            act.wait_ge(sq_used, KT)
            act.wait_ge(s_const, 16)
            A(root[:, :].rearrange("p (h n) -> p h n", h=2), acc[NORM], ACT.Sqrt, scale=1.0 / D, bias=eps).then_inc(root_ready, 1)
            for c in range(KT):
                act.wait_ge(hn_ready, c + 1)
                A(h_hi[:, c, :], hn[:, c % NHN, :], ACT.Copy).then_inc(hn_hi, 1)
                if c < NSPL:
                    hi_split(c)
            act.wait_ge(ln_fix, 2)
            A(sp4[:, 1, :], sp4[:, 0, :], ACT.Exp, scale=-1.0).then_inc(tab_link, 1)
            act.wait_ge(ln_fix, 3)
            A(sp4[:, 3, :], sp4[:, 2, :], ACT.Ln).then_inc(tab_link, 1)
            for lo in hn_lo:
                act.wait_ge(lo, KT // 2)
            act.wait_ge(vt_ready, 3)

            def head_unit(hp, j):
                u = hp * 9 + j
                hi_split(u + NSPL)
                act.wait_ge(unit_done, u + 1)
                a = acc[u % 2]
                if j < 6:
                    n = hp * 6 + j
                    if n:
                        act.wait_ge(qk_sum, n)
                    A(qk_sq[:, :].rearrange("p (h n) -> p h n", h=2), a, ACT.Square).then_inc(qk_sqd, 1)
                    if n >= 2:
                        act.wait_ge(qk_ready, n - 1)
                    g = (j % 2) * NG + j // 2
                    gain = qkg[:, g:g + 1]
                    A(qk_gn[:, n % 2, :].rearrange("p (h n) -> p h n", h=2), a, ACT.Identity, scale=gain).then_inc(acc_free[u % 2], 1)
                else:
                    n = hp * 6 + j - NG
                    if j > 6:
                        act.wait_ge(tok_ps, n)
                    i0 = HALF // NCLS
                    vi = by_class(vT[:, 0:SEQ])
                    A(vi[:, 0:i0, :], in_time(ps[u % 2][:, 0:HALF]), ACT.Copy)
                    A(vi[:, i0:P, :], in_time(ps[u % 2][:, 512:512 + SEQ - HALF]), ACT.Copy)
                    A(vT[:, SEQ:TOK], ps[u % 2][:, 512 + SEQ - HALF:512 + HALF], ACT.Copy).then_inc(acc_free[u % 2], 1)

            def qk_root_of(hp, j):
                n = hp * 6 + j
                act.wait_ge(qk_sum, n + 1)
                if n:
                    act.wait_ge(qk_rinv, n)
                A(qk_rt[:, :].rearrange("p (h n) -> p h n", h=2), acc[NORM], ACT.Sqrt, scale=1.0 / HD, bias=eps).then_inc(qk_root, 1)

            def rows_of(hp, g, kv):
                n = hp * 6 + NG * kv + g
                act.wait_ge(tok_ps, n + 1)
                if hp:
                    act.wait_ge(kv_out[2 * g + kv], 32 * hp)
                buf = v_tok if kv else k_tok
                A(buf[:, 0:4, g, :], ps[TRN][:, 0:SEQ].rearrange("p (r d) -> p r d", r=4), ACT.Copy)
                A(buf[0:NS, 4, g, :], ps[TRN][0:NS, SEQ:SEQ + HD], ACT.Copy).then_inc(tok_ready, 1)

            def exps(hp, i):
                e = hp * 5 + i
                act.wait_ge(mx_ready, e + 1)
                rows, n = (P, 6 * P) if i else (NS, 4 * P + NG * NS)
                pr = prob[0:rows, e % 2, 0:n]
                A(pr, pr, ACT.Exp, bias=stat[0:rows, e % 4, 2:3], accum_out=stat[0:rows, e % 4, 3:4]).then_inc(p_ready, 1)

            def take_probs_T(hp, i):
                e = hp * 5 + i
                act.wait_ge(pT_ps, e + 1)
                if e:
                    act.wait_ge(o_ps, e)
                if i:
                    A(probT[:, :], ps[TRN][:, 0:6 * P], ACT.Copy).then_inc(pT_ready, 1)
                else:
                    act.wait_ge(s_zero, 2)
                    for n in range(4):
                        src = ps[TRN][:, n * NS:(n + 1) * NS]
                        A(diag(p_dia[:, n, :]), src.rearrange("p (b t) -> p b t", b=NB), ACT.Copy)
                    A(p_new[:, :], ps[TRN][0:NS, 512:512 + NG * NS], ACT.Copy).then_inc(pT_ready, 1)

            def out_hi(hp, i):
                e = hp * 5 + i
                act.wait_ge(at_ps, e + 1)
                A(out_cols(att_hi, hp, i), oT_bank(i), ACT.Copy).then_inc(at_hi_rdy, 1)

            def take_cached_T(hp, b):
                n = hp * NB + b
                act.wait_ge(kcT_ps, n + 1)
                if n >= 2:
                    act.wait_ge(kcT_used, n - 1)
                A(kcT[:, n % 2, :], ps[1][:, 512 * (b % 2):512 * (b % 2) + 512], ACT.Copy).then_inc(kcT_rdy[n % 2], 1)

            for hp in range(NH):
                for j in range(9):
                    if hp and j == 0:
                        take_probs_T(hp - 1, 4)
                    if hp and j == 2:
                        out_hi(hp - 1, 4)
                    if 1 <= j <= 6:
                        qk_root_of(hp, j - 1)
                    if j in (3, 5, 7):
                        rows_of(hp, (j - 3) // 2, 0)
                    if j >= 7:
                        rows_of(hp, j - 7, 1)
                    head_unit(hp, j)
                rows_of(hp, 2, 1)
                for b in range(1, NB, 2):
                    take_cached_T(hp, b)
                for step in ATT_ACT:
                    {"E": exps, "P": take_probs_T, "H": out_hi}[step[0]](hp, int(step[1]))
            take_probs_T(NH - 1, 4)
            out_hi(NH - 1, 4)

            for s in kv_out:
                act.wait_ge(s, 32 * NH)
            act.wait_ge(at_ready, 5 * NH)
            act.wait_ge(kcT_used, NH * NB)

            def gates(c):
                act.wait_ge(gate_ps, c + 1)
                if c:
                    act.wait_ge(y_lo_rdy, c)
                for i, dst in enumerate((g_r, g_i)):
                    last = A(dst[:, :].rearrange("p (h n) -> p h n", h=2),
                             ps[2 + i][:, :].rearrange("p (h n) -> p h n", h=2)[:, :, 0:LW // 2], ACT.Tanh,
                             scale=0.5, bias=sp4[:, 2 + i, c:c + 1])
                    last.then_inc(gate_read if i else l_gr, 1)
                act.wait_ge(l_gr, c + 1)
                A(a_s[:, :], g_r[:, :], ACT.Tanh, scale=sp4[:, 0, c:c + 1], bias=sp4[:, 0, c:c + 1]).then_inc(as_rdy, 1)
                A(a_a[:, :], g_r[:, :], ACT.Exp, scale=sp4[:, 1, c:c + 1], bias=sp4[:, 1, c:c + 1]).then_inc(aa_rdy, 1)

            def y_part(c):
                act.wait_ge(y_rdy, c + 1)
                A(y_hi[:, c, :], l_y[:, :], ACT.Copy).then_inc(y_hi_rdy, 1)

            for c in range(KT + 1):
                if c < KT:
                    u = U_LRU + 2 * c
                    hi_split(u + NSPL)
                    act.wait_ge(unit_done, u + 1)
                    if c >= 2:
                        act.wait_ge(lst_rdy, c - 1)
                    p_ = ps[u % 2]
                    A(xa[:, c % 2, XPAD:XPAD + HALF], p_[:, 0:HALF], ACT.Copy)
                    A(xa[:, c % 2, XPAD + HALF:XS0], p_[:, 512:512 + SEQ - HALF], ACT.Copy)
                    A(seqs(xa[:, c % 2, XS0:XW], XSEQ)[:, :, XPAD:XSEQ],
                      seqs(p_[:, 512 + SEQ - HALF:512 + HALF], NT), ACT.Copy).then_inc(acc_free[u % 2], 1)
                if c:
                    gates(c - 1)
                if c < KT:
                    u += 1
                    hi_split(u + NSPL)
                    act.wait_ge(unit_done, u + 1)
                    if c >= 2:
                        act.wait_ge(y_rdy, c - 1)
                    A(ga[:, c % 2, :].rearrange("p (h n) -> p h n", h=2), acc[u % 2], ACT.Gelu_apprx_tanh).then_inc(acc_free[u % 2], 1)
                if c:
                    act.wait_ge(m2_rdy, c)
                    A(a_s[:, :], a_s[:, :], ACT.Sqrt).then_inc(mul_rdy, 1)
                    y_part(c - 1)

            for m in range(KT):
                for j in range(4):
                    u = U_MRG + 4 * m + j
                    hi_split(u + NSPL)
                    if j < 2:
                        act.wait_ge(unit_done, u + 1)
                        if m == 0 and j == 0:
                            act.wait_ge(y_lo_rdy, KT)
                            act.wait_ge(lst_rdy, KT)
                        if m:
                            act.wait_ge(mg_rdy, m)
                        A((sg_b if j else sg_a)[:, :].rearrange("p (h n) -> p h n", h=2), acc[u % 2], ACT.Sigmoid).then_inc(acc_free[u % 2], 1)
                    if m and j == 0:
                        A(mg_hi[:, m - 1, :], mg_s[:, 0, :], ACT.Copy).then_inc(mg_hi_rdy, 1)
                if m == 0:
                    act.wait_ge(lst_ps, 1)
                    A(l_row[:, :], ps[2][0:36, :], ACT.Copy).then_inc(lrow_rdy, 1)
            act.wait_ge(mg_rdy, KT)
            A(mg_hi[:, KT - 1, :], mg_s[:, 0, :], ACT.Copy).then_inc(mg_hi_rdy, 1)

            for c in range(KT):
                hi_split(U_OUT + c + NSPL)
                act.wait_ge(x2_ps, c + 1)
                if c:
                    taken(act, U_OUT + c - 1)
                A(xs[:, :], ps[3][:, 0:TOK], ACT.Copy).then_inc(x2_cp, 1)
                taken(act, U_OUT + c)
                if c >= 2:
                    act.wait_ge(sq2_used, c - 1)
                A(sq2[:, c % 2, :], x2[:, c, :], ACT.Square).then_inc(sq2_rdy, 1)
            act.wait_ge(sq2_used, KT)
            A(root2[:, :].rearrange("p (h n) -> p h n", h=2), acc[NORM], ACT.Sqrt, scale=1.0 / D, bias=eps).then_inc(root2_rdy, 1)
            for c in range(KT):
                act.wait_ge(hn2_rdy, c + 1)
                A(h_hi[:, c, :], hn2[:, c % NHN, :], ACT.Copy).then_inc(hn2_hi, 1)

            def gelu(i):
                act.wait_ge(cg_rdy, i + 1)
                A(cg[:, :], cg[:, :], ACT.Gelu_apprx_tanh).then_inc(gl_rdy, 1)

            def g_part(i):
                act.wait_ge(gm_rdy, i + 1)
                r = i // PPR
                if r >= 2:
                    act.wait_ge(unit_done, down_unit(r - 2, KT - 1) + 1)
                A(g_hi[r % 2][:, i % PPR, :], gm[:, :], ACT.Copy).then_inc(g_hi_rdy, 1)

            def frows(r):
                act.wait_ge(fst_ps, r + 1)
                if r:
                    act.wait_ge(f_out, 16 * 8 * r)
                for q in range(4):
                    A(f_row[:, q, :], ps[2 + q // 2][0:18, 512 * (q % 2):512 * (q % 2) + 512], ACT.Copy).then_inc(frow_rdy, 1)

            def y_take(m):
                act.wait_ge(yt_ps, m + 1)
                A(y_tok[:, 0:4, m * P:(m + 1) * P], ps[3][:, 0:SEQ].rearrange("p (n d) -> p n d", n=4), ACT.Copy)
                A(y_tok[0:NS, 4, m * P:(m + 1) * P], ps[3][0:NS, SEQ:SEQ + P], ACT.Copy).then_inc(yt_rdy, 1)

            for lo in hn2_lo:
                act.wait_ge(lo, KT // 2)
            act.wait_ge(u_pad, 2)
            for kind, i, m in ffn_steps():
                if kind == "up":
                    for j, buf in enumerate((ug, uv)):
                        u = up_unit(i) + j
                        hi_split(u + NSPL)
                        act.wait_ge(unit_done, u + 1)
                        if i >= 2:
                            act.wait_ge(fst_rdy, i - 1)
                        p_ = ps[u % 2]
                        A(buf[:, i % 2, UPAD:UPAD + HALF], p_[:, 0:HALF], ACT.Copy)
                        A(buf[:, i % 2, UPAD + HALF:US0], p_[:, 512:512 + SEQ - HALF], ACT.Copy)
                        A(seqs(buf[:, i % 2, US0:UW], USEQ)[:, :, UPAD:USEQ],
                          seqs(p_[:, 512 + SEQ - HALF:512 + HALF], NT), ACT.Copy).then_inc(acc_free[u % 2], 1)
                    gelu(i)
                    g_part(i)
                else:
                    hi_split(down_unit(i, m) + NSPL)
                    if m == 0:
                        frows(i)
                    if i == NRND - 1 and m:
                        y_take(m - 1)
            y_take(KT - 1)

        @block.vector
        def _(dve):
            STT, TT, TS = dve.scalar_tensor_tensor, dve.tensor_tensor, dve.tensor_scalar

            def lo_split(u):
                if u >= U_ALL:
                    return
                dve.wait_ge(hi_ready, u + 1)
                TT(w_lo[:, u % NSPL, 0:nkt[u], :], w_raw[:, u % NRAW, 0:nkt[u], :],
                   w_hi[:, u % NSPL, 0:nkt[u], :], ALU.subtract).then_inc(lo_ready, 1)

            for c in range(KT):
                dve.wait_ge(x_ps, c + 1)
                dve.tensor_copy(x_t[:, c, :], ps[c % 2][:, 0:TOK]).then_inc(x_copied, 1)
            dve.wait_ge(vt_ps, 1)
            dve.tensor_copy(qkg[:, :], ps[0][:, KT * V_N:KT * V_N + 2 * NG])
            dve.tensor_copy(vt[:, :, :], ps[0][:, 0:KT * V_N].rearrange("p (c n) -> p c n", c=KT)).then_inc(vt_ready, 1)
            dve.wait_ge(root_ready, 1)
            dve.reciprocal(rinv[:, :], root[:, :]).then_inc(rinv_ready, 1)
            dve.wait_ge(rinv_ready, 1)
            dve.wait_ge(x_copied, KT)
            dve.wait_ge(vt_ready, 1)

            def normed_tiles(src, gain, rinv_, buf, ready, his, los):
                for c in range(KT):
                    if c >= NHN:
                        dve.wait_ge(his, c - NHN + 1)
                        dve.wait_ge(los[c % 2], (c - NHN) // 2 + 1)
                    STT(buf[:, c % NHN, :], src[:, c, :], vt[:, c, gain:gain + 1], rinv_[:, :], ALU.mult, ALU.mult).then_inc(ready, 1)
                    if c % 2 and c:
                        dve.wait_ge(his, c)
                        TT(h_lo[:, c - 1, :], buf[:, (c - 1) % NHN, :], h_hi[:, c - 1, :], ALU.subtract).then_inc(los[0], 1)

            normed_tiles(x_t, V_N1, rinv, hn, hn_ready, hn_hi, hn_lo)
            for u in range(NSPL):
                lo_split(u)
            dve.wait_ge(vt_ps, 2)
            dve.tensor_copy(ft[:, :, :].rearrange("p (h c) n -> p h (c n)", h=2),
                            ps[3][:, :].rearrange("p (h n) -> p h n", h=2)[:, :, 0:FT * F_N]).then_inc(vt_ready, 1)
            lam = vt[:, :, V_LAM]

            def fixed(ins, n):
                ins.then_inc(ln_fix, 1)
                dve.wait_ge(ln_fix, n)

            dve.wait_ge(vt_ready, 1)
            fixed(TS(sp4[:, 2, :], lam, -1.0, None, ALU.mult), 1)
            fixed(TT(sp4[:, 0, :], lam, sp4[:, 2, :], ALU.max), 2)
            dve.wait_ge(tab_link, 1)
            fixed(TS(sp4[:, 2, :], sp4[:, 1, :], 1.0, None, ALU.add), 3)
            fixed(dve.reciprocal(sp_t[:, 0, :], sp4[:, 2, :]), 4)
            fixed(TS(sp_t[:, 1, :], sp4[:, 2, :], -1.0, None, ALU.add), 5)
            fixed(TT(sp_t[:, 1, :], sp4[:, 1, :], sp_t[:, 1, :], ALU.subtract), 6)
            fixed(TT(sp_t[:, 1, :], sp_t[:, 1, :], sp_t[:, 0, :], ALU.mult), 7)
            dve.wait_ge(tab_link, 2)
            fixed(TT(sp_t[:, 1, :], sp_t[:, 1, :], sp4[:, 3, :], ALU.add), 8)
            fixed(TS(sp_t[:, 0, :], lam, -1.0, 0.0, ALU.mult, ALU.max), 9)
            fixed(TT(sp_t[:, 0, :], sp_t[:, 0, :], sp_t[:, 1, :], ALU.add), 10)
            TS(sp4[:, 0, :], sp_t[:, 0, :], 4.0, None, ALU.mult)
            TS(sp4[:, 1, :], sp_t[:, 0, :], -4.0, None, ALU.mult)
            TS(sp4[:, 2, :], vt[:, :, V_BA], 0.5, None, ALU.mult)
            TS(sp4[:, 3, :], vt[:, :, V_BX], 0.5, None, ALU.mult).then_inc(vt_ready, 1)

            def qk_scale(hp, j):
                n, u, g = hp * 6 + j, hp * 9 + j, j // 2
                dve.wait_ge(qk_root, n + 1)
                if n:
                    dve.wait_ge(qk_ready, n)
                dve.reciprocal(qk_ri[:, :], qk_rt[:, :]).then_inc(qk_rinv, 1)
                dve.wait_ge(qk_rinv, n + 1)
                dve.wait_ge(acc_free[u % 2], u // 2 + 1)
                dst = (qT if j % 2 else kT)[:, g, :]
                TT(by_class(dst[:, 0:SEQ]), in_time(qk_gn[:, n % 2, 0:SEQ]), in_time(qk_ri[:, 0:SEQ]), ALU.mult)
                TT(dst[:, SEQ:TOK], qk_gn[:, n % 2, SEQ:TOK], qk_ri[:, SEQ:TOK], ALU.mult).then_inc(qk_ready, 1)

            def mask_max(hp, i):
                e, r, sc = hp * 5 + i, i - 1, ps[2 - i % 2]
                dve.wait_ge(sc_ps, e + 1)
                if e >= 2:
                    dve.wait_ge(pT_ps, e - 1)
                if e >= 4:
                    dve.wait_ge(o_ready, e - 3)
                st = stat[:, e % 4, :]
                if i:
                    rows, n0, n1, m0, m1 = P, 4 * P, 2 * P, C_PM + (3 - r) * P, C_PM + 7 * P
                else:
                    rows, n0, n1, m0, m1 = NS, 4 * P, NG * NS, C_SM, C_SM + 4 * P
                for w, (s0, n, m) in enumerate(((0, n0, m0), (512, n1, m1))):
                    last = dve.tensor_tensor_reduce(prob[0:rows, e % 2, s0:s0 + n], sc[0:rows, s0:s0 + n],
                                                    const[0:rows, m:m + n], SCALE, -3e38, ALU.add, ALU.max,
                                                    st[0:rows, w:w + 1])
                last.then_inc(sc_read, 1)
                dve.wait_ge(sc_read, e + 1)
                dve.tensor_reduce(st[0:rows, 2:3], st[0:rows, 0:2], AX_X, ALU.max, negate=True).then_inc(mx_ready, 1)

            def normed(hp, i):
                e = hp * 5 + i
                rows = P if i else NS
                st = stat[0:rows, e % 4, :]
                dve.wait_ge(p_ready, e + 1)
                dve.reciprocal(st[:, 4:5], st[:, 3:4]).then_inc(r_ready, 1)
                dve.wait_ge(r_ready, e + 1)
                dve.wait_ge(o_ps, e + 1)
                if e >= 2:
                    dve.wait_ge(at_ps, e - 1)
                TS(o_sb[0:rows, e % 2, :], o_bank(i), st[:, 4:5], None, ALU.mult).then_inc(o_ready, 1)

            def out_lo(hp, i):
                dve.wait_ge(at_hi_rdy, hp * 5 + i + 1)
                TT(out_cols(att_lo, hp, i), oT_bank(i), out_cols(att_hi, hp, i), ALU.subtract).then_inc(at_ready, 1)

            for hp in range(NH):
                for j in range(9):
                    if hp and j == 1:
                        normed(hp - 1, 4)
                    if hp and j == 2:
                        out_lo(hp - 1, 4)
                    if 1 <= j <= 6:
                        qk_scale(hp, j - 1)
                    lo_split(hp * 9 + j + NSPL)
                dve.wait_ge(qk_ready, 6 * hp + 6)
                dve.wait_ge(s_zero, 2)
                if hp:
                    dve.wait_ge(q_dia_rdy, hp)
                for g in range(NG):
                    last = dve.tensor_copy(diag(q_dia[:, g, :]), qT[:, g, SEQ:TOK].rearrange("p (b t) -> p b t", b=NB))
                last.then_inc(q_dia_rdy, 1)
                for b in range(0, NB, 2):
                    n = hp * NB + b
                    dve.wait_ge(kcT_ps, n + 1)
                    if n >= 2:
                        dve.wait_ge(kcT_used, n - 1)
                    dve.tensor_copy(kcT[:, n % 2, :], ps[1][:, 512 * (b % 2):512 * (b % 2) + 512]).then_inc(kcT_rdy[n % 2], 1)
                for step in ATT_DVE:
                    {"M": mask_max, "N": normed, "L": out_lo}[step[0]](hp, int(step[1]))
            normed(NH - 1, 4)
            out_lo(NH - 1, 4)

            link = [0]

            def linked(ins):
                ins.then_inc(l_link, 1)
                link[0] += 1
                dve.wait_ge(l_link, link[0])

            for s in kv_out:
                dve.wait_ge(s, 32 * NH)
            dve.wait_ge(gw_zero, 3)

            def conv(c):
                u = U_LRU + 2 * c
                x, y, v = xa[:, c % 2, :], xc[:, c % 2, :], vt[:, c, :]
                if c >= 2:
                    dve.wait_ge(lst_rdy, c - 1)
                dve.tensor_copy(seqs(x[:, XS0:XW], XSEQ)[:, :, 0:XPAD], seqs(v[:, V_SC:V_H0], 3)).then_inc(xa_pad, 1)
                dve.wait_ge(xa_pad, c + 1)
                dve.wait_ge(acc_free[u % 2], u // 2 + 1)
                linked(TS(y[:, :], x[:, 0:LW], v[:, V_CW:V_CW + 1], v[:, V_CB:V_CB + 1], ALU.mult, ALU.add))
                for i in (1, 2, 3):
                    ins = STT(y[:, :], x[:, i:i + LW], v[:, V_CW + i:V_CW + i + 1], y[:, :], ALU.mult, ALU.add)
                    if i < 3:
                        linked(ins)
                    else:
                        ins.then_inc(xc_rdy, 1)

            def recur(c):
                pads = lambda b: seqs(b[:, SEQ:LW], XSEQ)[:, :, XPAD - 1]
                dve.wait_ge(gate_read, c + 1)
                linked(STT(g_i[:, :], g_i[:, :], 1.0, xc[:, c % 2, :], ALU.add, ALU.mult))
                dve.wait_ge(as_rdy, c + 1)
                dve.wait_ge(a2_rdy, c + 1)
                STT(a_s[:, :], a_2[:, :], 1.0, a_s[:, :], ALU.add, ALU.mult).then_inc(m2_rdy, 1)
                dve.memset(pads(a_a[:, :]), 0.0)
                dve.wait_ge(mul_rdy, c + 1)
                linked(dve.memset(a_s[:, 0:1], 1.0))
                linked(STT(l_u[:, :], g_i[:, :], 0.5, a_s[:, :], ALU.mult, ALU.mult))
                linked(dve.tensor_copy(pads(l_u[:, :]), vt[:, c, V_H0:V_N]))
                if c:
                    dve.wait_ge(lst_rdy, c)
                    dve.wait_ge(y_lo_rdy, c)
                linked(dve.tensor_tensor_scan(l_h[:, :], a_a[:, :], l_u[:, :], 0.0, ALU.mult, ALU.add))
                g_ = ga[:, c % 2, :]
                u = U_LRU + 2 * c + 1
                dve.wait_ge(acc_free[u % 2], u // 2 + 1)
                TT(l_y[:, 0:SEQ], l_h[:, 0:SEQ], g_[:, 0:SEQ], ALU.mult)
                hs = seqs(l_h[:, SEQ:LW], XSEQ)[:, :, XPAD:XSEQ]
                TT(seqs(l_y[:, SEQ:TOK], NT), hs, seqs(g_[:, SEQ:TOK], NT), ALU.mult).then_inc(y_rdy, 1)
                x = xa[:, c % 2, :]
                dve.tensor_copy(l_st[:, c, 0:3], x[:, XS0 - 3:XS0])
                dve.tensor_copy(seqs(l_st[:, c, 3:27], 3), seqs(x[:, XS0:XW], XSEQ)[:, :, XSEQ - 3:XSEQ])
                dve.tensor_copy(l_st[:, c, 27:28], l_h[:, SEQ - 1:SEQ])
                dve.tensor_copy(l_st[:, c, 28:36], hs[:, :, NT - 1]).then_inc(lst_rdy, 1)
                dve.wait_ge(y_hi_rdy, c + 1)
                TT(y_lo[:, c, :], l_y[:, :], y_hi[:, c, :], ALU.subtract).then_inc(y_lo_rdy, 1)

            for c in range(KT + 1):
                if c < KT:
                    lo_split(U_LRU + 2 * c + NSPL)
                    conv(c)
                    lo_split(U_LRU + 2 * c + 1 + NSPL)
                if c:
                    recur(c - 1)

            for m in range(KT):
                for j in range(4):
                    u = U_MRG + 4 * m + j
                    lo_split(u + NSPL)
                    if j == 0 and m:
                        dve.wait_ge(mg_hi_rdy, m)
                        TT(mg_lo[:, m - 1, :], mg_s[:, 0, :], mg_hi[:, m - 1, :], ALU.subtract).then_inc(mg_lo_rdy, 1)
                    if j >= 2:
                        dve.wait_ge(unit_done, u + 1)
                        taken(dve, U_MRG + 4 * m + 3 - j)
                        if m:
                            dve.wait_ge(mg_lo_rdy, m)
                            dve.wait_ge(mg_hi_rdy, m)
                        sg = sg_b if j == 2 else sg_a
                        TT(mg_s[:, 3 - j, :].rearrange("p (h n) -> p h n", h=2), acc[u % 2],
                           sg[:, :].rearrange("p (h n) -> p h n", h=2), ALU.mult).then_inc(acc_free[u % 2], 1)
                for j in (2, 3):
                    taken(dve, U_MRG + 4 * m + j)
                TT(mg_s[:, 0, :], mg_s[:, 0, :], mg_s[:, 1, :], ALU.add).then_inc(mg_rdy, 1)
            dve.wait_ge(mg_hi_rdy, KT)
            TT(mg_lo[:, KT - 1, :], mg_s[:, 0, :], mg_hi[:, KT - 1, :], ALU.subtract).then_inc(mg_lo_rdy, 1)

            for c in range(KT):
                u = U_OUT + c
                lo_split(u + NSPL)
                dve.wait_ge(unit_done, u + 1)
                dve.wait_ge(x2_cp, c + 1)
                TT(x2[:, c, :].rearrange("p (h n) -> p h n", h=2), acc[u % 2],
                   xs[:, :].rearrange("p (h n) -> p h n", h=2), ALU.add).then_inc(acc_free[u % 2], 1)
            dve.wait_ge(root2_rdy, 1)
            for c in (KT - 2, KT - 1):
                taken(dve, U_OUT + c)
            dve.reciprocal(rinv2[:, :], root2[:, :]).then_inc(rinv2_rdy, 1)
            dve.wait_ge(rinv2_rdy, 1)
            normed_tiles(x2, V_N2, rinv2, hn2, hn2_rdy, hn2_hi, hn2_lo)

            dve.wait_ge(hn2_hi, KT)
            for lo in hn2_lo:
                dve.wait_ge(lo, KT // 2)
            dve.memset(ug[:, :, 0:UPAD], 0.0).then_inc(u_pad, 1)
            dve.memset(uv[:, :, 0:UPAD], 0.0).then_inc(u_pad, 1)
            flink = [0]

            def flinked(ins):
                ins.then_inc(f_link, 1)
                flink[0] += 1
                dve.wait_ge(f_link, flink[0])

            def ffn_conv(i, j):
                u, ti = up_unit(i) + j, i + j * FT
                x, y, v = (uv if j else ug)[:, i % 2, :], cv if j else cg, ft[:, ti, :]
                flinked(dve.tensor_copy(seqs(x[:, US0:UW], USEQ)[:, :, 0:UPAD], seqs(v[:, F_S:F_N], 2)))
                dve.wait_ge(acc_free[u % 2], u // 2 + 1)
                if j == 0 and i:
                    dve.wait_ge(gm_rdy, i)
                flinked(TS(y[:, :], x[:, 0:CW], v[:, F_W:F_W + 1], v[:, F_B:F_B + 1], ALU.mult, ALU.add))
                flinked(STT(y[:, :], x[:, 1:1 + CW], v[:, F_W + 1:F_W + 2], y[:, :], ALU.mult, ALU.add))
                STT(y[:, :], x[:, 2:2 + CW], v[:, F_W + 2:F_W + 3], y[:, :], ALU.mult, ALU.add).then_inc(cv_rdy if j else cg_rdy, 1)

            def product(i):
                dve.wait_ge(gl_rdy, i + 1)
                dve.wait_ge(cv_rdy, i + 1)
                if i:
                    dve.wait_ge(g_hi_rdy, i)
                    dve.wait_ge(g_lo_rdy, i)
                TT(gm[:, 0:SEQ], cg[:, 0:SEQ], cv[:, 0:SEQ], ALU.mult)
                ss = lambda b: b[:, SEQ:CW].rearrange("p (b n) -> p b n", n=USEQ)[:, :, UPAD:USEQ]
                TT(seqs(gm[:, SEQ:TOK], NT), ss(cg), ss(cv), ALU.mult).then_inc(gm_rdy, 1)
                q = i % PPR
                if q == 0 and i:
                    dve.wait_ge(fst_ps, i // PPR)
                for j, b in enumerate((ug, uv)):
                    x = b[:, i % 2, :]
                    dve.tensor_copy(f_st[:, j * PPR + q, 0:2], x[:, US0 - 2:US0])
                    last = dve.tensor_copy(seqs(f_st[:, j * PPR + q, 2:18], 2), seqs(x[:, US0:UW], USEQ)[:, :, USEQ - 2:USEQ])
                last.then_inc(fst_rdy, 1)
                dve.wait_ge(g_hi_rdy, i + 1)
                TT(g_lo[(i // PPR) % 2][:, i % PPR, :], gm[:, :], g_hi[(i // PPR) % 2][:, i % PPR, :], ALU.subtract).then_inc(g_lo_rdy, 1)

            for kind, i, m in ffn_steps():
                if kind == "up":
                    for j in range(2):
                        lo_split(up_unit(i) + j + NSPL)
                        ffn_conv(i, j)
                    product(i)
                else:
                    u = down_unit(i, m)
                    lo_split(u + NSPL)
                    dve.wait_ge(unit_done, u + 1)
                    TT(x2[:, m, :].rearrange("p (h n) -> p h n", h=2), acc[u % 2],
                       x2[:, m, :].rearrange("p (h n) -> p h n", h=2), ALU.add).then_inc(acc_free[u % 2], 1)


def constants(np):
    c = np.zeros((P, C_N), np.float32)
    c[:, C_ID:C_ID + P] = np.eye(P)
    c[:, C_ONE:C_ONE + P] = 1.0
    i, j = np.arange(P)[:, None], np.arange(P)[None, :]
    d = i - j
    below, same, above = (d >= 0) & (d <= 31), (d >= 0) & (d <= 32), (d >= 1) & (d <= 32)
    strip = [below] * 3 + [same] + [above] * 3
    strip += [d >= 0, (d >= 0) & (d % 4 == 0)]
    c[:, C_PM:C_PM + 9 * P] = np.where(np.concatenate(strip, 1), 0.0, NEG)
    b, t = np.divmod(np.arange(NS), NT)
    t = t[:, None]
    k = np.arange(PAST)[None, :]
    own = [np.arange(P)[None, :] >= t,
           (k - t) % 4 == 0,
           np.arange(P)[None, :] % NT == t]
    b2, t2 = np.divmod(np.arange(NS)[None, :], NT)
    mine = (b[:, None] == b2) & (t2 <= t)
    own += [mine, mine & ((t - t2) % 4 == 0), mine & (t == t2)]
    c[0:NS, C_SM:C_SM + 4 * P + NG * NS] = np.where(np.concatenate(own, 1), 0.0, NEG)
    c[:, C_EPS] = EPS
    return c


_INS = ["x_prompt", "x_sample", "state_lru_h", "state_lru_conv", "cache_k_g0", "cache_v_g0", "cache_k_g1", "cache_v_g1",
        "cache_k_g2", "cache_v_g2", "state_ffn_conv", "norm1_g", "w_in", "conv_a_w", "conv_a_b", "lru_wa", "lru_ba",
        "lru_wx", "lru_bx", "lru_lambda", "q_norm_g", "k_norm_g", "w_br_a", "w_br_b", "w_out", "norm2_g", "w_up",
        "conv_f_w", "conv_f_b", "w_down"]
_KV = [(P, P), (SEQ, SEQ), (SEQ, SEQ)]
_OUTS = ([(1, SEQ, D), (NB, NT, D), (1, 1, D), (1, 1, 3, D)]
         + [(1, 1, n, NH, HD) for pair in _KV for n in pair] + [(1, 1, 2, 2 * DFF)]
         + [(1, NB, D), (1, NB, 3, D)] + [(1, NB, NT, NH, HD)] * 6 + [(1, NB, 2, 2 * DFF)])


def kernel(**inputs):
    import numpy as np
    import concourse.bacc as bacc
    from concourse.bass_utils import run_bass_kernel_spmd

    nc = bacc.Bacc("TRN2", target_bir_lowering=False, num_devices=1)
    arrays = {f"in_{name}": np.ascontiguousarray(inputs[name]) for name in _INS}
    arrays["in_consts"] = constants(np)
    t = {name[3:]: nc.dram_tensor(name, a.shape, mybir.dt.from_np(a.dtype), kind="ExternalInput").ap()
         for name, a in arrays.items()}
    t["out"] = [nc.dram_tensor(f"out_{i}", shape, F32, kind="ExternalOutput").ap() for i, shape in enumerate(_OUTS)]
    build(nc, t)
    r = run_bass_kernel_spmd(nc, [arrays], core_ids=[0])
    return tuple(r.results[0][f"out_{i}"] for i in range(len(_OUTS)))
```

```python
from contextlib import ExitStack

import concourse.bass as bass
from concourse import mybir

F32 = mybir.dt.float32
F32R = mybir.dt.float32r
ALU = mybir.AluOpType
ACT = mybir.ActivationFunctionType
AX_X = mybir.AxisListType.X

P = 128
D = 1024
KT = D // P
SEQ = 512
NB, NT = 8, 8
NS = NB * NT
TOK = SEQ + NS
HALF = TOK // 2
PAST = 256
NG, NH, HD = 3, 4, 128
AW = NG * NH * HD
DFF = 3 * D
FT = DFF // P
NCLS = 4
XA0, GA0, Q0, K0, V0, GTA0, GTB0 = 0, D, 2 * D, 2 * D + AW, 2 * D + 2 * AW, 2 * D + 3 * AW, 3 * D + 3 * AW
SCALE = HD ** -0.5
EPS = 1e-6
NEG = -1e30

C_ID, C_ONE, C_EPS, C_PM = 0, P, 2 * P, 2 * P + 1
C_SM = C_PM + 9 * P
C_N = C_SM + 4 * P + NG * NS

V_CW, V_CB, V_BA, V_BX, V_LAM, V_N1, V_N2, V_SC, V_H0 = 0, 4, 5, 6, 7, 8, 9, 10, 34
V_N = 42
F_W, F_B, F_S, F_N = 0, 3, 4, 20

XPAD, XSEQ = 3, 3 + NT
XS0 = XPAD + SEQ
XW = XS0 + NB * XSEQ
LW = XW - XPAD
LS0 = XS0
UPAD, USEQ = 2, 2 + NT
US0 = UPAD + SEQ
UW = US0 + NB * USEQ
CW = UW - UPAD

NRAW, NSPL = 4, 2
U_LRU = 9 * NH
U_MRG = U_LRU + 2 * KT
U_OUT = U_MRG + 4 * KT
U_FFN = U_OUT + KT
U_ALL = U_FFN + 2 * FT + 3 * KT
NPAIR, NRND = FT, 3
NHN = 4
PPR = NPAIR // NRND


MERGE = [("gate_a", 0)]
for _m in range(KT):
    MERGE += [("gate_b", _m), ("branch_b", _m)] + [("gate_a", _m + 1)] * (_m + 1 < KT) + [("branch_a", _m)]


def merge_unit_of(kind, m):
    return U_MRG + MERGE.index((kind, m))


def up_unit(i):
    return U_FFN + 2 * i + KT * min((i - 1) // PPR if i else 0, NRND - 1)


def down_unit(r, m):
    pairs = min((r + 1) * PPR + 1, NPAIR)
    return U_FFN + 2 * pairs + KT * r + m


def ffn_steps():
    for i in range(NPAIR):
        yield "up", i, 0
        for r in range(NRND):
            if i == min((r + 1) * PPR, NPAIR - 1):
                for m in range(KT):
                    yield "down", r, m


K_ROWS = {1: (3, 5, 7), 2: (4, 6, 7)}
ATT_PE = "S1 R2 P0 S2 V0 P1 S3 V1 O0 P2 S4 V2 O1 P3 O2".split()
ATT_ACT = "E0 R2 P0 E1 E2 P1 E3 H0 P2 E4 H1 P3 H2".split()
ATT_DVE = "M0 M1 M2 N0 M3 N1 L0 M4 N2 L1 L2".split()
TAIL_PE = {0: {2: "V3", 4: "O3", 6: "P4"}, 1: {3: "V4", 6: "O4"}}
TAIL_ACT = {0: "H3 P4".split(), 1: "H4".split()}
TAIL_DVE = {0: "N3 L3".split(), 1: "N4 L4".split()}


def build(nc, t):
    w_in = t["w_in"][0].rearrange("(k p) n -> p k n", p=P)
    w_br_a = t["w_br_a"][0].rearrange("(k p) n -> p k n", p=P)
    w_br_b = t["w_br_b"][0].rearrange("(k p) n -> p k n", p=P)
    w_out = t["w_out"][0].rearrange("(k p) n -> p k n", p=P)
    w_up = t["w_up"][0].rearrange("(k p) n -> p k n", p=P)
    w_down = t["w_down"][0].rearrange("(k p) n -> p k n", p=P)
    out = t["out"]

    def cols(w, c, k0=0, kn=KT):
        return w[:, k0:k0 + kn, c:c + P]

    units = []
    for hp in range(NH):
        for g in range(NG):
            for base in (K0, Q0):
                units.append(cols(w_in, base + (g * NH + hp) * HD))
        for g in range(NG):
            units.append(cols(w_in, V0 + (g * NH + hp) * HD))
    for c in range(KT):
        units += [cols(w_in, XA0 + c * P), cols(w_in, GA0 + c * P)]
    for kind, m in MERGE:
        units.append({"gate_a": cols(w_in, GTA0 + m * P), "gate_b": cols(w_in, GTB0 + m * P),
                      "branch_b": cols(w_br_b, m * P, 0, NH), "branch_a": cols(w_br_a, m * P)}[kind])
    for m in range(KT):
        units.append(cols(w_out, m * P))
    for kind, i, m in ffn_steps():
        if kind == "up":
            assert up_unit(i) == len(units)
            units += [cols(w_up, i * P), cols(w_up, DFF + i * P)]
        else:
            assert down_unit(i, m) == len(units)
            units.append(cols(w_down, m * P, i * PPR, PPR))
    assert len(units) == U_ALL
    nkt = [u.shape[1] for u in units]

    ctx = ExitStack()
    with ctx:
        def sb(name, shape, dt=F32, at=ctx):
            return at.enter_context(nc.sbuf_tensor(name, shape, dt))

        def sem(name):
            return ctx.enter_context(nc.semaphore(name))

        const = sb("const", [P, C_PM])
        vt = sb("vt", [P, KT, V_N])
        ft = sb("ft", [P, 2 * FT, F_N])
        gains = sb("gains", [P, KT + 2 * NG])
        sp4 = sb("sp4", [P, 4, KT])
        sp_t = sb("sp_t", [P, 2, KT])
        w_raw = sb("w_raw", [P, NRAW, KT, P])
        w_hi = sb("w_hi", [P, NSPL, KT, P], F32R)
        w_lo = sb("w_lo", [P, NSPL, KT, P], F32R)
        h_hi = sb("h_hi", [P, KT, TOK], F32R)
        with ExitStack() as m:
            x_t = sb("x_t", [P, KT, TOK], at=m)
        h_lo = sb("h_lo", [P, KT, TOK], F32R)
        ident, ones = const[:, C_ID:C_ID + P], const[:, C_ONE:C_ONE + P]
        eps = const[:, C_EPS:C_EPS + 1]

        with ExitStack() as m:
            xg_hi = sb("xg_hi", [P, KT, TOK], F32R, m)
            xg_lo = sb("xg_lo", [P, KT, TOK], F32R, m)
            nat_v = sb("nat_v", [V_N, D], at=m)
            nat_g = sb("nat_g", [KT + 2 * NG, P], at=m)
            root = sb("root", [P, TOK], at=m)
            rinv = sb("rinv", [P, TOK], at=m)
            hn = sb("hn", [P, NHN, TOK], at=m)
            with ExitStack() as m2:
                x_tok = sb("x_tok", [P, 5, D], at=m2)
                sq = sb("sq", [P, 2, TOK], at=m2)
            nat_f = sb("nat_f", [F_N, 2 * DFF], at=m)
        mid = ExitStack()
        att_hi = sb("att_hi", [P, NH, TOK], F32R, mid)
        att_lo = sb("att_lo", [P, NH, TOK], F32R, mid)
        with ExitStack() as m:
            prob = sb("prob", [P, 2, 6 * P], at=m)
            probT = sb("probT", [P, 6 * P], at=m)
            q_dia = sb("q_dia", [P, NG, NB * (NS + NT)], at=m)
            p_dia = sb("p_dia", [P, 4, NB * (NS + NT)], at=m)
            p_new = sb("p_new", [NS, NG * NS], at=m)
            NKC = 8
            kc = sb("kc", [P, NKC, 4, HD], at=m)
            vc = sb("vc", [P, NB, 4, HD], at=m)
            kcT = sb("kcT", [P, 2, 4 * P], at=m)
            o_sb = sb("o_sb", [P, 2, HD], at=m)
            stat = sb("stat", [P, 4, 8], at=m)
            masks = sb("masks", [P, C_N - C_PM], at=m)
            k_tok = sb("k_tok", [P, 5, NG, HD], at=m)
            v_tok = sb("v_tok", [P, 5, NG, HD], at=m)
            vT = sb("vT", [P, TOK], at=m)
            kT = sb("kT", [P, NG, TOK], at=m)
            qT = sb("qT", [P, NG, TOK], at=m)
            qk_sq = sb("qk_sq", [P, TOK], at=m)
            qk_gn = sb("qk_gn", [P, 2, TOK], at=m)
            qk_rt = sb("qk_rt", [P, TOK], at=m)
            qk_ri = sb("qk_ri", [P, TOK], at=m)
        l_st = sb("l_st", [P, KT, 36], at=mid)
        l_row = sb("l_row", [36, D], at=mid)
        y_hi = sb("y_hi", [P, KT, TOK], F32R, mid)
        y_lo = sb("y_lo", [P, KT, TOK], F32R, mid)
        with ExitStack() as m:
            wa = sb("wa", [P, KT, P], at=m)
            wx = sb("wx", [P, KT, P], at=m)
            xa = sb("xa", [P, 2, XW], at=m)
            xc = sb("xc", [P, 2, LW], at=m)
            ga = sb("ga", [P, 2, TOK], at=m)
            g_r = sb("g_r", [P, LW], at=m)
            g_i = sb("g_i", [P, LW], at=m)
            a_s = sb("a_s", [P, LW], at=m)
            a_a = sb("a_a", [P, LW], at=m)
            a_2 = sb("a_2", [P, LW], at=m)
            l_u = sb("l_u", [P, LW], at=m)
            l_h = sb("l_h", [P, LW], at=m)
            l_y = sb("l_y", [P, TOK], at=m)
        with ExitStack() as m:
            mg_hi = sb("mg_hi", [P, KT, TOK], F32R, m)
            mg_lo = sb("mg_lo", [P, KT, TOK], F32R, m)
            mg_s = sb("mg_s", [P, 2, TOK], at=m)
            x_tok2 = sb("x_tok2", [P, 5, D], at=m)
            sg_a = sb("sg_a", [P, 2, TOK], at=m)
            sg_b = sb("sg_b", [P, TOK], at=m)
        mid.close()
        x2 = sb("x2", [P, KT, TOK])
        rinv2 = sb("rinv2", [P, TOK])
        with ExitStack() as m:
            sq2 = sb("sq2", [P, TOK], at=m)
            sq2_hi = sb("sq2_hi", [P, 2, TOK], F32R, m)
            sq2_lo = sb("sq2_lo", [P, 2, TOK], F32R, m)
            ones_r = sb("ones_r", [P, P], F32R, m)
            xs = sb("xs", [P, TOK], at=m)
            root2 = sb("root2", [P, TOK], at=m)
        g_hi, g_lo = [sb("g_hi0", [P, PPR, TOK], F32R)], [sb("g_lo0", [P, PPR, TOK], F32R)]
        ug = sb("ug", [P, 2, UW])
        uv = sb("uv", [P, 2, UW])
        cg = sb("cg", [P, CW])
        cv = sb("cv", [P, CW])
        gm = sb("gm", [P, TOK])
        f_st = sb("f_st", [P, 2 * PPR, 18])
        f_row = sb("f_row", [18, 4, 4 * P])
        with ExitStack() as m:
            g_hi.append(sb("g_hi1", [P, PPR, TOK], F32R, m))
            g_lo.append(sb("g_lo1", [P, PPR, TOK], F32R, m))
        y_tok = sb("y_tok", [P, 5, D])

        ps = [ctx.enter_context(nc.psum_tensor(f"ps{i}", [P, 1024], F32)) for i in range(4)]
        acc = [p[:, :].rearrange("p (h n) -> p h n", h=2)[:, :, 0:HALF] for p in ps]
        NORM, TRN = 2, 3

        s_const, s_mask, s_nat, s_gain, s_nat_f = (sem(x) for x in ("s_const", "s_mask", "s_nat", "s_gain", "s_nat_f"))
        xs_in, xs_ps, xs_copied, xg_hi_rdy, xg_lo_rdy = (sem(x) for x in ("xs_in", "xs_ps", "xs_copied", "xg_hi_rdy", "xg_lo_rdy"))
        qk_gained = sem("qk_gained")
        x_in = [sem(f"x_in{i}") for i in range(4)]
        raw_in = [sem(f"raw_in{i}") for i in range(NRAW)]
        hi_ready, lo_ready, unit_done = sem("hi_ready"), sem("lo_ready"), sem("unit_done")
        acc_free = [sem("acc_free0"), sem("acc_free1")]
        vt_ps, vt_ready, tab_link = sem("vt_ps"), sem("vt_ready"), sem("tab_link")
        x_ps, x_copied, sq_ready, sq_used = sem("x_ps"), sem("x_copied"), sem("sq_ready"), sem("sq_used")
        root_ready, rinv_ready, hn_ready, hn_hi = (sem(x) for x in ("root_ready", "rinv_ready", "hn_ready", "hn_hi"))
        hn_lo = [sem("hn_lo0"), sem("hn_lo1")]
        qk_sqd, qk_sum, qk_root, qk_rinv, qk_ready = (sem(x) for x in ("qk_sqd", "qk_sum", "qk_root", "qk_rinv", "qk_ready"))
        tok_ps, tok_ready = sem("tok_ps"), sem("tok_ready")
        kv_out = [sem(f"kv_out{i}") for i in range(2 * NG)]
        s_zero, q_dia_rdy = sem("s_zero"), sem("q_dia_rdy")
        sc_ps, sc_read, mx_ready, p_ready, pT_ps, pT_ready = (sem(x) for x in ("sc_ps", "sc_read", "mx_ready", "p_ready", "pT_ps", "pT_ready"))
        o_ps, r_ready, o_ready, at_ps, at_hi_rdy, at_ready = (sem(x) for x in ("o_ps", "r_ready", "o_ready", "at_ps", "at_hi_rdy", "at_ready"))
        kc_in = [sem(f"kc_in{i}") for i in range(NKC // 2)]
        vc_in = sem("vc_in")
        kcT_ps, kcT_used = sem("kcT_ps"), sem("kcT_used")
        kcT_rdy = [sem("kcT_rdy0"), sem("kcT_rdy1")]
        gw_zero, gw_in = sem("gw_zero"), sem("gw_in")
        l_link, xa_pad, xc_rdy, gate_ps, gate_read = (sem(x) for x in ("l_link", "xa_pad", "xc_rdy", "gate_ps", "gate_read"))
        as_rdy, aa_rdy, a2_rdy, m2_rdy, mul_rdy, y_rdy, y_hi_rdy, y_lo_rdy = (sem(x) for x in ("as_rdy", "aa_rdy", "a2_rdy", "m2_rdy", "mul_rdy", "y_rdy", "y_hi_rdy", "y_lo_rdy"))
        lst_rdy, lst_ps, lrow_rdy, l_out = sem("lst_rdy"), sem("lst_ps"), sem("lrow_rdy"), sem("l_out")
        mg_link, mg_rdy, mg_hi_rdy, mg_lo_rdy, br_b_rdy = (sem(x) for x in ("mg_link", "mg_rdy", "mg_hi_rdy", "mg_lo_rdy", "br_b_rdy"))
        x2_in, x2_ps, x2_cp, sq2_rdy, sq2_hi_rdy, sq2_lo_rdy, sq2_used = (sem(x) for x in (
            "x2_in", "x2_ps", "x2_cp", "sq2_rdy", "sq2_hi_rdy", "sq2_lo_rdy", "sq2_used"))
        ones_rdy = sem("ones_rdy")
        root2_rdy, rinv2_rdy, xg2_hi, xg2_lo = (sem(x) for x in ("root2_rdy", "rinv2_rdy", "xg2_hi", "xg2_lo"))
        u_pad, f_link, cg_rdy, gl_rdy, cv_rdy, gm_rdy, g_hi_rdy, g_lo_rdy = (sem(x) for x in ("u_pad", "f_link", "cg_rdy", "gl_rdy", "cv_rdy", "gm_rdy", "g_hi_rdy", "g_lo_rdy"))
        fst_rdy, fst_ps, frow_rdy, f_out = sem("fst_rdy"), sem("fst_ps"), sem("frow_rdy"), sem("f_out")
        yt_ps, yt_rdy, y_out = sem("yt_ps"), sem("yt_rdy"), sem("y_out")
        l_gr, ln_fix = sem("l_gr"), sem("ln_fix")

        def diag(row):
            return row.rearrange("p (b n) -> p b n", n=NS + NT)[:, :, 0:NT]

        def key_banks(hp):
            return ps[1 - hp % 2]

        def out_banks(hp):
            return ps[hp % 2]

        def row_banks(hp, g, kv):
            return out_banks(hp) if kv and g == NG - 1 else ps[TRN]

        def score_banks(hp, i):
            return key_banks(hp) if i % 2 else ps[NORM]

        def o_bank(hp, i):
            return ps[TRN][:, 6 * P:7 * P] if i == 4 else out_banks(hp)[0:P if i else NS, 0:HD]

        def oT_bank(hp, i):
            return ps[TRN][:, 7 * P:8 * P] if i == 4 else out_banks(hp)[:, 512:512 + (P if i else NS)]

        def out_cols(buf, hp, i):
            return in_time(buf[:, hp, 0:SEQ])[:, :, i - 1] if i else buf[:, hp, SEQ:TOK]

        def by_class(ap):
            return ap.rearrange("p (r i) -> p i r", r=NCLS)

        def in_time(ap):
            return ap.rearrange("p (i r) -> p i r", r=NCLS)

        def seqs(ap, width):
            return ap.rearrange("p (b n) -> p b n", n=width)

        def taken(eng, u):
            eng.wait_ge(acc_free[u % 2], u // 2 + 1)

        block = ctx.enter_context(nc.Block())

        @block.sync
        def _(sp):
            def load(u):
                if u >= NRAW:
                    sp.wait_ge(lo_ready, u - NRAW + 1)
                sp.dma_start(w_raw[:, u % NRAW, 0:nkt[u], :], units[u]).then_inc(raw_in[u % NRAW], 16)

            sp.dma_start(const[:, 0:C_PM], t["consts"][:, 0:C_PM]).then_inc(s_const, 16)
            sp.dma_start(x_tok[0:NS, 4, :], t["x_sample"].rearrange("b t d -> (b t) d")).then_inc(xs_in, 16)
            for q in range(4):
                c = slice(q * D // 4, (q + 1) * D // 4)
                sp.dma_start(x_tok[:, 0:4, c], t["x_prompt"][0].rearrange("(n p) d -> p n d", p=P)[:, :, c]).then_inc(x_in[q], 16)
                if q == 0:
                    load(0)
            for u in range(1, NRAW):
                load(u)
            sp.dma_start(masks[:, :], t["consts"][:, C_PM:C_N]).then_inc(s_mask, 16)
            for u in range(NRAW, U_ALL):
                load(u)

        @block.gpsimd
        def _(pool):
            for rows, name in ((slice(V_CW, V_CB), "conv_a_w"), (slice(V_CB, V_BA), "conv_a_b"),
                               (slice(V_BA, V_BX), "lru_ba"), (slice(V_BX, V_LAM), "lru_bx"),
                               (slice(V_LAM, V_N1), "lru_lambda"), (slice(V_N1, V_N2), "norm1_g"),
                               (slice(V_N2, V_SC), "norm2_g")):
                src = t[name]
                pool.dma_start(nat_v[rows, :], src[0] if len(src.shape) == 3 else src).then_inc(s_nat, 16)
            pool.dma_start(nat_v[V_SC:V_H0, :], t["state_lru_conv"][0].rearrange("b s d -> (b s) d")).then_inc(s_nat, 16)
            pool.dma_start(nat_v[V_H0:V_N, :], t["state_lru_h"][0]).then_inc(s_nat, 16)
            pool.wait_ge(sq_used, KT)
            pool.dma_start(nat_f[F_W:F_B, :], t["conv_f_w"][0]).then_inc(s_nat_f, 16)
            pool.dma_start(nat_f[F_B:F_S, :], t["conv_f_b"]).then_inc(s_nat_f, 16)
            pool.dma_start(nat_f[F_S:F_N, :], t["state_ffn_conv"][0].rearrange("b s d -> (b s) d")).then_inc(s_nat_f, 16)
            for c in range(1, KT, 2):
                pool.wait_ge(hn_hi, c + 1)
                pool.tensor_tensor(h_lo[:, c, :], hn[:, c % NHN, :], h_hi[:, c, :], ALU.subtract).then_inc(hn_lo[1], 1)
            for lo in hn_lo:
                pool.wait_ge(lo, KT // 2)
            pool.wait_ge(unit_done, 2)
            pool.wait_ge(vt_ps, 2)
            pool.wait_ge(acc_free[1], 1)
            pool.memset(q_dia[:, :, :], 0.0).then_inc(s_zero, 1)
            pool.memset(p_dia[:, :, :], 0.0).then_inc(s_zero, 1)

            def cached(dst, name, hp, b0, bn, s):
                of = lambda g: t[f"cache_{name}_g{g}"][0, b0:b0 + bn, :, hp, :]
                pool.dma_start(dst[:, :, 0, :], of(0).rearrange("b p d -> p b d")).then_inc(s, 16)
                for n in range(2):
                    pool.dma_start(dst[:, :, 1 + n, :], of(1)[:, n * P:(n + 1) * P, :].rearrange("b p d -> p b d")).then_inc(s, 16)
                for b in range(bn):
                    pool.dma_start(dst[:, b, 3, :], of(2)[b].rearrange("(c s) d -> c s d", s=16)[:, 0:NT, :]).then_inc(s, 16)

            def load_k(hp, b):
                n = hp * NB + b
                if n >= NKC:
                    pool.wait_ge(kcT_ps, n - NKC + 2)
                cached(kc[:, n % NKC:n % NKC + 2, :, :], "k", hp, b, 2, kc_in[n % NKC // 2])

            def load_v(hp):
                if hp:
                    pool.wait_ge(o_ps, 5 * hp - 4)
                cached(vc[:, :, :, :], "v", hp, 0, NB, vc_in)

            for hp in range(NH):
                load_v(hp)
                for b in range(0, NKC, 2):
                    load_k(hp, b)
                for kv, buf in enumerate((k_tok, v_tok)):
                    for g in range(NG):
                        if kv and g == NG - 1:
                            for b in range(NKC, NB, 2):
                                load_k(hp, b)
                        pool.wait_ge(tok_ready, hp * 6 + NG * kv + g + 1)
                        o_p, o_s = out[4 + 2 * g + kv][0, 0], out[13 + 2 * g + kv]
                        s = kv_out[2 * g + kv]
                        if g == 0:
                            dst = o_p[:, hp, :].rearrange("(i r) d -> i r d", r=NCLS)
                            pool.dma_start(dst, buf[P - SEQ // 16:P, 0:4, g, :]).then_inc(s, 16)
                        else:
                            dst = o_p[:, hp, :].rearrange("(i r) d -> i r d", r=NCLS)
                            pool.dma_start(dst, buf[:, 0:4, g, :]).then_inc(s, 16)
                        pool.dma_start(o_s[0, :, :, hp, :].rearrange("b t d -> (b t) d"), buf[0:NS, 4, g, :]).then_inc(s, 16)
            pool.wait_ge(o_ps, 5 * NH - 4)
            pool.wait_ge(kcT_used, NH * NB)
            pool.memset(wa[:, :, :], 0.0).then_inc(gw_zero, 1)
            pool.memset(wx[:, :, :], 0.0).then_inc(gw_zero, 1)
            pool.memset(xa[:, :, 0:XPAD], 0.0).then_inc(gw_zero, 1)
            pool.wait_ge(gw_zero, 3)
            for buf, name in ((wa, "lru_wa"), (wx, "lru_wx")):
                src = t[name][0].rearrange("(c j) d e -> j d c e", j=2)
                for j in range(2):
                    pool.dma_start(buf[64 * j:64 * j + 64, :, 64 * j:64 * j + 64], src[j]).then_inc(gw_in, 16)
            for c in range(KT):
                pool.wait_ge(aa_rdy, c + 1)
                if c:
                    pool.wait_ge(m2_rdy, c)
                pool.tensor_tensor(a_2[:, :], a_a[:, :], a_a[:, :], ALU.mult).then_inc(a2_rdy, 1)
            pool.wait_ge(y_lo_rdy, KT)
            pool.dma_start(x_tok2[:, 0:4, :], t["x_prompt"][0].rearrange("(n p) d -> p n d", p=P)).then_inc(x2_in, 16)
            pool.dma_start(x_tok2[0:NS, 4, :], t["x_sample"].rearrange("b t d -> (b t) d")).then_inc(x2_in, 16)
            pool.wait_ge(lrow_rdy, 1)
            pool.dma_start(out[3][0, 0], l_row[0:3, :]).then_inc(l_out, 16)
            pool.dma_start(out[12][0].rearrange("b s d -> (b s) d"), l_row[3:27, :]).then_inc(l_out, 16)
            pool.dma_start(out[2][0], l_row[27:28, :]).then_inc(l_out, 16)
            pool.dma_start(out[11][0], l_row[28:36, :]).then_inc(l_out, 16)
            for r in range(NRND):
                pool.wait_ge(frow_rdy, 4 * (r + 1))
                for half in range(2):
                    for q in range(2):
                        c0 = half * DFF + r * PPR * P + q * 4 * P
                        src = f_row[:, 2 * half + q, :]
                        pool.dma_start(out[10][0, 0, :, c0:c0 + 4 * P], src[0:2, :]).then_inc(f_out, 16)
                        pool.dma_start(out[19][0].rearrange("b s d -> (b s) d")[:, c0:c0 + 4 * P], src[2:18, :]).then_inc(f_out, 16)
            for m in range(KT):
                pool.wait_ge(yt_rdy, m + 1)
                pool.dma_start(out[0][0].rearrange("(n p) d -> p n d", p=P)[:, :, m * P:(m + 1) * P],
                               y_tok[:, 0:4, m * P:(m + 1) * P]).then_inc(y_out, 16)
                pool.dma_start(out[1].rearrange("b t d -> (b t) d")[:, m * P:(m + 1) * P],
                               y_tok[0:NS, 4, m * P:(m + 1) * P]).then_inc(y_out, 16)
            for s in kv_out:
                pool.wait_ge(s, 32 * NH)
            pool.wait_ge(l_out, 64)
            pool.wait_ge(f_out, 16 * 8 * NRND)
            pool.wait_ge(y_out, 32 * KT)

        @block.tensor
        def _(pe):
            mm, tr = pe.matmul, pe.transpose

            def unit(u, x_hi, x_lo, ready=None, between={}):
                looped_unit(u % 2, nkt[u], u + 1, u // 2, x_hi, x_lo, ready, between)

            def looped_unit(p, n, parts, freed, x_hi, x_lo, ready=None, between={}):
                pe.wait_ge(lo_ready, parts)
                if not (isinstance(freed, int) and freed == 0):
                    pe.wait_ge(acc_free[p], freed)
                for k in range(n):
                    if k in between:
                        between[k]()
                    if ready:
                        ready(k)
                    for w, x in ((w_hi, x_hi), (w_hi, x_lo), (w_lo, x_hi)):
                        for h in range(2):
                            last = mm(ps[p][:, 512 * h:512 * h + HALF], w[:, p, k, :],
                                      x[:, k, HALF * h:HALF * (h + 1)],
                                      start=(k == 0 and x is x_hi and w is w_hi), stop=(k == n - 1 and w is w_lo))
                last.then_inc(unit_done, 1)

            def feature_sum(src, k, n):
                for h in range(2):
                    last = mm(ps[NORM][:, 512 * h:512 * h + HALF], ones, src[:, HALF * h:HALF * (h + 1)],
                              start=(k == 0), stop=(k == n - 1))
                return last

            pe.wait_ge(s_const, 16)
            pe.wait_ge(s_gain, 48)
            tr(ps[NORM][:, SEQ:SEQ + KT + 2 * NG], nat_g[:, :], ident[0:KT + 2 * NG, 0:KT + 2 * NG])
            pe.wait_ge(xs_in, 16)
            for c in range(KT):
                last = tr(ps[NORM][:, c * NS:(c + 1) * NS], x_tok[0:NS, 4, c * P:(c + 1) * P], ident[0:NS, 0:NS])
            last.then_inc(xs_ps, 1)

            def x_to_features(c):
                pe.wait_ge(x_in[4 * c // KT], 16)
                if c >= 2:
                    pe.wait_ge(x_copied, c - 1)
                for n in range(4):
                    last = tr(ps[TRN][:, 512 * (c % 2) + n * P:512 * (c % 2) + (n + 1) * P], x_tok[:, n, c * P:(c + 1) * P], ident)
                last.then_inc(x_ps, 1)

            def start_step(c):
                if c + 2 < KT:
                    x_to_features(c + 2)
                if c == 1:
                    pe.wait_ge(xs_copied, 1)
                if c:
                    pe.wait_ge(sq_ready, c)
                    feature_sum(sq[:, (c - 1) % 2, :], c - 1, KT).then_inc(sq_used, 1)

            def vector_rows():
                pe.wait_ge(s_nat, 16 * 9)
                pe.wait_ge(x_copied, KT)
                for c in range(KT):
                    last = tr(ps[TRN][:, c * V_N:(c + 1) * V_N], nat_v[:, c * P:(c + 1) * P], ident[0:V_N, 0:V_N])
                last.then_inc(vt_ps, 1)

            def ffn_vector_rows():
                pe.wait_ge(s_nat_f, 48)
                pe.wait_ge(vt_ready, 1)
                for h in range(2):
                    for c in range(FT):
                        last = tr(ps[TRN][:, 512 * h + c * F_N:512 * h + (c + 1) * F_N],
                                  nat_f[:, (h * FT + c) * P:(h * FT + c + 1) * P], ident[0:F_N, 0:F_N])
                last.then_inc(vt_ps, 1)

            x_to_features(0)
            x_to_features(1)

            def qk_norm_sum(hp, j):
                n = hp * 6 + j
                pe.wait_ge(qk_sqd, n + 1)
                if n:
                    pe.wait_ge(qk_root, n)
                if hp and j == 0:
                    pe.wait_ge(sc_read, 5 * hp)
                feature_sum(qk_sq, 0, 1).then_inc(qk_sum, 1)

            def to_rows(hp, g, kv):
                n = hp * 6 + NG * kv + g
                if kv:
                    taken(pe, hp * 9 + 6 + g)
                else:
                    pe.wait_ge(qk_ready, hp * 6 + 2 * g + 1)
                if n:
                    pe.wait_ge(tok_ready, n)
                if hp and g == 0 and not kv:
                    pe.wait_ge(at_ready, 5 * hp)
                elif n == 0:
                    pe.wait_ge(vt_ready, 2)
                src = vT if kv else kT[:, g, :]
                bank = row_banks(hp, g, kv)
                for r in range(4):
                    tr(bank[:, r * P:(r + 1) * P], src[:, r * P:(r + 1) * P], ident)
                tr(bank[0:NS, SEQ:SEQ + P], src[:, SEQ:TOK], ident).then_inc(tok_ps, 1)

            def scores(hp, i):
                e, r = hp * 5 + i, i - 1
                if i == 1:
                    for p in range(2):
                        pe.wait_ge(kcT_rdy[p], 4 * (hp + 1))
                else:
                    pe.wait_ge(sc_read, e - 1)
                rows, s = slice(r * P, (r + 1) * P), score_banks(hp, i)
                mm(s[:, 0:SEQ], qT[:, 0, rows], kT[:, 0, 0:SEQ], start=True, stop=True)
                mm(s[:, SEQ:SEQ + P], qT[:, 1, rows], kT[:, 1, rows], start=True, stop=True)
                mm(s[:, SEQ + P:SEQ + 2 * P], qT[:, 2, rows], kT[:, 2, rows], start=True, stop=True).then_inc(sc_ps, 1)

            def cached_keys_T(hp, b):
                n = hp * NB + b
                pe.wait_ge(kc_in[n % NKC // 2], 80 * (n // NKC + 1))
                if n >= 2:
                    pe.wait_ge(kcT_rdy[n % 2], n // 2)
                bank = key_banks(hp)[:, 512 * (b % 2):512 * (b % 2) + 512]
                for i in range(4):
                    last = tr(bank[:, i * P:(i + 1) * P], kc[:, n % NKC, i, :], ident)
                last.then_inc(kcT_ps, 1)

            def sample_scores(hp):
                taken(pe, 9 * hp + 7)
                for b in range(NB + 1):
                    if b < NB:
                        cached_keys_T(hp, b)
                    if b == 0:
                        pe.wait_ge(q_dia_rdy, hp + 1)
                        continue
                    n = hp * NB + b - 1
                    pe.wait_ge(kcT_rdy[n % 2], n // 2 + 1)
                    for g, c0, cn in ((0, 0, P), (1, P, 2 * P), (2, 3 * P, P)):
                        last = mm(ps[2][0:NS, c0:c0 + cn], q_dia[:, g, (b - 1) * NS:b * NS], kcT[:, n % 2, c0:c0 + cn],
                                  start=(b == 1 and g == 0), stop=(b == NB), skip_group_check=True)
                    last.then_inc(kcT_used, 1)
                for g in range(NG):
                    last = mm(ps[2][0:NS, 512 + g * NS:512 + (g + 1) * NS], qT[:, g, SEQ:TOK], kT[:, g, SEQ:TOK],
                              start=True, stop=True)
                last.then_inc(sc_ps, 1)

            def probs_T(hp, i):
                e = hp * 5 + i
                pe.wait_ge(p_ready, e + 1)
                if e:
                    pe.wait_ge(pT_ready, e)
                if i == 0:
                    pe.wait_ge(tok_ready, 6 * hp + 5)
                pr = prob[:, e % 2, :]
                if i:
                    for n in range(6):
                        last = tr(ps[TRN][:, n * P:(n + 1) * P], pr[:, n * P:(n + 1) * P], ident)
                else:
                    for n in range(4):
                        tr(ps[TRN][:, n * NS:(n + 1) * NS], pr[0:NS, n * P:(n + 1) * P], ident[0:NS, 0:NS])
                    for g in range(NG):
                        last = tr(ps[TRN][0:NS, 512 + g * NS:512 + (g + 1) * NS],
                                  pr[0:NS, 512 + g * NS:512 + (g + 1) * NS], ident[0:NS, 0:NS])
                last.then_inc(pT_ps, 1)

            def values(hp, i):
                e, r = hp * 5 + i, i - 1
                pe.wait_ge(pT_ready, e + 1)
                if e:
                    pe.wait_ge(o_ready, e)
                if i:
                    srcs = [(probT[:, c * P:(c + 1) * P], v_tok[:, c, 0, :]) for c in range(4)]
                    srcs += [(probT[:, (3 + g) * P:(4 + g) * P], v_tok[:, r, g, :]) for g in (1, 2)]
                else:
                    pe.wait_ge(tok_ready, 6 * hp + 6)
                    pe.wait_ge(vc_in, 16 * (3 + NB) * (hp + 1))
                    srcs = [(p_dia[:, n, b * NS:(b + 1) * NS], vc[:, b, n, :]) for b in range(NB) for n in range(4)]
                    srcs += [(p_new[:, g * NS:(g + 1) * NS], v_tok[0:NS, 4, g, :]) for g in range(NG)]
                for n, (p_, v_) in enumerate(srcs):
                    last = mm(o_bank(hp, i), p_, v_, start=(n == 0), stop=(n == len(srcs) - 1))
                last.then_inc(o_ps, 1)

            def out_T(hp, i):
                e = hp * 5 + i
                pe.wait_ge(o_ready, e + 1)
                if e:
                    pe.wait_ge(at_ready, e)
                n = P if i else NS
                tr(oT_bank(hp, i), o_sb[0:n, e % 2, :], ident[0:n, 0:n]).then_inc(at_ps, 1)

            def attend(hp, step):
                {"S": scores, "P": probs_T, "V": values, "O": out_T,
                 "R": lambda hp, g: to_rows(hp, g, 1)}[step[0]](hp, int(step[1]))

            def tail(hp, j, then={}):
                rest = TAIL_PE.get(j, {}) if hp else {}
                return {k: (lambda k=k: (attend(hp - 1, rest[k]) if k in rest else None, then[k]() if k in then else None))
                        for k in {*rest, *then}}

            for hp in range(NH):
                lag = 1 if hp else 2
                for j in range(9):
                    def norm_sum():
                        if lag <= j < lag + 6:
                            qk_norm_sum(hp, j - lag)

                    def key_rows():
                        if j in K_ROWS[lag]:
                            to_rows(hp, K_ROWS[lag].index(j), 0)

                    def value_rows():
                        if j >= 7:
                            to_rows(hp, j - 7, 1)

                    if hp and j == 0:
                        pe.wait_ge(sc_read, 5 * hp - 1)
                    if hp and j == 1:
                        pe.wait_ge(at_ready, 5 * hp - 1)
                    if hp:
                        unit(hp * 9 + j, h_hi, h_lo, None, tail(hp, j, {4: norm_sum, 5: key_rows, 7: value_rows}))
                    elif j == 0:
                        unit(j, xg_hi, xg_lo, lambda k: (pe.wait_ge(xg_hi_rdy, k + 1), pe.wait_ge(xg_lo_rdy, k + 1)),
                             {c: (lambda c=c: start_step(c)) for c in range(KT)})
                        start_step(KT)
                    elif j == 1:
                        unit(j, xg_hi, xg_lo)
                    elif j == 2:
                        unit(j, h_hi, h_lo, lambda k: (pe.wait_ge(hn_hi, k + 1), pe.wait_ge(hn_lo[k % 2], k // 2 + 1)),
                             {1: vector_rows, 3: norm_sum})
                    elif j == 3:
                        unit(j, h_hi, h_lo, None, {2: norm_sum, 7: ffn_vector_rows})
                    else:
                        unit(j, h_hi, h_lo, None, {2: norm_sum, 5: key_rows, 7: value_rows})
                sample_scores(hp)
                for step in ATT_PE:
                    attend(hp, step)

            def gate_products(c):
                if c == 0:
                    pe.wait_ge(gw_in, 64)
                    pe.wait_ge(at_ready, 5 * NH)
                pe.wait_ge(xc_rdy, c + 1)
                if c:
                    pe.wait_ge(gate_read, c)
                for i, w in enumerate((wa, wx)):
                    for h in range(2):
                        last = mm(ps[2 + i][:, 512 * h:512 * h + LW // 2], w[:, c, :],
                                  xc[:, c % 2, h * LW // 2:(h + 1) * LW // 2], start=True, stop=True)
                last.then_inc(gate_ps, 1)

            for c in range(KT):
                if c == 0:
                    pe.wait_ge(sc_read, 5 * NH - 1)
                unit(U_LRU + 2 * c, h_hi, h_lo, None, tail(NH, 2 * c))
                if c == 0:
                    pe.wait_ge(at_ready, 5 * NH - 1)
                unit(U_LRU + 2 * c + 1, h_hi, h_lo, None, tail(NH, 2 * c + 1))
                gate_products(c)

            def merge_step(n):
                kind, m = MERGE[n]
                parts = {"branch_a": (y_hi, y_lo), "branch_b": (att_hi, att_lo)}.get(kind, (h_hi, h_lo))
                if (kind, m) == ("branch_a", 0):
                    pe.wait_ge(y_hi_rdy, KT)
                    pe.wait_ge(y_lo_rdy, KT)
                unit(U_MRG + n, *parts)

            for n in range(5):
                merge_step(n)
            pe.wait_ge(gate_read, KT)
            pe.wait_ge(lst_rdy, KT)
            for c in range(KT):
                last = tr(ps[2][0:36, c * P:(c + 1) * P], l_st[:, c, :], ident)
            last.then_inc(lst_ps, 1)
            with pe.Fori(0, KT - 2) as i:
                for j, (tiles, hi, lo) in enumerate(((KT, h_hi, h_lo), (NH, att_hi, att_lo), (KT, h_hi, h_lo), (KT, y_hi, y_lo))):
                    u = U_MRG + 5 + j
                    looped_unit(u % 2, tiles, i * 4 + (u + 1), i * 2 + u // 2, hi, lo)
            for n in range(5 + 4 * (KT - 2), len(MERGE)):
                merge_step(n)

            pe.wait_ge(lrow_rdy, 1)
            def x2_products(c):
                if c < KT:
                    if c == 0:
                        pe.wait_ge(x2_in, 32)
                    else:
                        pe.wait_ge(x2_cp, c)
                    for n in range(4):
                        tr(ps[3][:, n * P:(n + 1) * P], x_tok2[:, n, c * P:(c + 1) * P], ident)
                    tr(ps[3][:, SEQ:TOK], x_tok2[0:NS, 4, c * P:(c + 1) * P], ident[0:NS, 0:NS]).then_inc(x2_ps, 1)
                if c:
                    pe.wait_ge(ones_rdy, 1)
                    pe.wait_ge(sq2_hi_rdy, c)
                    pe.wait_ge(sq2_lo_rdy, c)
                    for part in (sq2_hi, sq2_lo):
                        for h in range(2):
                            last = mm(ps[NORM][:, 512 * h:512 * h + HALF], ones_r[:, :],
                                      part[:, (c - 1) % 2, HALF * h:HALF * (h + 1)],
                                      start=(c == 1 and part is sq2_hi), stop=(c == KT and part is sq2_lo))
                    last.then_inc(sq2_used, 1)

            for c in range(KT):
                unit(U_OUT + c, mg_hi, mg_lo,
                     (lambda k: (pe.wait_ge(mg_hi_rdy, k + 1), pe.wait_ge(mg_lo_rdy, k + 1))) if c == 0 else None,
                     {KT - 3: lambda: x2_products(c)})
            def state_rows(r):
                pe.wait_ge(fst_rdy, (r + 1) * PPR)
                for q in range(4):
                    if r and q == 0:
                        pe.wait_ge(frow_rdy, 4 * r)
                    for i in range(4):
                        last = tr(ps[2 + q // 2][0:18, 512 * (q % 2) + i * P:512 * (q % 2) + (i + 1) * P],
                                  f_st[:, 4 * q + i, :], ident)
                last.then_inc(fst_ps, 1)

            def y_rows(m):
                taken(pe, down_unit(NRND - 1, m))
                if m == 0:
                    pe.wait_ge(frow_rdy, 4 * NRND)
                if m >= 1:
                    pe.wait_ge(yt_rdy, m)
                for n in range(4):
                    tr(ps[3][:, n * P:(n + 1) * P], x2[:, m, n * P:(n + 1) * P], ident)
                tr(ps[3][0:NS, SEQ:SEQ + P], x2[:, m, SEQ:TOK], ident).then_inc(yt_ps, 1)

            def pairs(first, count):
                with pe.Fori(0, count) as i:
                    for j in range(2):
                        u = up_unit(first) + j
                        looped_unit(u % 2, KT, i * 2 + (u + 1), i + u // 2, h_hi, h_lo)

            def down(r, m):
                unit(down_unit(r, m), g_hi[r % 2], g_lo[r % 2],
                     (lambda k: (pe.wait_ge(g_hi_rdy, r * PPR + k + 1), pe.wait_ge(g_lo_rdy, r * PPR + k + 1))) if m == 0 else None)

            unit(up_unit(0), h_hi, h_lo, lambda k: (pe.wait_ge(xg2_hi, k + 1), pe.wait_ge(xg2_lo, k + 1)),
                 {KT - 3: lambda: x2_products(KT)})
            unit(up_unit(0) + 1, h_hi, h_lo)
            for r in range(NRND):
                pairs(r * PPR + 1, min(PPR, NPAIR - 1 - r * PPR))
                down(r, 0)
                state_rows(r)
                if r < NRND - 1:
                    down(r, 1)
                    with pe.Fori(0, KT // 2 - 1) as i:
                        for j in range(2):
                            u = down_unit(r, 2) + j
                            looped_unit(u % 2, PPR, i * 2 + (u + 1), i + u // 2, g_hi[r % 2], g_lo[r % 2])
                else:
                    for m in range(1, KT):
                        down(r, m)
                        y_rows(m - 1)
            y_rows(KT - 1)

        @block.scalar
        def _(act):
            A = act.activation

            def hi_split(u):
                if u >= U_ALL:
                    return
                act.wait_ge(raw_in[u % NRAW], 16 * (u // NRAW + 1))
                if u >= NSPL:
                    act.wait_ge(unit_done, u - NSPL + 1)
                A(w_hi[:, u % NSPL, 0:nkt[u], :], w_raw[:, u % NRAW, 0:nkt[u], :], ACT.Copy).then_inc(hi_ready, 1)

            act.dma_start(nat_g[0:KT, :], t["norm1_g"].rearrange("o (c p) -> (o c) p", p=P)).then_inc(s_gain, 16)
            act.dma_start(nat_g[KT:KT + NG, :], t["k_norm_g"][0]).then_inc(s_gain, 16)
            act.dma_start(nat_g[KT + NG:KT + 2 * NG, :], t["q_norm_g"][0]).then_inc(s_gain, 16)
            hi_split(0)
            act.wait_ge(xs_copied, 1)
            for c in range(KT):
                act.wait_ge(x_copied, c + 1)
                A(xg_hi[:, c, :], x_t[:, c, :], ACT.Identity, scale=gains[:, c:c + 1]).then_inc(xg_hi_rdy, 1)
                if c >= 2:
                    act.wait_ge(sq_used, c - 1)
                A(sq[:, c % 2, :], x_t[:, c, :], ACT.Square).then_inc(sq_ready, 1)
                if c == 4:
                    hi_split(1)
            hi_split(2)
            act.wait_ge(sq_used, KT)
            A(root[:, :].rearrange("p (h n) -> p h n", h=2), acc[NORM], ACT.Sqrt, scale=1.0 / D, bias=eps).then_inc(root_ready, 1)

            def first_qk(j):
                act.wait_ge(acc_free[j], 1)
                if j:
                    act.wait_ge(qk_sum, j)
                A(qk_sq[:, :], qk_gn[:, j, :], ACT.Square).then_inc(qk_sqd, 1)
                act.wait_ge(qk_sqd, j + 1)
                g = KT + j * NG
                A(qk_gn[:, j, :], qk_gn[:, j, :], ACT.Identity, scale=gains[:, g:g + 1]).then_inc(qk_gained, 1)

            for c in range(KT):
                act.wait_ge(hn_ready, c + 1)
                A(h_hi[:, c, :], hn[:, c % NHN, :], ACT.Copy).then_inc(hn_hi, 1)
                if c == 3:
                    first_qk(0)
                if c == 4:
                    hi_split(3)
            first_qk(1)

            def softplus():
                act.wait_ge(ln_fix, 2)
                A(sp4[:, 1, :], sp4[:, 0, :], ACT.Exp, scale=-1.0).then_inc(tab_link, 1)
                act.wait_ge(ln_fix, 3)
                A(sp4[:, 3, :], sp4[:, 2, :], ACT.Ln).then_inc(tab_link, 1)

            def head_unit(hp, j):
                u = hp * 9 + j
                if j < 8:
                    hi_split(u + NSPL)
                act.wait_ge(unit_done, u + 1)
                a = acc[u % 2]
                if j < 6:
                    n = hp * 6 + j
                    if n:
                        act.wait_ge(qk_sum, n)
                    A(qk_sq[:, :].rearrange("p (h n) -> p h n", h=2), a, ACT.Square).then_inc(qk_sqd, 1)
                    if n >= 2:
                        act.wait_ge(qk_ready, n - 1)
                    g = (j % 2) * NG + j // 2
                    gain = gains[:, KT + g:KT + g + 1]
                    A(qk_gn[:, n % 2, :].rearrange("p (h n) -> p h n", h=2), a, ACT.Identity, scale=gain).then_inc(acc_free[u % 2], 1)
                else:
                    n = hp * 6 + j - NG
                    if j > 6:
                        act.wait_ge(tok_ps, n)
                    i0 = HALF // NCLS
                    vi = by_class(vT[:, 0:SEQ])
                    A(vi[:, 0:i0, :], in_time(ps[u % 2][:, 0:HALF]), ACT.Copy)
                    A(vi[:, i0:P, :], in_time(ps[u % 2][:, 512:512 + SEQ - HALF]), ACT.Copy)
                    A(vT[:, SEQ:TOK], ps[u % 2][:, 512 + SEQ - HALF:512 + HALF], ACT.Copy).then_inc(acc_free[u % 2], 1)

            def qk_root_of(hp, j):
                n = hp * 6 + j
                act.wait_ge(qk_sum, n + 1)
                if n:
                    act.wait_ge(qk_rinv, n)
                A(qk_rt[:, :].rearrange("p (h n) -> p h n", h=2), acc[NORM], ACT.Sqrt, scale=1.0 / HD, bias=eps).then_inc(qk_root, 1)

            def rows_of(hp, g, kv):
                n = hp * 6 + NG * kv + g
                act.wait_ge(tok_ps, n + 1)
                if hp:
                    act.wait_ge(kv_out[2 * g + kv], 32 * hp)
                buf, bank = v_tok if kv else k_tok, row_banks(hp, g, kv)
                A(buf[:, 0:4, g, :], bank[:, 0:SEQ].rearrange("p (r d) -> p r d", r=4), ACT.Copy)
                A(buf[0:NS, 4, g, :], bank[0:NS, SEQ:SEQ + HD], ACT.Copy).then_inc(tok_ready, 1)

            def exps(hp, i):
                e = hp * 5 + i
                act.wait_ge(mx_ready, e + 1)
                rows, n = (P, 6 * P) if i else (NS, 4 * P + NG * NS)
                pr = prob[0:rows, e % 2, 0:n]
                A(pr, pr, ACT.Exp, bias=stat[0:rows, e % 4, 2:3], accum_out=stat[0:rows, e % 4, 3:4]).then_inc(p_ready, 1)

            def take_probs_T(hp, i):
                e = hp * 5 + i
                act.wait_ge(pT_ps, e + 1)
                if e:
                    act.wait_ge(o_ps, e)
                if i:
                    A(probT[:, :], ps[TRN][:, 0:6 * P], ACT.Copy).then_inc(pT_ready, 1)
                else:
                    act.wait_ge(s_zero, 2)
                    for n in range(4):
                        src = ps[TRN][:, n * NS:(n + 1) * NS]
                        A(diag(p_dia[:, n, :]), src.rearrange("p (b t) -> p b t", b=NB), ACT.Copy)
                    A(p_new[:, :], ps[TRN][0:NS, 512:512 + NG * NS], ACT.Copy).then_inc(pT_ready, 1)

            def out_hi(hp, i):
                e = hp * 5 + i
                act.wait_ge(at_ps, e + 1)
                A(out_cols(att_hi, hp, i), oT_bank(hp, i), ACT.Copy).then_inc(at_hi_rdy, 1)

            def take_cached_T(hp, b):
                n = hp * NB + b
                act.wait_ge(kcT_ps, n + 1)
                if n >= 2:
                    act.wait_ge(kcT_used, n - 1)
                A(kcT[:, n % 2, :], key_banks(hp)[:, 512 * (b % 2):512 * (b % 2) + 512], ACT.Copy).then_inc(kcT_rdy[n % 2], 1)

            def attend(hp, step):
                {"E": exps, "P": take_probs_T, "H": out_hi,
                 "R": lambda hp, g: rows_of(hp, g, 1)}[step[0]](hp, int(step[1]))

            def tail(hp, j):
                for step in TAIL_ACT.get(j, ()):
                    attend(hp - 1, step)

            for hp in range(NH):
                for j in range(9):
                    if hp:
                        tail(hp, j)
                    lag = 1 if hp else 2
                    if lag <= j < lag + 6:
                        qk_root_of(hp, j - lag)
                    if j in K_ROWS[lag]:
                        rows_of(hp, K_ROWS[lag].index(j), 0)
                    if j >= 7:
                        rows_of(hp, j - 7, 1)
                    if lag == 1 or j >= 2:
                        head_unit(hp, j)
                    if hp == 0 and j == 7:
                        softplus()
                for b in range(1, NB, 2):
                    take_cached_T(hp, b)
                hi_split(hp * 9 + 8 + NSPL)
                for step in ATT_ACT:
                    attend(hp, step)

            for s in kv_out:
                act.wait_ge(s, 32 * NH)
            act.wait_ge(kcT_used, NH * NB)

            def gates(c):
                act.wait_ge(gate_ps, c + 1)
                if c:
                    act.wait_ge(y_rdy, c)
                gate = lambda i, dst: A(dst[:, :].rearrange("p (h n) -> p h n", h=2),
                                        ps[2 + i][:, :].rearrange("p (h n) -> p h n", h=2)[:, :, 0:LW // 2], ACT.Tanh,
                                        scale=0.5, bias=sp4[:, 2 + i, c:c + 1])
                gate(0, g_r).then_inc(l_gr, 1)
                gate(1, g_i).then_inc(gate_read, 1)
                act.wait_ge(l_gr, c + 1)
                A(a_a[:, :], g_r[:, :], ACT.Exp, scale=sp4[:, 1, c:c + 1], bias=sp4[:, 1, c:c + 1]).then_inc(aa_rdy, 1)
                A(a_s[:, :], g_r[:, :], ACT.Tanh, scale=sp4[:, 0, c:c + 1], bias=sp4[:, 0, c:c + 1]).then_inc(as_rdy, 1)

            def merge_unit(n):
                kind, m = MERGE[n]
                u = U_MRG + n
                if n:
                    hi_split(u + NSPL)
                if kind == "gate_a":
                    act.wait_ge(unit_done, u + 1)
                    if m >= 2:
                        act.wait_ge(mg_rdy, m - 1)
                    A(sg_a[:, m % 2, :].rearrange("p (h n) -> p h n", h=2), acc[u % 2], ACT.Sigmoid).then_inc(acc_free[u % 2], 1)
                if kind == "gate_b":
                    if m:
                        act.wait_ge(mg_rdy, m)
                        A(mg_hi[:, m - 1, :], mg_s[:, 0, :], ACT.Copy).then_inc(mg_hi_rdy, 1)
                    act.wait_ge(unit_done, u + 1)
                    A(sg_b[:, :].rearrange("p (h n) -> p h n", h=2), acc[u % 2], ACT.Sigmoid).then_inc(acc_free[u % 2], 1)

            def y_part(c):
                act.wait_ge(y_rdy, c + 1)
                A(y_hi[:, c, :], l_y[:, :], ACT.Copy).then_inc(y_hi_rdy, 1)

            for c in range(KT + 1):
                if c < KT:
                    tail(NH, 2 * c)
                    u = U_LRU + 2 * c
                    hi_split(u + NSPL)
                    act.wait_ge(unit_done, u + 1)
                    if c >= 2:
                        act.wait_ge(lst_rdy, c - 1)
                    p_ = ps[u % 2]
                    A(xa[:, c % 2, XPAD:XPAD + HALF], p_[:, 0:HALF], ACT.Copy)
                    A(xa[:, c % 2, XPAD + HALF:XS0], p_[:, 512:512 + SEQ - HALF], ACT.Copy)
                    A(seqs(xa[:, c % 2, XS0:XW], XSEQ)[:, :, XPAD:XSEQ],
                      seqs(p_[:, 512 + SEQ - HALF:512 + HALF], NT), ACT.Copy).then_inc(acc_free[u % 2], 1)
                if c == KT:
                    hi_split(U_MRG + NSPL)
                if c:
                    gates(c - 1)
                if c == KT:
                    merge_unit(0)
                if c < KT:
                    tail(NH, 2 * c + 1)
                    u += 1
                    hi_split(u + NSPL)
                if c:
                    act.wait_ge(m2_rdy, c)
                    A(a_s[:, :], a_s[:, :], ACT.Sqrt).then_inc(mul_rdy, 1)
                if c < KT:
                    act.wait_ge(unit_done, u + 1)
                    if c >= 2:
                        act.wait_ge(y_rdy, c - 1)
                    A(ga[:, c % 2, :].rearrange("p (h n) -> p h n", h=2), acc[u % 2], ACT.Gelu_apprx_tanh).then_inc(acc_free[u % 2], 1)
                if c == KT:
                    merge_unit(1)
                if c:
                    y_part(c - 1)

            for n in range(2, len(MERGE)):
                merge_unit(n)
                if n == MERGE.index(("branch_a", 0)):
                    act.wait_ge(lst_ps, 1)
                    A(l_row[:, :], ps[2][0:36, :], ACT.Copy).then_inc(lrow_rdy, 1)
            act.wait_ge(mg_rdy, KT)
            A(mg_hi[:, KT - 1, :], mg_s[:, 0, :], ACT.Copy).then_inc(mg_hi_rdy, 1)

            act.wait_ge(l_out, 64)
            A(ones_r[:, :], ones, ACT.Copy).then_inc(ones_rdy, 1)
            for c in range(KT):
                act.wait_ge(x2_ps, c + 1)
                if c:
                    taken(act, U_OUT + c - 1)
                A(xs[:, :], ps[3][:, 0:TOK], ACT.Copy).then_inc(x2_cp, 1)
                taken(act, U_OUT + c)
                A(h_hi[:, c, :], x2[:, c, :], ACT.Identity, scale=vt[:, c, V_N2:V_N2 + 1]).then_inc(xg2_hi, 1)
                if c:
                    act.wait_ge(sq2_lo_rdy, c)
                A(sq2[:, :], x2[:, c, :], ACT.Square).then_inc(sq2_rdy, 1)
                act.wait_ge(sq2_rdy, c + 1)
                if c >= 2:
                    act.wait_ge(sq2_used, c - 1)
                A(sq2_hi[:, c % 2, :], sq2[:, :], ACT.Copy).then_inc(sq2_hi_rdy, 1)
                hi_split(U_OUT + c + NSPL)
            act.wait_ge(sq2_used, KT)
            A(root2[:, :].rearrange("p (h n) -> p h n", h=2), acc[NORM], ACT.Sqrt, scale=1.0 / D, bias=eps).then_inc(root2_rdy, 1)

            def gelu(i):
                act.wait_ge(cg_rdy, i + 1)
                A(cg[:, :], cg[:, :], ACT.Gelu_apprx_tanh).then_inc(gl_rdy, 1)

            def g_part(i):
                act.wait_ge(gm_rdy, i + 1)
                r = i // PPR
                if r >= 2:
                    act.wait_ge(unit_done, down_unit(r - 2, KT - 1) + 1)
                A(g_hi[r % 2][:, i % PPR, :], gm[:, :], ACT.Copy).then_inc(g_hi_rdy, 1)

            def frows(r):
                act.wait_ge(fst_ps, r + 1)
                if r:
                    act.wait_ge(f_out, 16 * 8 * r)
                for q in range(4):
                    A(f_row[:, q, :], ps[2 + q // 2][0:18, 512 * (q % 2):512 * (q % 2) + 512], ACT.Copy).then_inc(frow_rdy, 1)

            def y_take(m):
                act.wait_ge(yt_ps, m + 1)
                A(y_tok[:, 0:4, m * P:(m + 1) * P], ps[3][:, 0:SEQ].rearrange("p (n d) -> p n d", n=4), ACT.Copy)
                A(y_tok[0:NS, 4, m * P:(m + 1) * P], ps[3][0:NS, SEQ:SEQ + P], ACT.Copy).then_inc(yt_rdy, 1)

            for kind, i, m in ffn_steps():
                if kind == "up":
                    for j in range(2):
                        hi_split(up_unit(i) + j + NSPL)
                    gelu(i)
                    g_part(i)
                else:
                    hi_split(down_unit(i, m) + NSPL)
                    if m == 0:
                        frows(i)
                    if i == NRND - 1 and m:
                        y_take(m - 1)
            y_take(KT - 1)

        @block.vector
        def _(dve):
            STT, TT, TS = dve.scalar_tensor_tensor, dve.tensor_tensor, dve.tensor_scalar

            def lo_split(u):
                if u >= U_ALL:
                    return
                dve.wait_ge(hi_ready, u + 1)
                TT(w_lo[:, u % NSPL, 0:nkt[u], :], w_raw[:, u % NRAW, 0:nkt[u], :],
                   w_hi[:, u % NSPL, 0:nkt[u], :], ALU.subtract).then_inc(lo_ready, 1)

            dve.wait_ge(xs_ps, 1)
            dve.tensor_copy(gains[:, :], ps[NORM][:, SEQ:SEQ + KT + 2 * NG])
            dve.tensor_copy(x_t[:, :, SEQ:TOK], ps[NORM][:, 0:KT * NS].rearrange("p (c n) -> p c n", c=KT)).then_inc(xs_copied, 1)
            for c in range(KT + 1):
                if c < KT:
                    dve.wait_ge(x_ps, c + 1)
                    dve.tensor_copy(x_t[:, c, 0:SEQ], ps[TRN][:, 512 * (c % 2):512 * (c % 2) + SEQ]).then_inc(x_copied, 1)
                if c:
                    dve.wait_ge(xg_hi_rdy, c)
                    STT(xg_lo[:, c - 1, :], x_t[:, c - 1, :], gains[:, c - 1:c], xg_hi[:, c - 1, :], ALU.mult, ALU.subtract).then_inc(xg_lo_rdy, 1)
                if c in (0, 5):
                    lo_split(c // 5)
            lo_split(2)
            dve.wait_ge(root_ready, 1)
            dve.reciprocal(rinv[:, :], root[:, :]).then_inc(rinv_ready, 1)
            dve.wait_ge(rinv_ready, 1)

            def with_rms(j):
                dve.wait_ge(unit_done, j + 1)
                TT(qk_gn[:, j, :].rearrange("p (h n) -> p h n", h=2), acc[j],
                   rinv[:, :].rearrange("p (h n) -> p h n", h=2), ALU.mult).then_inc(acc_free[j], 1)

            with_rms(0)
            for c in range(KT):
                if c >= NHN:
                    dve.wait_ge(hn_hi, c - NHN + 1)
                    dve.wait_ge(hn_lo[c % 2], (c - NHN) // 2 + 1)
                STT(hn[:, c % NHN, :], x_t[:, c, :], gains[:, c:c + 1], rinv[:, :], ALU.mult, ALU.mult).then_inc(hn_ready, 1)
                if c % 2:
                    dve.wait_ge(hn_hi, c)
                    TT(h_lo[:, c - 1, :], hn[:, (c - 1) % NHN, :], h_hi[:, c - 1, :], ALU.subtract).then_inc(hn_lo[0], 1)
                if c == 5:
                    lo_split(3)
            with_rms(1)
            dve.wait_ge(vt_ps, 1)
            dve.tensor_copy(vt[:, :, :], ps[TRN][:, 0:KT * V_N].rearrange("p (c n) -> p c n", c=KT)).then_inc(vt_ready, 1)

            def softplus():
                lam = vt[:, :, V_LAM]
                def fixed(ins, n):
                    ins.then_inc(ln_fix, 1)
                    dve.wait_ge(ln_fix, n)
                dve.wait_ge(vt_ready, 1)
                fixed(TS(sp4[:, 2, :], lam, -1.0, None, ALU.mult), 1)
                fixed(TT(sp4[:, 0, :], lam, sp4[:, 2, :], ALU.max), 2)
                dve.wait_ge(tab_link, 1)
                fixed(TS(sp4[:, 2, :], sp4[:, 1, :], 1.0, None, ALU.add), 3)
                fixed(dve.reciprocal(sp_t[:, 0, :], sp4[:, 2, :]), 4)
                fixed(TS(sp_t[:, 1, :], sp4[:, 2, :], -1.0, None, ALU.add), 5)
                fixed(TT(sp_t[:, 1, :], sp4[:, 1, :], sp_t[:, 1, :], ALU.subtract), 6)
                fixed(TT(sp_t[:, 1, :], sp_t[:, 1, :], sp_t[:, 0, :], ALU.mult), 7)
                dve.wait_ge(tab_link, 2)
                fixed(TT(sp_t[:, 1, :], sp_t[:, 1, :], sp4[:, 3, :], ALU.add), 8)
                fixed(TS(sp_t[:, 0, :], lam, -1.0, 0.0, ALU.mult, ALU.max), 9)
                fixed(TT(sp_t[:, 0, :], sp_t[:, 0, :], sp_t[:, 1, :], ALU.add), 10)
                TS(sp4[:, 0, :], sp_t[:, 0, :], 4.0, None, ALU.mult)
                TS(sp4[:, 1, :], sp_t[:, 0, :], -4.0, None, ALU.mult)
                TS(sp4[:, 2, :], vt[:, :, V_BA], 0.5, None, ALU.mult)
                TS(sp4[:, 3, :], vt[:, :, V_BX], 0.5, None, ALU.mult).then_inc(vt_ready, 1)

            def qk_scale(hp, j):
                n, u, g = hp * 6 + j, hp * 9 + j, j // 2
                dve.wait_ge(qk_root, n + 1)
                if n:
                    dve.wait_ge(qk_ready, n)
                dve.reciprocal(qk_ri[:, :], qk_rt[:, :]).then_inc(qk_rinv, 1)
                dve.wait_ge(qk_rinv, n + 1)
                if n < 2:
                    dve.wait_ge(qk_gained, n + 1)
                else:
                    dve.wait_ge(acc_free[u % 2], u // 2 + 1)
                dst = (qT if j % 2 else kT)[:, g, :]
                TT(by_class(dst[:, 0:SEQ]), in_time(qk_gn[:, n % 2, 0:SEQ]), in_time(qk_ri[:, 0:SEQ]), ALU.mult)
                TT(dst[:, SEQ:TOK], qk_gn[:, n % 2, SEQ:TOK], qk_ri[:, SEQ:TOK], ALU.mult).then_inc(qk_ready, 1)

            def mask_max(hp, i):
                e, r, sc = hp * 5 + i, i - 1, score_banks(hp, i)
                dve.wait_ge(sc_ps, e + 1)
                if e == 0:
                    dve.wait_ge(s_mask, 16)
                if e >= 2:
                    dve.wait_ge(pT_ps, e - 1)
                if e >= 4:
                    dve.wait_ge(o_ready, e - 3)
                st = stat[:, e % 4, :]
                if i:
                    rows, n0, n1, m0, m1 = P, 4 * P, 2 * P, C_PM + (3 - r) * P, C_PM + 7 * P
                else:
                    rows, n0, n1, m0, m1 = NS, 4 * P, NG * NS, C_SM, C_SM + 4 * P
                for w, (s0, n, m) in enumerate(((0, n0, m0), (512, n1, m1))):
                    last = dve.tensor_tensor_reduce(prob[0:rows, e % 2, s0:s0 + n], sc[0:rows, s0:s0 + n],
                                                    masks[0:rows, m - C_PM:m - C_PM + n], SCALE, -3e38, ALU.add, ALU.max,
                                                    st[0:rows, w:w + 1])
                last.then_inc(sc_read, 1)
                dve.wait_ge(sc_read, e + 1)
                dve.tensor_reduce(st[0:rows, 2:3], st[0:rows, 0:2], AX_X, ALU.max, negate=True).then_inc(mx_ready, 1)

            def normed(hp, i):
                e = hp * 5 + i
                rows = P if i else NS
                st = stat[0:rows, e % 4, :]
                dve.wait_ge(p_ready, e + 1)
                dve.reciprocal(st[:, 4:5], st[:, 3:4]).then_inc(r_ready, 1)
                dve.wait_ge(r_ready, e + 1)
                dve.wait_ge(o_ps, e + 1)
                if e >= 2:
                    dve.wait_ge(at_ps, e - 1)
                TS(o_sb[0:rows, e % 2, :], o_bank(hp, i), st[:, 4:5], None, ALU.mult).then_inc(o_ready, 1)

            def out_lo(hp, i):
                dve.wait_ge(at_hi_rdy, hp * 5 + i + 1)
                TT(out_cols(att_lo, hp, i), oT_bank(hp, i), out_cols(att_hi, hp, i), ALU.subtract).then_inc(at_ready, 1)

            def attend(hp, step):
                {"M": mask_max, "N": normed, "L": out_lo}[step[0]](hp, int(step[1]))

            def tail(hp, j):
                for step in TAIL_DVE.get(j, ()):
                    attend(hp - 1, step)

            for hp in range(NH):
                for j in range(9):
                    if hp:
                        tail(hp, j)
                    lag = 1 if hp else 2
                    if lag <= j < lag + 6:
                        qk_scale(hp, j - lag)
                    if (hp or j >= 2) and j < 8:
                        lo_split(hp * 9 + j + NSPL)
                    if hp == 0 and j == 3:
                        dve.wait_ge(vt_ps, 2)
                        dve.tensor_copy(ft[:, :, :].rearrange("p (h c) n -> p h (c n)", h=2),
                                        ps[TRN][:, :].rearrange("p (h n) -> p h n", h=2)[:, :, 0:FT * F_N]).then_inc(vt_ready, 1)
                    if hp == 0 and j == 7:
                        softplus()
                dve.wait_ge(qk_ready, 6 * hp + 6)
                dve.wait_ge(s_zero, 2)
                if hp:
                    dve.wait_ge(q_dia_rdy, hp)
                for g in range(NG):
                    last = dve.tensor_copy(diag(q_dia[:, g, :]), qT[:, g, SEQ:TOK].rearrange("p (b t) -> p b t", b=NB))
                last.then_inc(q_dia_rdy, 1)
                for b in range(0, NB, 2):
                    n = hp * NB + b
                    dve.wait_ge(kcT_ps, n + 1)
                    if n >= 2:
                        dve.wait_ge(kcT_used, n - 1)
                    dve.tensor_copy(kcT[:, n % 2, :], key_banks(hp)[:, 512 * (b % 2):512 * (b % 2) + 512]).then_inc(kcT_rdy[n % 2], 1)
                lo_split(hp * 9 + 8 + NSPL)
                for step in ATT_DVE:
                    attend(hp, step)

            link = [0]

            def linked(ins):
                ins.then_inc(l_link, 1)
                link[0] += 1
                dve.wait_ge(l_link, link[0])

            for s in kv_out:
                dve.wait_ge(s, 32 * NH)
            dve.wait_ge(gw_zero, 3)

            def conv(c):
                u = U_LRU + 2 * c
                x, y, v = xa[:, c % 2, :], xc[:, c % 2, :], vt[:, c, :]
                if c >= 2:
                    dve.wait_ge(lst_rdy, c - 1)
                dve.tensor_copy(seqs(x[:, XS0:XW], XSEQ)[:, :, 0:XPAD], seqs(v[:, V_SC:V_H0], 3)).then_inc(xa_pad, 1)
                dve.wait_ge(xa_pad, c + 1)
                dve.wait_ge(acc_free[u % 2], u // 2 + 1)
                linked(TS(y[:, :], x[:, 0:LW], v[:, V_CW:V_CW + 1], v[:, V_CB:V_CB + 1], ALU.mult, ALU.add))
                for i in (1, 2, 3):
                    ins = STT(y[:, :], x[:, i:i + LW], v[:, V_CW + i:V_CW + i + 1], y[:, :], ALU.mult, ALU.add)
                    if i < 3:
                        linked(ins)
                    else:
                        ins.then_inc(xc_rdy, 1)

            pads = lambda b: seqs(b[:, SEQ:LW], XSEQ)[:, :, XPAD - 1]

            def multiplier(c):
                dve.wait_ge(gate_read, c + 1)
                linked(STT(g_i[:, :], g_i[:, :], 1.0, xc[:, c % 2, :], ALU.add, ALU.mult))
                dve.wait_ge(as_rdy, c + 1)
                dve.wait_ge(a2_rdy, c + 1)
                STT(a_s[:, :], a_2[:, :], 1.0, a_s[:, :], ALU.add, ALU.mult).then_inc(m2_rdy, 1)

            def recur(c):
                dve.memset(pads(a_a[:, :]), 0.0)
                dve.wait_ge(mul_rdy, c + 1)
                linked(dve.memset(a_s[:, 0:1], 1.0))
                linked(STT(l_u[:, :], g_i[:, :], 0.5, a_s[:, :], ALU.mult, ALU.mult))
                linked(dve.tensor_copy(pads(l_u[:, :]), vt[:, c, V_H0:V_N]))
                if c:
                    dve.wait_ge(lst_rdy, c)
                    dve.wait_ge(y_lo_rdy, c)
                linked(dve.tensor_tensor_scan(l_h[:, :], a_a[:, :], l_u[:, :], 0.0, ALU.mult, ALU.add))
                g_ = ga[:, c % 2, :]
                u = U_LRU + 2 * c + 1
                dve.wait_ge(acc_free[u % 2], u // 2 + 1)
                TT(l_y[:, 0:SEQ], l_h[:, 0:SEQ], g_[:, 0:SEQ], ALU.mult)
                hs = seqs(l_h[:, SEQ:LW], XSEQ)[:, :, XPAD:XSEQ]
                TT(seqs(l_y[:, SEQ:TOK], NT), hs, seqs(g_[:, SEQ:TOK], NT), ALU.mult).then_inc(y_rdy, 1)
                if c == KT - 1:
                    lo_split(U_MRG + 1 + NSPL)
                x = xa[:, c % 2, :]
                dve.tensor_copy(l_st[:, c, 0:3], x[:, XS0 - 3:XS0])
                dve.tensor_copy(seqs(l_st[:, c, 3:27], 3), seqs(x[:, XS0:XW], XSEQ)[:, :, XSEQ - 3:XSEQ])
                dve.tensor_copy(l_st[:, c, 27:28], l_h[:, SEQ - 1:SEQ])
                dve.tensor_copy(l_st[:, c, 28:36], hs[:, :, NT - 1]).then_inc(lst_rdy, 1)
                dve.wait_ge(y_hi_rdy, c + 1)
                TT(y_lo[:, c, :], l_y[:, :], y_hi[:, c, :], ALU.subtract).then_inc(y_lo_rdy, 1)

            for c in range(KT + 1):
                if c < KT:
                    tail(NH, 2 * c)
                    lo_split(U_LRU + 2 * c + NSPL)
                    tail(NH, 2 * c + 1)
                    conv(c)
                else:
                    lo_split(U_MRG + NSPL)
                if c:
                    multiplier(c - 1)
                if c < KT:
                    lo_split(U_LRU + 2 * c + 1 + NSPL)
                if c:
                    recur(c - 1)

            dve.wait_ge(lst_rdy, KT)
            dve.wait_ge(y_lo_rdy, KT)
            halves = lambda b: b.rearrange("p (h n) -> p h n", h=2)
            for n, (kind, m) in enumerate(MERGE):
                u = U_MRG + n
                if n >= 2:
                    lo_split(u + NSPL)
                if kind == "gate_b" and m:
                    dve.wait_ge(mg_hi_rdy, m)
                    TT(mg_lo[:, m - 1, :], mg_s[:, 0, :], mg_hi[:, m - 1, :], ALU.subtract).then_inc(mg_lo_rdy, 1)
                if kind in ("branch_a", "branch_b"):
                    dve.wait_ge(unit_done, u + 1)
                    taken(dve, merge_unit_of("gate_" + kind[-1], m))
                    if m:
                        dve.wait_ge(mg_lo_rdy, m)
                        dve.wait_ge(mg_hi_rdy, m)
                if kind == "branch_b":
                    TT(halves(mg_s[:, 1, :]), acc[u % 2], halves(sg_b[:, :]), ALU.mult).then_inc(acc_free[u % 2], 1)
                if kind == "branch_a":
                    TT(halves(mg_s[:, 0, :]), acc[u % 2], halves(sg_a[:, m % 2, :]), ALU.mult).then_inc(acc_free[u % 2], 1)
                    taken(dve, u)
                    taken(dve, merge_unit_of("branch_b", m))
                    TT(mg_s[:, 0, :], mg_s[:, 0, :], mg_s[:, 1, :], ALU.add).then_inc(mg_rdy, 1)
            dve.wait_ge(mg_hi_rdy, KT)
            TT(mg_lo[:, KT - 1, :], mg_s[:, 0, :], mg_hi[:, KT - 1, :], ALU.subtract).then_inc(mg_lo_rdy, 1)

            dve.wait_ge(l_out, 64)
            for c in range(KT):
                u = U_OUT + c
                dve.wait_ge(unit_done, u + 1)
                dve.wait_ge(x2_cp, c + 1)
                TT(x2[:, c, :].rearrange("p (h n) -> p h n", h=2), acc[u % 2],
                   xs[:, :].rearrange("p (h n) -> p h n", h=2), ALU.add).then_inc(acc_free[u % 2], 1)
                dve.wait_ge(xg2_hi, c + 1)
                STT(h_lo[:, c, :], x2[:, c, :], vt[:, c, V_N2:V_N2 + 1], h_hi[:, c, :], ALU.mult, ALU.subtract).then_inc(xg2_lo, 1)
                dve.wait_ge(sq2_hi_rdy, c + 1)
                TT(sq2_lo[:, c % 2, :], sq2[:, :], sq2_hi[:, c % 2, :], ALU.subtract).then_inc(sq2_lo_rdy, 1)
                lo_split(u + NSPL)
            dve.wait_ge(root2_rdy, 1)
            dve.reciprocal(rinv2[:, :], root2[:, :]).then_inc(rinv2_rdy, 1)
            dve.wait_ge(rinv2_rdy, 1)

            dve.memset(ug[:, :, 0:UPAD], 0.0).then_inc(u_pad, 1)
            dve.memset(uv[:, :, 0:UPAD], 0.0).then_inc(u_pad, 1)
            flink = [0]

            def flinked(ins):
                ins.then_inc(f_link, 1)
                flink[0] += 1
                dve.wait_ge(f_link, flink[0])

            def ffn_conv(i, j):
                u, ti = up_unit(i) + j, i + j * FT
                x, y, v = (uv if j else ug)[:, i % 2, :], cv if j else cg, ft[:, ti, :]
                flinked(dve.tensor_copy(seqs(x[:, US0:UW], USEQ)[:, :, 0:UPAD], seqs(v[:, F_S:F_N], 2)))
                dve.wait_ge(unit_done, u + 1)
                if i >= 2:
                    dve.wait_ge(fst_rdy, i - 1)
                p_ = ps[u % 2]
                TT(x[:, UPAD:UPAD + HALF], p_[:, 0:HALF], rinv2[:, 0:HALF], ALU.mult)
                TT(x[:, UPAD + HALF:US0], p_[:, 512:512 + SEQ - HALF], rinv2[:, HALF:SEQ], ALU.mult)
                TT(seqs(x[:, US0:UW], USEQ)[:, :, UPAD:USEQ], seqs(p_[:, 512 + SEQ - HALF:512 + HALF], NT),
                   seqs(rinv2[:, SEQ:TOK], NT), ALU.mult).then_inc(acc_free[u % 2], 1)
                lo_split(u + NSPL)
                dve.wait_ge(acc_free[u % 2], u // 2 + 1)
                if j == 0 and i:
                    dve.wait_ge(gm_rdy, i)
                flinked(TS(y[:, :], x[:, 0:CW], v[:, F_W:F_W + 1], v[:, F_B:F_B + 1], ALU.mult, ALU.add))
                flinked(STT(y[:, :], x[:, 1:1 + CW], v[:, F_W + 1:F_W + 2], y[:, :], ALU.mult, ALU.add))
                STT(y[:, :], x[:, 2:2 + CW], v[:, F_W + 2:F_W + 3], y[:, :], ALU.mult, ALU.add).then_inc(cv_rdy if j else cg_rdy, 1)

            def product(i):
                dve.wait_ge(gl_rdy, i + 1)
                dve.wait_ge(cv_rdy, i + 1)
                if i:
                    dve.wait_ge(g_hi_rdy, i)
                    dve.wait_ge(g_lo_rdy, i)
                TT(gm[:, 0:SEQ], cg[:, 0:SEQ], cv[:, 0:SEQ], ALU.mult)
                ss = lambda b: b[:, SEQ:CW].rearrange("p (b n) -> p b n", n=USEQ)[:, :, UPAD:USEQ]
                TT(seqs(gm[:, SEQ:TOK], NT), ss(cg), ss(cv), ALU.mult).then_inc(gm_rdy, 1)
                q = i % PPR
                if q == 0 and i:
                    dve.wait_ge(fst_ps, i // PPR)
                for j, b in enumerate((ug, uv)):
                    x = b[:, i % 2, :]
                    dve.tensor_copy(f_st[:, j * PPR + q, 0:2], x[:, US0 - 2:US0])
                    last = dve.tensor_copy(seqs(f_st[:, j * PPR + q, 2:18], 2), seqs(x[:, US0:UW], USEQ)[:, :, USEQ - 2:USEQ])
                last.then_inc(fst_rdy, 1)
                dve.wait_ge(g_hi_rdy, i + 1)
                TT(g_lo[(i // PPR) % 2][:, i % PPR, :], gm[:, :], g_hi[(i // PPR) % 2][:, i % PPR, :], ALU.subtract).then_inc(g_lo_rdy, 1)

            for kind, i, m in ffn_steps():
                if kind == "up":
                    for j in range(2):
                        ffn_conv(i, j)
                    product(i)
                else:
                    u = down_unit(i, m)
                    lo_split(u + NSPL)
                    dve.wait_ge(unit_done, u + 1)
                    TT(x2[:, m, :].rearrange("p (h n) -> p h n", h=2), acc[u % 2],
                       x2[:, m, :].rearrange("p (h n) -> p h n", h=2), ALU.add).then_inc(acc_free[u % 2], 1)


def constants(np):
    c = np.zeros((P, C_N), np.float32)
    c[:, C_ID:C_ID + P] = np.eye(P)
    c[:, C_ONE:C_ONE + P] = 1.0
    i, j = np.arange(P)[:, None], np.arange(P)[None, :]
    d = i - j
    below, same, above = (d >= 0) & (d <= 31), (d >= 0) & (d <= 32), (d >= 1) & (d <= 32)
    strip = [below] * 3 + [same] + [above] * 3
    strip += [d >= 0, (d >= 0) & (d % 4 == 0)]
    c[:, C_PM:C_PM + 9 * P] = np.where(np.concatenate(strip, 1), 0.0, NEG)
    b, t = np.divmod(np.arange(NS), NT)
    t = t[:, None]
    k = np.arange(PAST)[None, :]
    own = [np.arange(P)[None, :] >= t,
           (k - t) % 4 == 0,
           np.arange(P)[None, :] % NT == t]
    b2, t2 = np.divmod(np.arange(NS)[None, :], NT)
    mine = (b[:, None] == b2) & (t2 <= t)
    own += [mine, mine & ((t - t2) % 4 == 0), mine & (t == t2)]
    c[0:NS, C_SM:C_SM + 4 * P + NG * NS] = np.where(np.concatenate(own, 1), 0.0, NEG)
    c[:, C_EPS] = EPS
    return c


_INS = ["x_prompt", "x_sample", "state_lru_h", "state_lru_conv", "cache_k_g0", "cache_v_g0", "cache_k_g1", "cache_v_g1",
        "cache_k_g2", "cache_v_g2", "state_ffn_conv", "norm1_g", "w_in", "conv_a_w", "conv_a_b", "lru_wa", "lru_ba",
        "lru_wx", "lru_bx", "lru_lambda", "q_norm_g", "k_norm_g", "w_br_a", "w_br_b", "w_out", "norm2_g", "w_up",
        "conv_f_w", "conv_f_b", "w_down"]
_KV = [(P, P), (SEQ, SEQ), (SEQ, SEQ)]
_OUTS = ([(1, SEQ, D), (NB, NT, D), (1, 1, D), (1, 1, 3, D)]
         + [(1, 1, n, NH, HD) for pair in _KV for n in pair] + [(1, 1, 2, 2 * DFF)]
         + [(1, NB, D), (1, NB, 3, D)] + [(1, NB, NT, NH, HD)] * 6 + [(1, NB, 2, 2 * DFF)])


def kernel(**inputs):
    import numpy as np
    import concourse.bacc as bacc
    from concourse.bass_utils import run_bass_kernel_spmd

    nc = bacc.Bacc("TRN2", target_bir_lowering=False, num_devices=1)
    arrays = {f"in_{name}": np.ascontiguousarray(inputs[name]) for name in _INS}
    arrays["in_consts"] = constants(np)
    t = {name[3:]: nc.dram_tensor(name, a.shape, mybir.dt.from_np(a.dtype), kind="ExternalInput").ap()
         for name, a in arrays.items()}
    t["out"] = [nc.dram_tensor(f"out_{i}", shape, F32, kind="ExternalOutput").ap() for i, shape in enumerate(_OUTS)]
    build(nc, t)
    r = run_bass_kernel_spmd(nc, [arrays], core_ids=[0])
    return tuple(r.results[0][f"out_{i}"] for i in range(len(_OUTS)))
```
